# Optimizing a Trainium2 kernel written in Bass

```python
import math
import jax, jax.numpy as jnp
from jax import lax
import numpy as np

D_MODEL = 1024
BATCH = 1
SEQ = 256
DEPTH = 2

N_MIXERS = 2
N_A_LAYERS = (DEPTH + 1) // 2
N_B_LAYERS = DEPTH // 2

GDN_HEADS = 8
GDN_DK = 128
GDN_DV = 128
GDN_CONV = 4
GDN_CHUNK = 64
GDN_HK = GDN_HEADS * GDN_DK
GDN_HV = GDN_HEADS * GDN_DV
GDN_IN = 2 * GDN_HK + 2 * GDN_HV + 2 * GDN_HEADS
GDN_CONV_CH = 2 * GDN_HK + GDN_HV

DSW_GROUPS = ((128, 1), (512, 4), (2048, 16))
DSW_N_GROUPS = len(DSW_GROUPS)
DSW_HEADS = 8
DSW_DH = 64
DSW_HG = DSW_HEADS * DSW_DH
DSW_IN = 3 * DSW_N_GROUPS * DSW_HG

REL_BUCKETS = 32
REL_MAX_DIST = 2048
REL_HEADS = DSW_N_GROUPS * DSW_HEADS

FFN_HIDDEN = -(-8 * D_MODEL // (3 * 256)) * 256

RMS_EPS = 1e-6


def rms_norm(x, gain):
    xf = x.astype(jnp.float32)
    y = xf * lax.rsqrt(jnp.mean(xf * xf, axis=-1, keepdims=True) + RMS_EPS)
    return y * gain.astype(jnp.float32)

def l2_norm(x):
    xf = x.astype(jnp.float32)
    return xf * lax.rsqrt(jnp.sum(xf * xf, axis=-1, keepdims=True) + RMS_EPS)

def causal_depthwise_conv(x, w):
    K, C = w.shape
    return lax.conv_general_dilated(
        x, w[:, None, :].astype(x.dtype), window_strides=(1,),
        padding=((K - 1, 0),), dimension_numbers=("NWC", "WIO", "NWC"),
        feature_group_count=C)

def chunk_gated_delta_rule(q, k, v, g, beta):
    Bsz, S, H, dk = q.shape
    dv = v.shape[-1]
    C = GDN_CHUNK
    N = S // C
    to_chunks = lambda t: jnp.transpose(t.reshape(Bsz, N, C, H, t.shape[-1]), (0, 3, 1, 2, 4))
    q = to_chunks(q * (dk ** -0.5))
    k = to_chunks(k)
    v = to_chunks(v.astype(jnp.float32))
    beta = jnp.transpose(beta.reshape(Bsz, N, C, H), (0, 3, 1, 2))
    g = jnp.cumsum(jnp.transpose(g.reshape(Bsz, N, C, H), (0, 3, 1, 2)), axis=-1)

    causal = jnp.tril(jnp.ones((C, C), dtype=bool))
    strict = jnp.tril(jnp.ones((C, C), dtype=bool), -1)
    decay = jnp.exp(jnp.where(causal, g[..., :, None] - g[..., None, :], -jnp.inf))
    kb = k * beta[..., None]
    vb = v * beta[..., None]
    Lmat = jnp.where(strict, jnp.einsum('bhncd,bhnmd->bhncm', kb, k) * decay, 0.0)
    rhs = jnp.concatenate([vb, kb * jnp.exp(g)[..., None]], axis=-1)
    sol = lax.linalg.triangular_solve(Lmat, rhs, left_side=True, lower=True, unit_diagonal=True)
    u = sol[..., :dv]
    w = sol[..., dv:]
    qk = jnp.where(causal, jnp.einsum('bhncd,bhnmd->bhncm', q, k) * decay, 0.0)

    g_last = g[..., -1]
    q_dec = q * jnp.exp(g)[..., None]
    k_dec = k * jnp.exp(g_last[..., None] - g)[..., None]

    def step(state, inp):
        qd, a, uu, ww, kd, gl = inp
        v_new = uu - jnp.einsum('bhck,bhkv->bhcv', ww, state)
        o = jnp.einsum('bhck,bhkv->bhcv', qd, state) + jnp.einsum('bhcm,bhmv->bhcv', a, v_new)
        state = state * jnp.exp(gl)[..., None, None] + jnp.einsum('bhck,bhcv->bhkv', kd, v_new)
        return state, o

    xs = tuple(jnp.moveaxis(t, 2, 0) for t in (q_dec, qk, u, w, k_dec, g_last))
    state0 = jnp.zeros((Bsz, H, dk, dv), jnp.float32)
    _, o = lax.scan(step, state0, xs)
    return jnp.transpose(o, (1, 0, 3, 2, 4)).reshape(Bsz, S, H, dv)

def gated_deltanet_mixer(h, w_in, conv_w, a_log, dt_bias, out_gain, w_out):
    Bsz, S, _ = h.shape
    proj = h @ w_in
    qkv, z, a, b = jnp.split(proj, [GDN_CONV_CH, GDN_CONV_CH + GDN_HV,
                                    GDN_CONV_CH + GDN_HV + GDN_HEADS], axis=-1)
    qkv = jax.nn.silu(causal_depthwise_conv(qkv, conv_w))
    q, k, v = jnp.split(qkv, [GDN_HK, 2 * GDN_HK], axis=-1)
    q = l2_norm(q.reshape(Bsz, S, GDN_HEADS, GDN_DK))
    k = l2_norm(k.reshape(Bsz, S, GDN_HEADS, GDN_DK))
    v = v.reshape(Bsz, S, GDN_HEADS, GDN_DV)
    beta = jax.nn.sigmoid(b.astype(jnp.float32))
    g = -jnp.exp(a_log.astype(jnp.float32)) * jax.nn.softplus(a.astype(jnp.float32) + dt_bias.astype(jnp.float32))
    o = chunk_gated_delta_rule(q, k, v, g, beta)
    zf = z.reshape(Bsz, S, GDN_HEADS, GDN_DV).astype(jnp.float32)
    o = rms_norm(o, out_gain) * jax.nn.silu(zf)
    return o.reshape(Bsz, S, GDN_HV).astype(h.dtype) @ w_out

def t5_causal_bucket(dist):
    max_exact = REL_BUCKETS // 2
    scaled = jnp.log(jnp.maximum(dist, 1).astype(jnp.float32) / max_exact) / math.log(REL_MAX_DIST / max_exact)
    large = max_exact + (scaled * (REL_BUCKETS - max_exact)).astype(jnp.int32)
    large = jnp.minimum(large, REL_BUCKETS - 1)
    return jnp.where(dist < max_exact, dist, large)

def dilated_window_group(q, k, v, bias_table, window, dilation):
    Bsz, S, H, dh = q.shape
    span = window // dilation
    blk = span
    unit = dilation * blk
    S_pad = -(-S // unit) * unit
    nb = S_pad // unit

    def sub(t):
        t = jnp.pad(t, ((0, 0), (0, S_pad - S), (0, 0), (0, 0)))
        return jnp.transpose(t.reshape(Bsz, nb, blk, dilation, H, dh), (0, 3, 1, 2, 4, 5))

    qs, ks, vs = sub(q), sub(k), sub(v)
    shift = lambda t: jnp.concatenate([jnp.zeros_like(t[:, :, :1]), t[:, :, :-1]], axis=2)
    kb = jnp.concatenate([shift(ks), ks], axis=3)
    vb = jnp.concatenate([shift(vs), vs], axis=3)

    qi = jnp.arange(blk)[:, None] + blk
    ki = jnp.arange(2 * blk)[None, :]
    dist = qi - ki
    band = (dist >= 0) & (dist <= span)
    valid = band[None] & ((jnp.arange(nb) > 0)[:, None, None] | (ki >= blk)[None])
    bias = jnp.transpose(bias_table.astype(jnp.float32)[t5_causal_bucket(jnp.maximum(dist, 0) * dilation)], (2, 0, 1))

    logits = jnp.einsum('brnqhd,brnkhd->brnhqk', qs, kb) + bias[None, None, None]
    logits = jnp.where(valid[None, None, :, None], logits, -jnp.inf)
    m = jnp.max(logits, axis=-1, keepdims=True)
    p = jnp.exp(logits - m)
    l = jnp.sum(p, axis=-1, keepdims=True)
    o = jnp.einsum('brnhqk,brnkhd->brnqhd', p / l, vb)
    lse = (m + jnp.log(l))[..., 0]
    o = jnp.transpose(o, (0, 2, 3, 1, 4, 5)).reshape(Bsz, S_pad, H, dh)[:, :S]
    lse = jnp.transpose(lse, (0, 2, 4, 1, 3)).reshape(Bsz, S_pad, H)[:, :S]
    return o, lse

def dilated_attention_mixer(h, w_in, q_gain, k_gain, rel_bias, w_out):
    Bsz, S, _ = h.shape
    proj = (h @ w_in).reshape(Bsz, S, 3, DSW_N_GROUPS, DSW_HEADS, DSW_DH)
    q = rms_norm(proj[:, :, 0], q_gain) * (DSW_DH ** -0.5)
    k = rms_norm(proj[:, :, 1], k_gain)
    v = proj[:, :, 2].astype(jnp.float32)
    outs, lses = [], []
    for gi, (window, dilation) in enumerate(DSW_GROUPS):
        o, lse = dilated_window_group(q[:, :, gi], k[:, :, gi], v[:, :, gi],
                                      rel_bias[:, gi * DSW_HEADS:(gi + 1) * DSW_HEADS], window, dilation)
        outs.append(o)
        lses.append(lse)
    wts = jax.nn.softmax(jnp.stack(lses), axis=0)
    o = jnp.sum(wts[..., None] * jnp.stack(outs), axis=0)
    return o.reshape(Bsz, S, DSW_HG).astype(h.dtype) @ w_out

def swiglu(h, w_in, w_out):
    gate, up = jnp.split(h @ w_in, 2, axis=-1)
    return (jax.nn.silu(gate) * up) @ w_out

def first_inputs(seed: int = 0) -> dict:
    key = jax.random.key(seed)
    ks = jax.random.split(key, 20)
    nrm = lambda k, shape, s: jax.random.normal(k, shape, jnp.float32) * s
    D = D_MODEL
    a_init = jax.random.uniform(ks[10], (N_A_LAYERS, GDN_HEADS), jnp.float32, 1.0, 16.0)
    dt = jnp.exp(jax.random.uniform(ks[11], (N_A_LAYERS, GDN_HEADS), jnp.float32,
                                    math.log(1e-3), math.log(1e-1)))
    return {
        "x": nrm(ks[0], (BATCH, SEQ, D), 1.0),
        "c": nrm(ks[1], (BATCH, D), 1.0),
        "w_ada": nrm(ks[2], (DEPTH, D, 6 * D), D ** -0.5),
        "b_ada": nrm(ks[3], (DEPTH, 6 * D), 0.02),
        "norm_mix": 1.0 + nrm(ks[4], (DEPTH, D), 0.02),
        "norm_ffn": 1.0 + nrm(ks[5], (DEPTH, D), 0.02),
        "w_ffn_in": nrm(ks[6], (DEPTH, D, 2 * FFN_HIDDEN), D ** -0.5),
        "w_ffn_out": nrm(ks[7], (DEPTH, FFN_HIDDEN, D), FFN_HIDDEN ** -0.5),
        "gdn_w_in": nrm(ks[8], (N_A_LAYERS, D, GDN_IN), D ** -0.5),
        "gdn_conv": nrm(ks[9], (N_A_LAYERS, GDN_CONV, GDN_CONV_CH), GDN_CONV ** -0.5),
        "gdn_a_log": jnp.log(a_init),
        "gdn_dt_bias": dt + jnp.log(-jnp.expm1(-dt)),
        "gdn_out_norm": 1.0 + nrm(ks[12], (N_A_LAYERS, GDN_DV), 0.02),
        "gdn_w_out": nrm(ks[13], (N_A_LAYERS, GDN_HV, D), GDN_HV ** -0.5),
        "dsw_w_in": nrm(ks[14], (N_B_LAYERS, D, DSW_IN), D ** -0.5),
        "dsw_q_norm": 1.0 + nrm(ks[15], (N_B_LAYERS, DSW_DH), 0.02),
        "dsw_k_norm": 1.0 + nrm(ks[16], (N_B_LAYERS, DSW_DH), 0.02),
        "dsw_w_out": nrm(ks[17], (N_B_LAYERS, DSW_HG, D), DSW_HG ** -0.5),
        "rel_bias": nrm(ks[18], (REL_BUCKETS, REL_HEADS), 0.5),
    }

def first_block(x, c, w_ada, b_ada, norm_mix, norm_ffn, w_ffn_in, w_ffn_out,
              gdn_w_in, gdn_conv, gdn_a_log, gdn_dt_bias, gdn_out_norm, gdn_w_out,
              dsw_w_in, dsw_q_norm, dsw_k_norm, dsw_w_out, rel_bias):
    cond = jax.nn.silu(c.astype(jnp.float32))
    for layer in range(DEPTH):
        mod = (cond @ w_ada[layer].astype(jnp.float32) + b_ada[layer].astype(jnp.float32)).astype(x.dtype)
        sh1, sc1, g1, sh2, sc2, g2 = jnp.split(mod[:, None, :], 6, axis=-1)

        h = (rms_norm(x, norm_mix[layer]) * (1.0 + sc1) + sh1).astype(x.dtype)
        j = layer // N_MIXERS
        if layer % N_MIXERS == 0:
            y = gated_deltanet_mixer(h, gdn_w_in[j], gdn_conv[j], gdn_a_log[j], gdn_dt_bias[j],
                                     gdn_out_norm[j], gdn_w_out[j])
        else:
            y = dilated_attention_mixer(h, dsw_w_in[j], dsw_q_norm[j], dsw_k_norm[j],
                                        rel_bias, dsw_w_out[j])
        x = x + g1 * y

        h = (rms_norm(x, norm_ffn[layer]) * (1.0 + sc2) + sh2).astype(x.dtype)
        x = x + g2 * swiglu(h, w_ffn_in[layer], w_ffn_out[layer])
    return x


GRID_W = 64
CTX_LEN = 256
HEAD_DIM = 64
Q_BLOCK = 128
ROPE_THETA = 10000.0
EPS = 1e-6
N_MOD = 6

A_HEADS = D_MODEL // 256
A_VDIM = 2 * HEAD_DIM
B_HEADS = D_MODEL // 128
B_KV_HEADS = B_HEADS // 4
B_GROUP = B_HEADS // B_KV_HEADS
A_Q = A_HEADS * 2 * HEAD_DIM
A_K = A_HEADS * 2 * HEAD_DIM
A_V = A_HEADS * A_VDIM
B_Q = B_HEADS * HEAD_DIM
B_K = B_KV_HEADS * HEAD_DIM
B_V = B_KV_HEADS * HEAD_DIM
EVEN_SPLITS = [A_Q, A_Q + A_K, A_Q + A_K + A_V, A_Q + A_K + A_V + B_Q, A_Q + A_K + A_V + B_Q + B_K]
EVEN_IN = A_Q + A_K + A_V + B_Q + B_K + B_V
A_OUT = A_HEADS * A_VDIM
B_OUT = B_HEADS * HEAD_DIM

MLA_HEADS = D_MODEL // 64
MLA_NOPE = 64
MLA_ROPE = 32
MLA_VDIM = 64
MLA_Q_RANK = D_MODEL // 4
MLA_KV_RANK = D_MODEL // 8
ODD_IN = MLA_Q_RANK + MLA_KV_RANK + MLA_ROPE
MLA_OUT = MLA_HEADS * MLA_VDIM

N_EXPERTS = 16
EC_CAPACITY_FACTOR = 2
D_EXPERT = D_MODEL

N_EVEN = (DEPTH + 1) // 2
N_ODD = DEPTH // 2


def rmsnorm(x, g):
    xf = x.astype(jnp.float32)
    y = xf * lax.rsqrt(jnp.mean(xf * xf, axis=-1, keepdims=True) + EPS)
    return y.astype(x.dtype) * g

def modulate(h, shift, scale):
    return h * (1 + scale) + shift

def grid_angles(n_tokens, rot_dim):
    rows = n_tokens // GRID_W
    row = jnp.repeat(jnp.arange(rows, dtype=jnp.float32), GRID_W)
    col = jnp.tile(jnp.arange(GRID_W, dtype=jnp.float32), rows)
    half = rot_dim // 2
    freqs = ROPE_THETA ** (-jnp.arange(0, half, 2, dtype=jnp.float32) / half)
    return row[:, None] * freqs, col[:, None] * freqs

def rope_1d(x, ang):
    ang = ang.reshape((ang.shape[0],) + (1,) * (x.ndim - 3) + (ang.shape[1],))
    cos = jnp.cos(ang).astype(x.dtype)
    sin = jnp.sin(ang).astype(x.dtype)
    x1, x2 = jnp.split(x, 2, axis=-1)
    return jnp.concatenate([x1 * cos - x2 * sin, x2 * cos + x1 * sin], axis=-1)

def rope_2d(x, ang_row, ang_col):
    xr, xc = jnp.split(x, 2, axis=-1)
    return jnp.concatenate([rope_1d(xr, ang_row), rope_1d(xc, ang_col)], axis=-1)

def sweep_query_blocks(fn, *qs):
    bsz, t = qs[0].shape[:2]
    nb = t // Q_BLOCK
    blocks = tuple(jnp.moveaxis(q.reshape((bsz, nb, Q_BLOCK) + q.shape[2:]), 1, 0) for q in qs)
    out = lax.map(lambda qb: fn(*qb), blocks)
    return jnp.moveaxis(out, 0, 1).reshape((bsz, t) + out.shape[3:])

def diff_attend(q, k, v, lam, scale):
    s = jnp.einsum('bqhcd,bkhcd->bhcqk', q, k).astype(jnp.float32) * scale
    p = jax.nn.softmax(s, axis=-1)
    w = (p[:, :, 0] - lam * p[:, :, 1]).astype(v.dtype)
    return jnp.einsum('bhqk,bkhd->bqhd', w, v)

def gqa_attend(q, k, v, scale):
    s = jnp.einsum('bqhgd,bkhd->bhgqk', q, k).astype(jnp.float32) * scale
    p = jax.nn.softmax(s, axis=-1).astype(v.dtype)
    return jnp.einsum('bhgqk,bkhd->bqhgd', p, v)

def mla_attend(qn, qr, kn, kr, v, scale):
    s = jnp.einsum('bqhd,bkhd->bhqk', qn, kn) + jnp.einsum('bqhr,bkr->bhqk', qr, kr)
    p = jax.nn.softmax(s.astype(jnp.float32) * scale, axis=-1).astype(v.dtype)
    return jnp.einsum('bhqk,bkhd->bqhd', p, v)

def even_project(h, w_in, a_qk, b_qk):
    bsz, t = h.shape[:2]
    qa, ka, va, qb, kb, vb = jnp.split(h @ w_in, EVEN_SPLITS, axis=-1)
    qa = rmsnorm(qa.reshape(bsz, t, A_HEADS, 2, HEAD_DIM), a_qk[0])
    ka = rmsnorm(ka.reshape(bsz, t, A_HEADS, 2, HEAD_DIM), a_qk[1])
    va = va.reshape(bsz, t, A_HEADS, A_VDIM)
    qb = rmsnorm(qb.reshape(bsz, t, B_KV_HEADS, B_GROUP, HEAD_DIM), b_qk[0])
    kb = rmsnorm(kb.reshape(bsz, t, B_KV_HEADS, HEAD_DIM), b_qk[1])
    vb = vb.reshape(bsz, t, B_KV_HEADS, HEAD_DIM)
    return qa, ka, va, qb, kb, vb

def even_mixer(h_lat, h_ctx, w_in, a_qk, lam_vecs, a_subln, b_qk, w_out, layer_idx, ctx_out):
    lam_init = 0.8 - 0.6 * math.exp(-0.3 * layer_idx)
    lv = lam_vecs.astype(jnp.float32)
    lam = jnp.exp(jnp.sum(lv[0] * lv[1])) - jnp.exp(jnp.sum(lv[2] * lv[3])) + lam_init
    scale = HEAD_DIM ** -0.5
    qa_l, ka_l, va_l, qb_l, kb_l, vb_l = even_project(h_lat, w_in, a_qk, b_qk)
    qa_c, ka_c, va_c, qb_c, kb_c, vb_c = even_project(h_ctx, w_in, a_qk, b_qk)
    ang_row, ang_col = grid_angles(h_lat.shape[1], HEAD_DIM)
    qa_l, ka_l, qb_l, kb_l = (rope_2d(t, ang_row, ang_col) for t in (qa_l, ka_l, qb_l, kb_l))
    ka = jnp.concatenate([ka_l, ka_c], axis=1)
    va = jnp.concatenate([va_l, va_c], axis=1)
    kb = jnp.concatenate([kb_l, kb_c], axis=1)
    vb = jnp.concatenate([vb_l, vb_c], axis=1)
    oa_l = sweep_query_blocks(lambda q: diff_attend(q, ka, va, lam, scale), qa_l)
    ob_l = sweep_query_blocks(lambda q: gqa_attend(q, kb, vb, scale), qb_l)

    def merge(oa, ob):
        bsz, t = oa.shape[:2]
        oa = rmsnorm(oa, a_subln) * (1.0 - lam_init)
        return jnp.concatenate([oa.reshape(bsz, t, A_OUT), ob.reshape(bsz, t, B_OUT)], axis=-1) @ w_out

    y_lat = merge(oa_l, ob_l)
    y_ctx = None
    if ctx_out:
        y_ctx = merge(diff_attend(qa_c, ka_c, va_c, lam, scale), gqa_attend(qb_c, kb_c, vb_c, scale))
    return y_lat, y_ctx

def mla_project(h, w_in, q_norm, w_q_up, kv_norm, w_kv_up, qk_norm):
    bsz, t = h.shape[:2]
    cq, ckv, kr = jnp.split(h @ w_in, [MLA_Q_RANK, MLA_Q_RANK + MLA_KV_RANK], axis=-1)
    q = (rmsnorm(cq, q_norm) @ w_q_up).reshape(bsz, t, MLA_HEADS, MLA_NOPE + MLA_ROPE)
    kv = (rmsnorm(ckv, kv_norm) @ w_kv_up).reshape(bsz, t, MLA_HEADS, MLA_NOPE + MLA_VDIM)
    qn = rmsnorm(q[..., :MLA_NOPE], qk_norm[0, :MLA_NOPE])
    qr = rmsnorm(q[..., MLA_NOPE:], qk_norm[0, MLA_NOPE:])
    kn = rmsnorm(kv[..., :MLA_NOPE], qk_norm[1, :MLA_NOPE])
    v = kv[..., MLA_NOPE:]
    kr = rmsnorm(kr, qk_norm[1, MLA_NOPE:])
    return qn, qr, kn, kr, v

def odd_mixer(h_lat, h_ctx, w_in, q_norm, w_q_up, kv_norm, w_kv_up, qk_norm, w_out, ctx_out):
    scale = (MLA_NOPE + MLA_ROPE) ** -0.5
    qn_l, qr_l, kn_l, kr_l, v_l = mla_project(h_lat, w_in, q_norm, w_q_up, kv_norm, w_kv_up, qk_norm)
    qn_c, qr_c, kn_c, kr_c, v_c = mla_project(h_ctx, w_in, q_norm, w_q_up, kv_norm, w_kv_up, qk_norm)
    ang_row, ang_col = grid_angles(h_lat.shape[1], MLA_ROPE)
    qr_l = rope_2d(qr_l, ang_row, ang_col)
    kr_l = rope_2d(kr_l, ang_row, ang_col)
    kn = jnp.concatenate([kn_l, kn_c], axis=1)
    kr = jnp.concatenate([kr_l, kr_c], axis=1)
    v = jnp.concatenate([v_l, v_c], axis=1)
    o_l = sweep_query_blocks(lambda a, b: mla_attend(a, b, kn, kr, v, scale), qn_l, qr_l)
    bsz, t = h_lat.shape[:2]
    y_lat = o_l.reshape(bsz, t, MLA_OUT) @ w_out
    y_ctx = None
    if ctx_out:
        o_c = mla_attend(qn_c, qr_c, kn_c, kr_c, v_c, scale)
        y_ctx = o_c.reshape(bsz, h_ctx.shape[1], MLA_OUT) @ w_out
    return y_lat, y_ctx

def ec_moe(h, w_router, w_gate, w_up, w_down):
    bsz, t, d = h.shape
    cap = EC_CAPACITY_FACTOR * t // N_EXPERTS
    aff = jax.nn.softmax(jnp.einsum('btd,de->bte', h, w_router).astype(jnp.float32), axis=-1)
    gates, idx = lax.top_k(jnp.swapaxes(aff, 1, 2), cap)
    xs = jax.vmap(lambda hb, ib: hb[ib])(h, idx)
    a = jnp.einsum('becd,edf->becf', xs, w_gate)
    u = jnp.einsum('becd,edf->becf', xs, w_up)
    y = jnp.einsum('becf,efd->becd', jax.nn.silu(a) * u, w_down)
    y = y * gates[..., None].astype(y.dtype)
    return jax.vmap(lambda yb, ib: jnp.zeros((t, d), y.dtype).at[ib.reshape(-1)].add(yb.reshape(-1, d)))(y, idx)

def second_inputs(seed: int = 0) -> dict:
    key = jax.random.key(seed)
    ks = iter(jax.random.split(key, 32))

    def nrm(shape, scale):
        return jax.random.normal(next(ks), shape, jnp.float32) * scale

    def gain(shape):
        return 1.0 + nrm(shape, 0.1)

    D = D_MODEL
    return {
        'x': nrm((BATCH, SEQ, D), 1.0),
        'c': nrm((BATCH, D), 1.0),
        'ctx': nrm((BATCH, CTX_LEN, D), 1.0),
        'c_ctx': nrm((D,), 1.0),
        'w_ada': nrm((DEPTH, D, N_MOD * D), 0.5 * D ** -0.5),
        'b_ada': nrm((DEPTH, N_MOD * D), 0.01),
        'norm_mix': gain((DEPTH, D)),
        'norm_ffn': gain((DEPTH, D)),
        'w_in_even': nrm((N_EVEN, D, EVEN_IN), D ** -0.5),
        'a_qk_norm': gain((N_EVEN, 2, HEAD_DIM)),
        'diff_lambda': nrm((N_EVEN, 4, HEAD_DIM), 0.1),
        'a_subln': gain((N_EVEN, A_VDIM)),
        'b_qk_norm': gain((N_EVEN, 2, HEAD_DIM)),
        'w_out_even': nrm((N_EVEN, A_OUT + B_OUT, D), (A_OUT + B_OUT) ** -0.5),
        'w_in_odd': nrm((N_ODD, D, ODD_IN), D ** -0.5),
        'mla_q_norm': gain((N_ODD, MLA_Q_RANK)),
        'w_q_up': nrm((N_ODD, MLA_Q_RANK, MLA_HEADS * (MLA_NOPE + MLA_ROPE)), MLA_Q_RANK ** -0.5),
        'mla_kv_norm': gain((N_ODD, MLA_KV_RANK)),
        'w_kv_up': nrm((N_ODD, MLA_KV_RANK, MLA_HEADS * (MLA_NOPE + MLA_VDIM)), MLA_KV_RANK ** -0.5),
        'mla_qk_norm': gain((N_ODD, 2, MLA_NOPE + MLA_ROPE)),
        'w_out_odd': nrm((N_ODD, MLA_OUT, D), MLA_OUT ** -0.5),
        'w_router': nrm((DEPTH, D, N_EXPERTS), D ** -0.5),
        'w_exp_gate': nrm((DEPTH, N_EXPERTS, D, D_EXPERT), D ** -0.5),
        'w_exp_up': nrm((DEPTH, N_EXPERTS, D, D_EXPERT), D ** -0.5),
        'w_exp_down': nrm((DEPTH, N_EXPERTS, D_EXPERT, D), D_EXPERT ** -0.5),
    }

def second_block(x, c, ctx, c_ctx, w_ada, b_ada, norm_mix, norm_ffn, w_in_even, a_qk_norm, diff_lambda,
              a_subln, b_qk_norm, w_out_even, w_in_odd, mla_q_norm, w_q_up, mla_kv_norm, w_kv_up,
              mla_qk_norm, w_out_odd, w_router, w_exp_gate, w_exp_up, w_exp_down):
    bsz = x.shape[0]
    sc = jax.nn.silu(c)
    sc_ctx = jax.nn.silu(c_ctx)
    for i in range(DEPTH):
        last = i == DEPTH - 1
        m = (sc @ w_ada[i] + b_ada[i]).reshape(bsz, 1, N_MOD, D_MODEL)
        mc = (sc_ctx @ w_ada[i] + b_ada[i]).reshape(N_MOD, D_MODEL)
        h_lat = modulate(rmsnorm(x, norm_mix[i]), m[:, :, 0], m[:, :, 1])
        h_ctx = modulate(rmsnorm(ctx, norm_mix[i]), mc[0], mc[1])
        if i % 2 == 0:
            j = i // 2
            y_lat, y_ctx = even_mixer(h_lat, h_ctx, w_in_even[j], a_qk_norm[j], diff_lambda[j], a_subln[j],
                                      b_qk_norm[j], w_out_even[j], i, not last)
        else:
            j = i // 2
            y_lat, y_ctx = odd_mixer(h_lat, h_ctx, w_in_odd[j], mla_q_norm[j], w_q_up[j], mla_kv_norm[j],
                                     w_kv_up[j], mla_qk_norm[j], w_out_odd[j], not last)
        x = x + m[:, :, 2] * y_lat
        h_lat = modulate(rmsnorm(x, norm_ffn[i]), m[:, :, 3], m[:, :, 4])
        x = x + m[:, :, 5] * ec_moe(h_lat, w_router[i], w_exp_gate[i], w_exp_up[i], w_exp_down[i])
        if not last:
            ctx = ctx + mc[2] * y_ctx
            h_ctx = modulate(rmsnorm(ctx, norm_ffn[i]), mc[3], mc[4])
            ctx = ctx + mc[5] * ec_moe(h_ctx, w_router[i], w_exp_gate[i], w_exp_up[i], w_exp_down[i])
    return x


def setup_inputs(seed=0):
    out = dict(first_inputs(seed))
    for name, value in second_inputs(seed + 1).items():
        if name != "x":
            out[name + "_2"] = value
    return out


def reference(
    x, c, w_ada, b_ada, norm_mix, norm_ffn, w_ffn_in, w_ffn_out, gdn_w_in, gdn_conv, gdn_a_log,
    gdn_dt_bias, gdn_out_norm, gdn_w_out, dsw_w_in, dsw_q_norm, dsw_k_norm, dsw_w_out, rel_bias,
    c_2, ctx_2, c_ctx_2, w_ada_2, b_ada_2, norm_mix_2, norm_ffn_2, w_in_even_2, a_qk_norm_2,
    diff_lambda_2, a_subln_2, b_qk_norm_2, w_out_even_2, w_in_odd_2, mla_q_norm_2, w_q_up_2,
    mla_kv_norm_2, w_kv_up_2, mla_qk_norm_2, w_out_odd_2, w_router_2, w_exp_gate_2, w_exp_up_2,
    w_exp_down_2,
):
    x = first_block(
        x, c, w_ada, b_ada, norm_mix, norm_ffn, w_ffn_in, w_ffn_out, gdn_w_in, gdn_conv,
        gdn_a_log, gdn_dt_bias, gdn_out_norm, gdn_w_out, dsw_w_in, dsw_q_norm, dsw_k_norm,
        dsw_w_out, rel_bias,
    )
    return second_block(
        x, c_2, ctx_2, c_ctx_2, w_ada_2, b_ada_2, norm_mix_2, norm_ffn_2, w_in_even_2,
        a_qk_norm_2, diff_lambda_2, a_subln_2, b_qk_norm_2, w_out_even_2, w_in_odd_2,
        mla_q_norm_2, w_q_up_2, mla_kv_norm_2, w_kv_up_2, mla_qk_norm_2, w_out_odd_2,
        w_router_2, w_exp_gate_2, w_exp_up_2, w_exp_down_2,
    )


_drawn_inputs = setup_inputs


def setup_inputs(seed=0):
    import zlib

    import numpy as np

    out = dict(_drawn_inputs(seed))
    spreads = {}
    factors = {'norm_mix': 3.639,
     'norm_ffn': 2.934,
     'gdn_out_norm': 5.358,
     'dsw_q_norm': 8.0,
     'dsw_k_norm': 8.0,
     'b_ada_2': 6.624,
     'norm_mix_2': 4.557,
     'norm_ffn_2': 3.353,
     'a_qk_norm_2': 7.929,
     'diff_lambda_2': 5.857,
     'a_subln_2': 4.099,
     'b_qk_norm_2': 8.0,
     'mla_q_norm_2': 8.0,
     'mla_kv_norm_2': 8.0,
     'mla_qk_norm_2': 8.0}
    for name, (base, spread) in spreads.items():
        noise = np.random.default_rng([zlib.crc32(name.encode()), seed]).standard_normal(out[name].shape)
        drawn = base * np.exp(spread * noise) if base else spread * noise
        out[name] = __import__('jax').numpy.asarray(drawn.astype(out[name].dtype))
    for name, factor in factors.items():
        out[name] = (out[name] * factor).astype(out[name].dtype)
    return out
```

```python
import math
from contextlib import ExitStack

import numpy as np
import concourse.bass as bass
from concourse import mybir

F32 = mybir.dt.float32
ALU = mybir.AluOpType
ACT = mybir.ActivationFunctionType
AX = mybir.AxisListType

P = 128
D = 1024
KC = D // P
S = 256
NT = S // P
STRIP = 512
SLOTS = 6
SLOT = KC * STRIP
EPS = 1e-6
HIDDEN = 2816
HC = HIDDEN // P
N_MOD = 6
MODC = N_MOD * KC
GH = 8
CH = 64
TAPS = 4
LEVELS = [1, 2, 4, 8, 16, 32]
EXPERTS = 16
CAP = 2 * S // EXPERTS


class Ring:

    def __init__(self, nc, ctx):
        self.tile = ctx.enter_context(nc.sbuf_tensor("weight_ring", [P, SLOTS, SLOT], F32))
        self.full = [ctx.enter_context(nc.semaphore(f"ring_full_{s}")) for s in range(SLOTS)]
        self.read = [ctx.enter_context(nc.semaphore(f"ring_read_{s}")) for s in range(SLOTS)]
        self.units = []
        self.loaded = 0
        self.taken = 0

    def take(self, count):
        first = self.taken
        self.taken += count
        return first

    def view(self, n):
        _, k, w = self.units[n]
        return self.tile[:, n % SLOTS, 0:k * w].rearrange("p (k w) -> p k w", k=k)

    def load(self, sp, n):
        if n >= SLOTS:
            sp.wait_ge(self.read[n % SLOTS], n // SLOTS)
        sp.dma_start(self.view(n), self.units[n][0]).then_inc(self.full[n % SLOTS], 16)

    def load_ahead(self, sp, upto):
        while self.loaded < min(upto, len(self.units)):
            self.load(sp, self.loaded)
            self.loaded += 1

    def wait(self, pe, n):
        pe.wait_ge(self.full[n % SLOTS], 16 * (n // SLOTS + 1))

    def wait_read(self, eng, n):
        eng.wait_ge(self.read[n % SLOTS], n // SLOTS + 1)


class Core:

    def __init__(self, nc, ctx):
        self.nc = nc
        sb = lambda name, shape: ctx.enter_context(nc.sbuf_tensor(name, shape, F32))
        self.ring = Ring(nc, ctx)
        self.x = sb("x", [P, NT, D])
        self.ctx_x = sb("ctx_x", [P, NT, D])
        self.hT = sb("hT", [P, KC, 2 * S])
        self.ident = sb("ident", [P, P])
        self.ones = sb("ones", [P, P])
        self.mods = sb("mods", [P, 4, MODC, 2])
        self.cond = sb("cond", [P, 2, KC, 32])
        self.norms = sb("norms", [P, 88])
        self.bias = sb("bias", [P, 4, MODC])
        self.convw = sb("convw", [P, TAPS, 24])
        self.half = sb("half", [P, 16])
        self.stored = ctx.enter_context(nc.semaphore("result_stored"))
        self.ps = ctx.enter_context(nc.psum_tensor("ps", [P, 8, STRIP], F32))

    def gain(self, kind, s):
        v = (s // 2) * 4 + kind * 2 + s % 2
        return self.norms[:, v * KC:(v + 1) * KC]

    def mod(self, s, which, m=0):
        return self.mods[:, s, which * KC:(which + 1) * KC, m]


class Stage:

    def __init__(self, core, name):
        self.core, self.nc, self.name = core, core.nc, name
        self.sems = []
        self.stack = ExitStack()

    def sb(self, name, shape):
        return self.stack.enter_context(self.nc.sbuf_tensor(f"{self.name}_{name}", shape, F32))

    def sem(self, name):
        s = self.nc.alloc_semaphore(f"{self.name}_{name}")
        self.sems.append(s)
        return s

    def __enter__(self):
        return self

    def block(self):
        return self.nc.Block(no_gpsimd_drain=True)

    def __exit__(self, *error):
        self.stack.__exit__(*error)
        if error[0] is None and self.sems:
            for s in self.sems:
                self.nc.gpsimd.sem_clear(s)
                self.nc.release_semaphore(s)
        return False


def ring_in_stage(core, block, count):
    ring = core.ring

    @block.sync
    def _(sp):
        ring.load_ahead(sp, ring.taken + SLOTS)


def stage_setup(core, t):
    nc, ps = core.nc, core.ps
    with Stage(core, "setup") as st:
        rows = st.sb("rows", [96, 4, P])
        filled = st.sem("filled")
        loaded_const, loaded_x, loaded_rows = st.sem("loaded_const"), st.sem("loaded_x"), st.sem("loaded_rows")
        transposed, cols_ready, zeroed, conds = (st.sem(n) for n in ("transposed", "cols_ready", "zeroed", "conds"))
        row_loads = [(0, rows[0:16, 0, :], t["norm_mix"].rearrange("l (c p) -> (l c) p", p=P)),
                     (0, rows[16:32, 0, :], t["norm_ffn"].rearrange("l (c p) -> (l c) p", p=P)),
                     (0, rows[32:48, 0, :], t["norm_mix_2"].rearrange("l (c p) -> (l c) p", p=P)),
                     (0, rows[48:64, 0, :], t["norm_ffn_2"].rearrange("l (c p) -> (l c) p", p=P)),
                     (0, rows[64:72, 0, :], t["c"].rearrange("l (c p) -> (l c) p", p=P)),
                     (0, rows[72:80, 0, :], t["c_2"].rearrange("l (c p) -> (l c) p", p=P)),
                     (0, rows[80:88, 0, :], t["c_ctx_2"].rearrange("(c p) -> c p", p=P)),
                     (0, rows[:, 1, :], t["b_ada"].rearrange("l (c p) -> (l c) p", p=P)),
                     (0, rows[:, 2, :], t["b_ada_2"].rearrange("l (c p) -> (l c) p", p=P)),
                     (0, rows[:, 3, :], t["gdn_conv"].rearrange("l k (c p) -> (l k c) p", p=P))]
        with st.block() as block:
            @block.sync
            def _(sp):
                core.ring.load_ahead(sp, SLOTS)

            @block.scalar
            def _(act):
                act.dma_start(core.ident[:], t["const"][:, 0:P]).then_inc(loaded_const, 16)
                for _, dst, src in row_loads:
                    act.dma_start(dst, src).then_inc(loaded_rows, 16)
                act.dma_start(core.x[:], t["x"].rearrange("b (j p) d -> p (b j) d", p=P)).then_inc(loaded_x, 16)
                act.wait_ge(transposed, 1)
                act.wait_ge(zeroed, 1)
                pairs = ((64, 64), (72, 80))
                for b in range(2):
                    for m in range(2):
                        v = pairs[b][m]
                        nc.scalar.activation(core.cond[:, b, :, m], ps[:, 0, v:v + KC], ACT.Silu).then_inc(conds, 1)
                act.wait_ge(conds, 4)
                act.wait_ge(loaded_x, 16)
                act.wait_ge(filled, 2)

            @block.gpsimd
            def _(pool):
                nc.gpsimd.memset(core.half[:], -0.5).then_inc(filled, 1)
                nc.gpsimd.memset(core.ones[:], 1.0).then_inc(filled, 1)

            @block.tensor
            def _(pe):
                pe.wait_ge(loaded_const, 16)
                pe.wait_ge(loaded_rows, 16 * len(row_loads))
                for i in range(4):
                    n = 88 if i == 0 else 96
                    nc.tensor.transpose(ps[:, i, 0:n], rows[0:n, i, :], core.ident[0:n, 0:n]).then_inc(transposed, 1)

            @block.vector
            def _(dve):
                nc.vector.memset(core.cond[:], 0.0).then_inc(zeroed, 1)
                dve.wait_ge(transposed, 4)
                dve.wait_ge(conds, 4)
                nc.vector.tensor_copy(core.norms[:], ps[:, 0, 0:88])
                nc.vector.tensor_copy(core.bias[:, 0:2, :], ps[:, 1, 0:96].rearrange("p (l c) -> p l c", l=2))
                nc.vector.tensor_copy(core.bias[:, 2:4, :], ps[:, 2, 0:96].rearrange("p (l c) -> p l c", l=2))
                nc.vector.tensor_copy(core.convw[:], ps[:, 3, 0:96].rearrange("p (k c) -> p k c", k=TAPS))


ADA_COLS = 2048


def ada_units(w, layer):
    return [(w[layer, 2 * P * i:2 * P * (i + 1), g * ADA_COLS:(g + 1) * ADA_COLS].rearrange("(k p) n -> p k n", p=P), 2, ADA_COLS)
            for g in range(3) for i in range(4)]


class Modulation:

    def __init__(self, core, st, groups):
        self.core, self.groups = core, groups
        self.first = core.ring.take(4 * len(groups))
        self.rows = st.sb("mod_rows", [P, STRIP])
        self.rows_copied, self.turned, self.stored = (st.sem("mod_" + n) for n in ("rows_copied", "turned", "stored"))

    def multiply(self, pe, u):
        nc, ps, ring = self.core.nc, self.core.ps, self.core.ring
        q, i = u // 4, u % 4
        s, _, bank, _ = self.groups[q]
        if q and i == 0:
            pe.wait_ge(self.rows_copied, q)
        ring.wait(pe, self.first + u)
        for k in range(2):
            for f in range(4):
                last = nc.tensor.matmul(ps[32 * f:32 * f + 32, bank, :], self.core.cond[:, s // 2, 2 * i + k, :],
                                        ring.view(self.first + u)[:, k, f * STRIP:(f + 1) * STRIP],
                                        start=(i + k == 0), stop=(i + k == 4), skip_group_check=True)
        last.then_inc(ring.read[(self.first + u) % SLOTS], 1)

    def copy(self, act, q):
        self.core.ring.wait_read(act, self.first + 4 * q + 3)
        if q:
            act.wait_ge(self.turned, q)
        self.core.nc.scalar.activation(self.rows[:], self.core.ps[:, self.groups[q][2], :], ACT.Copy).then_inc(self.rows_copied, 1)

    def turn(self, pe, q):
        nc, ps = self.core.nc, self.core.ps
        pe.wait_ge(self.rows_copied, q + 1)
        if q:
            pe.wait_ge(self.stored, q)
        for n in range(4):
            last = nc.tensor.transpose(ps[:, self.groups[q][3], n * P:(n + 1) * P], self.rows[:, n * P:(n + 1) * P], self.core.ident[:])
        last.then_inc(self.turned, 1)

    def store(self, dve, q):
        core, nc = self.core, self.core.nc
        s, g, _, bank = self.groups[q]
        dve.wait_ge(self.turned, q + 1)
        src = core.ps[:, bank, :].rearrange("p (n f r) -> p f n r", n=4, f=4)
        for m in range(2):
            out = core.mods[:, s, 16 * g:16 * (g + 1), m].rearrange("p (f n) -> p f n", f=4)
            b = core.bias[:, s, 16 * g:16 * (g + 1)].rearrange("p (f n) -> p f n", f=4)
            last = nc.vector.tensor_tensor(out, src[:, :, :, m], b, ALU.add)
        last.then_inc(self.stored, 1)


def stage_ada(core, s):
    with Stage(core, f"ada{s}") as st:
        mod = Modulation(core, st, [(s, g, g % 2, 2 + g % 2) for g in range(3)])
        with st.block() as block:
            ring_in_stage(core, block, 12)

            @block.tensor
            def _(pe):
                for g in range(3):
                    for i in range(4):
                        mod.multiply(pe, 4 * g + i)
                    mod.turn(pe, g)

            @block.scalar
            def _(act):
                for g in range(3):
                    mod.copy(act, g)

            @block.vector
            def _(dve):
                for g in range(3):
                    mod.store(dve, g)


def stage_norm(core, s, kind, streams, name, xn_keep=None):
    nc, ps = core.nc, core.ps
    T = NT * len(streams)
    with Stage(core, name) as st:
        junk = st.sb("junk", [P, D])
        xn = xn_keep if xn_keep is not None else st.sb("xn", [P, T, D])
        ssq, rstd, ms = st.sb("ssq", [P, T]), st.sb("rstd", [P, T]), st.sb("ms", [P, T])
        scale = st.sb("scale", [P, 2, KC])
        squared, mean, rstds, normed, turned, scales = (st.sem(n) for n in ("squared", "mean", "rstds", "normed", "turned", "scales"))
        with st.block() as block:
            @block.scalar
            def _(act):
                for j in range(T):
                    if j:
                        act.wait_ge(squared, j)
                    nc.scalar.activation(junk[:], streams[j // NT][0][:, j % NT, :], ACT.Square,
                                         accum_out=ssq[:, j:j + 1]).then_inc(squared, 1)
                act.wait_ge(scales, 2 * len(streams))
                for c in range(0, KC, 2):
                    act.wait_ge(turned, c + 1)
                    for i, (_, m) in enumerate(streams):
                        nc.scalar.activation(core.hT[:, c, i * S:(i + 1) * S], ps[:, c, i * S:(i + 1) * S], ACT.Identity,
                                             bias=core.mod(s, 3 * kind, m)[:, c:c + 1], scale=scale[:, m, c:c + 1])

            @block.gpsimd
            def _(pool):
                pool.wait_ge(squared, T)
                nc.gpsimd.tensor_scalar(ms[:], ssq[:], 1.0 / D, EPS, ALU.mult, ALU.add).then_inc(mean, 1)
                pool.wait_ge(mean, 1)
                nc.gpsimd.tensor_tensor(rstd[:], ms[:], core.half[:, 0:T], ALU.pow).then_inc(rstds, 1)

            @block.vector
            def _(dve):
                for i, (_, m) in enumerate(streams):
                    nc.vector.tensor_scalar(scale[:, m, :], core.mod(s, 3 * kind + 1, m), 1.0, None, ALU.add).then_inc(scales, 1)
                    dve.wait_ge(scales, 2 * i + 1)
                    nc.vector.tensor_tensor(scale[:, m, :], scale[:, m, :], core.gain(kind, s), ALU.mult).then_inc(scales, 1)
                dve.wait_ge(rstds, 1)
                for j in range(T):
                    nc.vector.tensor_scalar(xn[:, j, :], streams[j // NT][0][:, j % NT, :], rstd[:, j:j + 1], None,
                                            ALU.mult).then_inc(normed, 1)
                dve.wait_ge(scales, 2 * len(streams))
                for c in range(1, KC, 2):
                    dve.wait_ge(turned, c + 1)
                    for i, (_, m) in enumerate(streams):
                        nc.vector.tensor_scalar(core.hT[:, c, i * S:(i + 1) * S], ps[:, c, i * S:(i + 1) * S],
                                                scale[:, m, c:c + 1], core.mod(s, 3 * kind, m)[:, c:c + 1], ALU.mult, ALU.add)

            @block.tensor
            def _(pe):
                pe.wait_ge(normed, T)
                for c in range(KC):
                    for j in range(T):
                        last = nc.tensor.transpose(ps[:, c, j * P:(j + 1) * P], xn[:, j, c * P:(c + 1) * P], core.ident[:])
                    last.then_inc(turned, 1)


def k_units(w, c0, c1, rows=D):
    out = []
    for k0 in range(0, rows // P, KC):
        k1 = min(k0 + KC, rows // P)
        out.append((w[k0 * P:k1 * P, c0:c1].rearrange("(k p) n -> p k n", p=P), k1 - k0, c1 - c0))
    return out


def strips(cols):
    return [(c, min(c + STRIP, cols)) for c in range(0, cols, STRIP)]


def residual_units(w, rows):
    return [u for c0, c1 in strips(D) for u in k_units(w, c0, c1, rows)]


def project_strip(core, pe, lhs, tiles, first, count, banks):
    nc, ring = core.nc, core.ring
    total = sum(ring.units[i][1] for i in range(first, first + count))
    k0 = 0
    for n in range(first, first + count):
        ring.wait(pe, n)
        kc, w = ring.units[n][1:]
        for j in range(tiles):
            for k in range(kc):
                last = nc.tensor.matmul(core.ps[:, banks[j], 0:w], lhs(k0 + k, j), ring.view(n)[:, k, :],
                                        start=(k0 + k == 0), stop=(k0 + k == total - 1))
        last.then_inc(ring.read[n % SLOTS], 1)
        k0 += kc


def stage_residual(core, name, s, which, lhs, rows, streams, rhs=None):
    nc, ps, ring = core.nc, core.ps, core.ring
    T = NT * len(streams)
    per = (rows // P + KC - 1) // KC
    with Stage(core, name) as st:
        diag = st.sb("diag", [P, len(streams), D])
        gate = st.sb("gate", [P, len(streams), D])
        part = st.sb("part", [P, 2, STRIP])
        diags, spread, gates, gated, added = (st.sem(n) for n in ("diags", "spread", "gates", "gated", "added"))
        first = ring.take(0 if rhs else 2 * per)
        multiplied = st.sem("multiplied")

        def product(pe, n, banks):
            if not rhs:
                return project_strip(core, pe, lhs, T, first + n * per, per, banks)
            for j in range(T):
                for k in range(rows // P):
                    last = nc.tensor.matmul(ps[:, banks[j], :], lhs(k, j), rhs(k, j // NT, n), start=(k == 0), stop=(k == rows // P - 1))
            last.then_inc(multiplied, 1)

        with st.block() as block:
            ring_in_stage(core, block, 2 * per)

            @block.tensor
            def _(pe):
                pe.wait_ge(diags, len(streams))
                for i in range(len(streams)):
                    for half in range(2):
                        last = nc.tensor.matmul(ps[:, 2 * i + half, :], core.ones[:], diag[:, i, half * STRIP:(half + 1) * STRIP],
                                                start=True, stop=True)
                last.then_inc(spread, 1)
                product(pe, 0, [4 + j for j in range(T)])
                pe.wait_ge(gates, 1)
                product(pe, 1, list(range(T)))

            @block.scalar
            def _(act):
                act.wait_ge(spread, 1)
                nc.scalar.activation(gate[:].rearrange("p i n -> p (i n)"),
                                     ps[:, 0:2 * len(streams), :].rearrange("p b n -> p (b n)"), ACT.Copy).then_inc(gates, 1)

            @block.vector
            def _(dve):
                for i, (_, m) in enumerate(streams):
                    nc.vector.tensor_tensor(diag[:, i, :].rearrange("p (c q) -> p c q", c=KC),
                                            core.ident[:].unsqueeze(1).broadcast_to([P, KC, P]),
                                            core.mod(s, which, m).unsqueeze(2).broadcast_to([P, KC, P]), ALU.mult).then_inc(diags, 1)
                dve.wait_ge(gates, 1)
                i = 0
                for n in range(2):
                    if rhs:
                        dve.wait_ge(multiplied, n + 1)
                    else:
                        ring.wait_read(dve, first + (n + 1) * per - 1)
                    for j in range(T):
                        if i >= 2:
                            dve.wait_ge(added, i - 1)
                        nc.vector.tensor_tensor(part[:, i % 2, :], ps[:, (4 if n == 0 else 0) + j, :],
                                                gate[:, j // NT, n * STRIP:(n + 1) * STRIP], ALU.mult).then_inc(gated, 1)
                        i += 1
                dve.wait_ge(added, 2 * T)

            @block.gpsimd
            def _(pool):
                i = 0
                for n in range(2):
                    for j in range(T):
                        pool.wait_ge(gated, i + 1)
                        x = streams[j // NT][0][:, j % NT, n * STRIP:(n + 1) * STRIP]
                        nc.gpsimd.tensor_tensor(x, x, part[:, i % 2, :], ALU.add).then_inc(added, 1)
                        i += 1


def ffn_units(w, layer):
    out = []
    for c0, c1 in strips(HIDDEN):
        out += k_units(w[layer], c0, c1) + k_units(w[layer], HIDDEN + c0, HIDDEN + c1)
    return out


def stage_ffn(core, name, aT):
    nc, ps, ring = core.nc, core.ps, core.ring
    pairs = strips(HIDDEN)
    with Stage(core, name) as st:
        sg = st.sb("sg", [P, 2, NT, STRIP])
        a = st.sb("a", [P, 2, NT, STRIP])
        silus, products, turned, copied = (st.sem(n) for n in ("silus", "products", "turned", "copied"))
        first = ring.take(2 * len(pairs))
        with st.block() as block:
            ring_in_stage(core, block, 2 * len(pairs))

            @block.tensor
            def _(pe):
                def turn(i):
                    pe.wait_ge(products, i + 1)
                    for j in range(NT):
                        for q in range((pairs[i][1] - pairs[i][0]) // P):
                            last = nc.tensor.transpose(ps[:, 4 * (i % 2) + j, q * P:(q + 1) * P],
                                                       a[:, i % 2, j, q * P:(q + 1) * P], core.ident[:])
                    last.then_inc(turned, 1)
                for i in range(len(pairs)):
                    if i >= 2:
                        pe.wait_ge(copied, i - 1)
                    for up in range(2):
                        project_strip(core, pe, lambda k, j: core.hT[:, k, j * P:(j + 1) * P], NT, first + 2 * i + up, 1,
                                      [4 * (i % 2) + 2 * up + j for j in range(NT)])
                    if i >= 1:
                        turn(i - 1)
                turn(len(pairs) - 1)

            @block.scalar
            def _(act):
                def copy(i):
                    w = pairs[i][1] - pairs[i][0]
                    act.wait_ge(turned, i + 1)
                    for j in range(NT):
                        last = nc.scalar.activation(aT[:, pairs[i][0] // P:pairs[i][1] // P, j * P:(j + 1) * P],
                                                    ps[:, 4 * (i % 2) + j, 0:w].rearrange("p (q t) -> p q t", t=P), ACT.Copy)
                    last.then_inc(copied, 1)
                for i, (c0, c1) in enumerate(pairs):
                    ring.wait_read(act, first + 2 * i)
                    if i >= 2:
                        act.wait_ge(products, i - 1)
                    for j in range(NT):
                        last = nc.scalar.activation(sg[:, i % 2, j, 0:c1 - c0], ps[:, 4 * (i % 2) + j, 0:c1 - c0], ACT.Silu)
                    last.then_inc(silus, 1)
                    if i >= 1:
                        copy(i - 1)
                copy(len(pairs) - 1)

            @block.vector
            def _(dve):
                for i, (c0, c1) in enumerate(pairs):
                    dve.wait_ge(silus, i + 1)
                    ring.wait_read(dve, first + 2 * i + 1)
                    if i >= 2:
                        dve.wait_ge(turned, i - 1)
                    for j in range(NT):
                        last = nc.vector.tensor_tensor(a[:, i % 2, j, 0:c1 - c0], sg[:, i % 2, j, 0:c1 - c0],
                                                       ps[:, 4 * (i % 2) + 2 + j, 0:c1 - c0], ALU.mult)
                    last.then_inc(products, 1)


def stage_gdn_project(core, t, conv, zs, ab):
    nc, ps, ring = core.nc, core.ps, core.ring
    with Stage(core, "gdnproj") as st:
        pre = st.sb("pre", [P, 2, 4, TAPS - 1 + S])
        acc = st.sb("acc", [P, 2, 4, S])
        padded, pre_copied, convolved, tap, silus = (st.sem(n) for n in ("padded", "pre_copied", "convolved", "tap", "silus"))
        first = ring.take(9)
        with st.block() as block:
            ring_in_stage(core, block, 9)

            @block.tensor
            def _(pe):
                for u in range(6):
                    ring.wait(pe, first + u)
                    if u >= 2:
                        pe.wait_ge(pre_copied, u - 1)
                    w = ring.view(first + u)
                    for q in range(4):
                        for k in range(KC):
                            last = nc.tensor.matmul(ps[:, 2 * (u % 2) + q // 2, (q % 2) * S:(q % 2 + 1) * S],
                                                    w[:, k, q * P:(q + 1) * P], core.hT[:, k, 0:S],
                                                    start=(k == 0), stop=(k == KC - 1))
                    last.then_inc(ring.read[(first + u) % SLOTS], 1)
                lhs = lambda k, j: core.hT[:, k, j * P:(j + 1) * P]
                for i in range(2):
                    project_strip(core, pe, lhs, NT, first + 6 + i, 1, [4 + 2 * i, 5 + 2 * i])
                pe.wait_ge(pre_copied, 5)
                project_strip(core, pe, lhs, NT, first + 8, 1, [0, 1])

            @block.scalar
            def _(act):
                act.wait_ge(padded, 1)
                for u in range(6):
                    if u >= 2:
                        act.wait_ge(convolved, 4 * (u - 1))
                    ring.wait_read(act, first + u)
                    nc.scalar.activation(pre[:, u % 2, :, TAPS - 1:], ps[:, 2 * (u % 2):2 * (u % 2) + 2, :].rearrange(
                        "p b (q t) -> p (b q) t", t=S), ACT.Copy).then_inc(pre_copied, 1)
                    if u >= 1:
                        act.wait_ge(convolved, 4 * u)
                        nc.scalar.activation(conv[:, 4 * (u - 1):4 * u, :], acc[:, (u - 1) % 2, :, :], ACT.Silu).then_inc(silus, 1)
                act.wait_ge(convolved, 24)
                nc.scalar.activation(conv[:, 20:24, :], acc[:, 1, :, :], ACT.Silu).then_inc(silus, 1)
                ring.wait_read(act, first + 7)
                for i in range(2):
                    nc.scalar.activation(zs[:, :, i * STRIP:(i + 1) * STRIP], ps[:, 4 + 2 * i:6 + 2 * i, :], ACT.Silu)
                ring.wait_read(act, first + 8)
                nc.scalar.activation(ab[:], ps[:, 0:2, 0:16], ACT.Copy)

            @block.vector
            def _(dve):
                nc.vector.memset(pre[:, :, :, 0:TAPS - 1], 0.0).then_inc(padded, 1)
                taps = 0
                for u in range(6):
                    dve.wait_ge(pre_copied, u + 1)
                    if u >= 2:
                        dve.wait_ge(silus, u - 1)
                    for q in range(4):
                        c, b = 4 * u + q, u % 2
                        w = core.convw
                        nc.vector.tensor_scalar(acc[:, b, q, :], pre[:, b, q, 0:S], w[:, 0, c:c + 1], None, ALU.mult).then_inc(tap, 1)
                        for k in range(1, TAPS):
                            taps += 1
                            dve.wait_ge(tap, taps)
                            nc.vector.scalar_tensor_tensor(acc[:, b, q, :], pre[:, b, q, k:k + S], w[:, k, c:c + 1], acc[:, b, q, :],
                                                           ALU.mult, ALU.add).then_inc(tap if k < TAPS - 1 else convolved, 1)


def stage_gdn_gates(core, t, conv, ab, masks, co):
    nc, ps = core.nc, core.ps
    with Stage(core, "gdngate") as st:
        sq, lnr = st.sb("sq", [P, 2, 2 * S]), st.sb("lnr", [P, 2, 2 * S])
        alog, dtb = st.sb("alog", [P, GH]), st.sb("dtb", [P, GH])
        y, e, l, nb, ea, g = (st.sb(n, [P, NT, GH]) for n in ("y", "e", "l", "nb", "ea", "g"))
        loaded, masks_in = st.sem("loaded"), st.sem("masks_in")
        squares, sums, logs, rsqrts, scaled = (st.sem(n) for n in ("squares", "sums", "logs", "rsqrts", "scaled"))
        acts, dves, gsums = st.sem("gate_acts"), st.sem("gate_dves"), st.sem("gsums")
        mod = Modulation(core, st, [(1, g, 4, 5) for g in range(3)])
        with st.block() as block:
            @block.sync
            def _(sp):
                sp.dma_start(alog[:], t["gdn_a_log"].broadcast_to([P, GH])).then_inc(loaded, 16)
                sp.dma_start(dtb[:], t["gdn_dt_bias"].broadcast_to([P, GH])).then_inc(loaded, 16)
                sp.dma_start(masks[:], t["const"][:, P:P + masks.shape[1]]).then_inc(masks_in, 16)
                core.ring.load_ahead(sp, core.ring.taken + SLOTS)

            @block.scalar
            def _(act):
                def link(i, ins):
                    ins.then_inc(acts, 1)
                act.wait_ge(loaded, 32)
                act.wait_ge(dves, 2)
                nc.scalar.activation(e[:], l[:], ACT.Exp, scale=-1.0).then_inc(acts, 1)
                nc.scalar.activation(nb[:], ab[:, :, GH:], ACT.Exp, scale=-1.0).then_inc(acts, 1)
                nc.scalar.activation(ea[:, 0, :], alog[:], ACT.Exp).then_inc(acts, 1)
                act.wait_ge(dves, 3)
                nc.scalar.activation(l[:], e[:], ACT.Ln).then_inc(acts, 1)
                for i in range(8):
                    if i in (3, 6):
                        mod.copy(act, i // 3 - 1)
                    pair = conv[:, 2 * i:2 * i + 2, :].rearrange("p c t -> p (c t)")
                    if i >= 2:
                        act.wait_ge(sums, i - 1)
                    nc.scalar.activation(sq[:, i % 2, :], pair, ACT.Square).then_inc(squares, 1)
                    act.wait_ge(sums, i + 1)
                    if i >= 2:
                        act.wait_ge(scaled, i - 1)
                    nc.scalar.activation(lnr[:, i % 2, :], ps[:, i % 2, :], ACT.Ln, bias=co["eps"][:, 0:1]).then_inc(logs, 1)
                    act.wait_ge(logs, i + 1)
                    nc.scalar.activation(lnr[:, i % 2, :], lnr[:, i % 2, :], ACT.Exp, scale=-0.5).then_inc(rsqrts, 1)
                act.wait_ge(gsums, 1)
                act.wait_ge(dves, 9)
                nc.scalar.activation(co["kbg"][:], co["gc"][:], ACT.Exp).then_inc(acts, 1)
                nc.scalar.activation(co["kd"][:], y[:], ACT.Exp)
                nc.scalar.activation(co["tot"][:], ps[:, 3, 64:96].rearrange("p (f j h) -> p f j h", f=2, j=NT), ACT.Exp)
                mod.copy(act, 2)

            @block.vector
            def _(dve):
                nc.vector.memset(co["eps"][:], EPS)
                dve.wait_ge(loaded, 32)
                nc.vector.tensor_tensor(y[:], ab[:, :, 0:GH], dtb[:].unsqueeze(1).broadcast_to([P, NT, GH]), ALU.add).then_inc(dves, 1)
                dve.wait_ge(dves, 1)
                nc.vector.scalar_tensor_tensor(l[:], y[:], -1.0, y[:], ALU.mult, ALU.max).then_inc(dves, 1)
                dve.wait_ge(acts, 3)
                nc.vector.tensor_scalar(e[:], e[:], 1.0, None, ALU.add).then_inc(dves, 1)
                nc.vector.tensor_scalar(nb[:], nb[:], 1.0, None, ALU.add).then_inc(dves, 1)
                dve.wait_ge(dves, 4)
                nc.vector.reciprocal(co["beta"][:], nb[:]).then_inc(dves, 1)
                dve.wait_ge(acts, 4)
                nc.vector.scalar_tensor_tensor(g[:], y[:], 0.0, l[:], ALU.max, ALU.add).then_inc(dves, 1)
                dve.wait_ge(dves, 6)
                nc.vector.scalar_tensor_tensor(g[:], g[:], -1.0, ea[:, 0, :].unsqueeze(1).broadcast_to([P, NT, GH]),
                                               ALU.mult, ALU.mult).then_inc(dves, 1)
                dve.wait_ge(gsums, 1)
                nc.vector.tensor_copy(co["gc"][:], ps[:, 3, 0:16].rearrange("p (j h) -> p j h", j=NT)).then_inc(dves, 1)
                dve.wait_ge(dves, 8)
                nc.vector.scalar_tensor_tensor(y[:], co["gc"][:], -1.0, ps[:, 3, 32:48].rearrange("p (j h) -> p j h", j=NT),
                                               ALU.mult, ALU.add).then_inc(dves, 1)
                for i in range(8):
                    pair = conv[:, 2 * i:2 * i + 2, :].rearrange("p c t -> p (c t)")
                    dve.wait_ge(rsqrts, i + 1)
                    nc.vector.scalar_tensor_tensor(pair, pair, P ** -0.5 if i < 4 else 1.0, lnr[:, i % 2, :],
                                                   ALU.mult, ALU.mult).then_inc(scaled, 1)
                    if i in (4, 7):
                        mod.store(dve, (i - 4) // 3)
                dve.wait_ge(acts, 5)
                nc.vector.tensor_tensor(co["kbg"][:], co["kbg"][:], co["beta"][:], ALU.mult)
                mod.store(dve, 2)

            @block.tensor
            def _(pe):
                pe.wait_ge(masks_in, 16)
                pe.wait_ge(dves, 7)
                gg = g[:].rearrange("p j h -> p (j h)")
                for i, mask in enumerate(("upto", "chunk", "first_half", "second_half")):
                    at = (0, 32, 64, 80)[i]
                    last = nc.tensor.matmul(ps[:, 3, at:at + 16], mask_of(masks, mask), gg, start=True, stop=True)
                last.then_inc(gsums, 1)
                for i in range(8):
                    pe.wait_ge(squares, i + 1)
                    if i >= 2:
                        pe.wait_ge(logs, i - 1)
                    nc.tensor.matmul(ps[:, i % 2, :], core.ones[:], sq[:, i % 2, :], start=True, stop=True).then_inc(sums, 1)
                    for u in ((0, 1), (2,), (3,), (4, 5), (6,), (7,), (8, 9), (10, 11))[i]:
                        mod.multiply(pe, u)
                    if i in (3, 6):
                        mod.turn(pe, i // 3 - 1)
                mod.turn(pe, 2)


MASKS = ["upto", "chunk", "first_half", "second_half"] + [f"level{s}" for s in LEVELS]


def mask_of(masks, name):
    i = MASKS.index(name)
    return masks[:, i * P:(i + 1) * P]


def shape_constants():
    m, t = np.meshgrid(np.arange(P), np.arange(P), indexing="ij")
    same = m // CH == t // CH
    out = [m == t, same & (m <= t), same, m < CH, m >= CH]
    for s in LEVELS:
        out.append((m // (2 * s) == t // (2 * s)) & (t % (2 * s) >= s) & (m % (2 * s) < s))
    out.append(m + t == P - 1)
    return np.concatenate(out, axis=1).astype(np.float32)


def stage_gdn_tile(core, j, conv, masks, co, work, state):
    nc, ps = core.nc, core.ps
    kbg, kd, vb, qdT = work["kbg"], work["kd"], work["vb"], work["qdT"]
    aT, u, wT, vnew = work["aT"], work["u"], work["wT"], work["vnew"]
    tok = slice(j * P, (j + 1) * P)
    NL = len(LEVELS) - 1
    with Stage(core, f"gdntile{j}") as st:
        mod = Modulation(core, st, [(2 + j, 0, 4, 5), (2 + j, 1, 4, 5), (2 + j, 2, 6, 7)])
        both = lambda n: [st.sb(f"{n}{g}", [P, 4, P]) for g in range(2)]
        L, X, Pm, T, TT = both("L"), both("X"), both("Pm"), both("T"), both("TT")
        dg, db, E = Pm, T, TT
        pair = lambda n: [st.sem(f"{n}{g}") for g in range(2)]
        turned, tok_scaled, diags, spread, raws, raws_read = (st.sem(n) for n in ("turned", "tok_scaled", "diags", "spread", "raws", "raws_read"))
        exps, dd, lt, solved = st.sem("exps"), st.sem("decay_steps"), st.sem("lead"), st.sem("solved")
        x_ready, p_made, p_copied, tp_made, t_ready = (pair(n) for n in ("x_ready", "p_made", "p_copied", "tp_made", "t_ready"))
        uw_made, w_copied = st.sem("uw_made"), st.sem("w_copied")
        ws_made, v_ready, o_made, kv_made, o_copied, s_step = (st.sem(n) for n in ("ws_made", "v_ready", "o_made", "kv_made", "o_copied", "s_step"))
        flat = lambda a: a[:].rearrange("p h t -> p (h t)")
        four = lambda b: ps[:, b, :].rearrange("p (h t) -> p h t", h=4)
        over_t = lambda a: a.unsqueeze(2).broadcast_to([P, 4, P])
        over_h = lambda a: a.unsqueeze(1).broadcast_to([P, 4, P])
        K_BANK, V_BANK = (0, 6), (1, 7)
        P_BANK, TT_BANK, T_BANK = (7, 1), (6, 2), (0, 3)
        with st.block() as block:
            ring_in_stage(core, block, 12)

            @block.tensor
            def _(pe):
                for g in range(2):
                    for i in range(4):
                        h = 4 * g + i
                        nc.tensor.transpose(ps[:, K_BANK[g], i * P:(i + 1) * P], conv[:, 8 + h, tok], core.ident[:])
                        last = nc.tensor.transpose(ps[:, V_BANK[g], i * P:(i + 1) * P], conv[:, 16 + h, tok], core.ident[:])
                    last.then_inc(turned, 1)
                    if g:
                        pe.wait_ge(raws_read, 1)
                    for i in range(4):
                        h = 4 * g + i
                        nc.tensor.matmul(ps[:, 4, i * P:(i + 1) * P], conv[:, 8 + h, tok], conv[:, 8 + h, tok], start=True, stop=True)
                        last = nc.tensor.matmul(ps[:, 5, i * P:(i + 1) * P], conv[:, 8 + h, tok], conv[:, h, tok], start=True, stop=True)
                    last.then_inc(raws, 1)
                    pe.wait_ge(diags, 2 * (g + 1))
                    nc.tensor.matmul(ps[:, 2, :], core.ones[:], flat(dg[g]), start=True, stop=True)
                    nc.tensor.matmul(ps[:, 3, :], core.ones[:], flat(db[g]), start=True, stop=True).then_inc(spread, 1)
                pe.wait_ge(raws_read, 2)
                for g in range(2):
                    pe.wait_ge(t_ready[g], 1)
                    for i in range(4):
                        last = nc.tensor.transpose(ps[:, TT_BANK[g], i * P:(i + 1) * P], TT[g][:, i, :], core.ident[:])
                    last.then_inc(tp_made[g], 1)
                for n in range(NL):
                    for g in range(2):
                        pe.wait_ge(x_ready[g], n + 1)
                        pe.wait_ge(t_ready[g], 2 * (n + 1))
                        for i in range(4):
                            last = nc.tensor.matmul(ps[:, P_BANK[g], i * P:(i + 1) * P], X[g][:, i, :], T[g][:, i, :], start=True, stop=True)
                        last.then_inc(p_made[g], 1)
                    if n < 4:
                        mod.multiply(pe, 2 * n)
                    for g in range(2):
                        pe.wait_ge(p_copied[g], n + 1)
                        for i in range(4):
                            last = nc.tensor.matmul(ps[:, TT_BANK[g], i * P:(i + 1) * P], Pm[g][:, i, :], TT[g][:, i, :], start=True, stop=True)
                            if n < NL - 1:
                                last = nc.tensor.matmul(ps[:, T_BANK[g], i * P:(i + 1) * P], TT[g][:, i, :], Pm[g][:, i, :], start=True, stop=True)
                        last.then_inc(tp_made[g], 1)
                    if n < 4:
                        mod.multiply(pe, 2 * n + 1)
                    if n in (2, 4):
                        mod.turn(pe, n // 2 - 1)
                for g in range(2):
                    pe.wait_ge(t_ready[g], 2 * NL + 1)
                    for i in range(4):
                        h = 4 * g + i
                        nc.tensor.matmul(ps[:, P_BANK[g], i * P:(i + 1) * P], TT[g][:, i, :], vb[:, h, :], start=True, stop=True)
                        last = nc.tensor.matmul(ps[:, TT_BANK[g], i * P:(i + 1) * P], kbg[:, h, :], TT[g][:, i, :], start=True, stop=True)
                    last.then_inc(uw_made, 1)
                pe.wait_ge(w_copied, 2)
                pe.wait_ge(solved, 2)
                for half in range(2):
                    r = slice(half * CH, (half + 1) * CH)
                    if half:
                        pe.wait_ge(s_step, 2)
                    for h in range(GH):
                        last = nc.tensor.matmul(ps[r, h // 4, (h % 4) * P:(h % 4 + 1) * P], wT[:, h, r], state[:, h, :],
                                                start=True, stop=True)
                    last.then_inc(ws_made, 1)
                    mod.multiply(pe, 8 + 2 * half)
                    pe.wait_ge(v_ready, half + 1)
                    if half:
                        pe.wait_ge(o_copied, 1)
                    else:
                        pe.wait_ge(mod.stored, 2)
                    for h in range(GH):
                        o = ps[r, 2 + h // 4, (h % 4) * P:(h % 4 + 1) * P]
                        nc.tensor.matmul(o, qdT[:, h, r], state[:, h, :], start=True, stop=False)
                        last = nc.tensor.matmul(o, aT[:, h, r], vnew[:, h, :], start=False, stop=True)
                    last.then_inc(o_made, 1)
                    for h in range(GH):
                        last = nc.tensor.matmul(ps[:, 4 + h // 4, (h % 4) * P:(h % 4 + 1) * P], kd[r, h, :], vnew[r, h, :],
                                                start=True, stop=True)
                    last.then_inc(kv_made, 1)
                    mod.multiply(pe, 9 + 2 * half)
                mod.turn(pe, 2)

            @block.vector
            def _(dve):
                steps = 0

                def link(ins):
                    nonlocal steps
                    steps += 1
                    ins.then_inc(dd, 1)
                    dve.wait_ge(dd, steps)

                if j == 0:
                    nc.vector.memset(state[:], 0.0)
                    nc.vector.memset(vnew[:], 0.0)
                for g in range(2):
                    h4 = slice(4 * g, 4 * g + 4)
                    gc, beta = co["gc"][:, j, h4], co["beta"][:, j, h4]
                    nc.vector.tensor_tensor(dg[g][:], over_h(core.ident[:]), over_t(gc), ALU.mult).then_inc(diags, 1)
                    nc.vector.tensor_tensor(db[g][:], over_h(core.ident[:]), over_t(beta), ALU.mult).then_inc(diags, 1)
                for g in range(2):
                    h4 = slice(4 * g, 4 * g + 4)
                    gc, beta = co["gc"][:, j, h4], co["beta"][:, j, h4]
                    dve.wait_ge(turned, g + 1)
                    nc.vector.tensor_tensor(kbg[:, h4, :], four(K_BANK[g]), over_t(co["kbg"][:, j, h4]), ALU.mult)
                    nc.vector.tensor_tensor(kd[:, h4, :], four(K_BANK[g]), over_t(co["kd"][:, j, h4]), ALU.mult)
                    dve.wait_ge(spread, g + 1)
                    link(nc.vector.tensor_tensor(E[g][:], four(2), over_t(gc), ALU.subtract))
                    nc.vector.tensor_scalar(E[g][:], E[g][:], 0.0, None, ALU.min).then_inc(lt, 1)
                    nc.vector.tensor_tensor(vb[:, h4, :], four(V_BANK[g]), over_t(beta), ALU.mult).then_inc(tok_scaled, 1)
                    dve.wait_ge(exps, 2 * g + 1)
                    nc.vector.tensor_tensor(qdT[:, h4, :], conv[:, h4, tok], X[g][:], ALU.mult)
                    dve.wait_ge(exps, 2 * g + 2)
                    link(nc.vector.tensor_tensor(E[g][:], E[g][:], over_h(mask_of(masks, "upto")), ALU.mult))
                    dve.wait_ge(raws, g + 1)
                    nc.vector.tensor_tensor(aT[:, h4, :], four(5), E[g][:], ALU.mult)
                    link(nc.vector.tensor_tensor(L[g][:], E[g][:], four(3), ALU.mult))
                    nc.vector.tensor_tensor(L[g][:], four(4), L[g][:], ALU.mult).then_inc(raws_read, 1)
                    dve.wait_ge(raws_read, g + 1)
                    link(nc.vector.tensor_tensor(X[g][:], L[g][:], over_h(mask_of(masks, "level1")), ALU.mult))
                    nc.vector.tensor_tensor(TT[g][:], over_h(core.ident[:]), X[g][:], ALU.subtract).then_inc(t_ready[g], 1)
                for n in range(NL + 1):
                    for g in range(2):
                        dve.wait_ge(tp_made[g], n + 1)
                        if n == 0:
                            nc.vector.tensor_copy(T[g][:], four(TT_BANK[g])).then_inc(t_ready[g], 1)
                        else:
                            nc.vector.tensor_tensor(TT[g][:], TT[g][:], four(TT_BANK[g]), ALU.subtract).then_inc(t_ready[g], 1)
                            if n < NL:
                                nc.vector.tensor_tensor(T[g][:], T[g][:], four(T_BANK[g]), ALU.subtract).then_inc(t_ready[g], 1)
                        if n < NL:
                            nc.vector.tensor_tensor(X[g][:], L[g][:], over_h(mask_of(masks, f"level{LEVELS[n + 1]}")),
                                                    ALU.mult).then_inc(x_ready[g], 1)
                    if n == 3:
                        mod.store(dve, 0)
                mod.store(dve, 1)
                for g in range(2):
                    dve.wait_ge(uw_made, g + 1)
                    nc.vector.tensor_copy(u[:, 4 * g:4 * g + 4, :], four(P_BANK[g])).then_inc(solved, 1)
                dve.wait_ge(solved, 2)
                for half in range(2):
                    r = slice(half * CH, (half + 1) * CH)
                    dve.wait_ge(ws_made, half + 1)
                    nc.vector.tensor_tensor(vnew[r, :, :], u[r, :, :], ps[r, 0:2, :].rearrange("p b (h d) -> p (b h) d", h=4),
                                            ALU.subtract).then_inc(v_ready, 1)
                    dve.wait_ge(o_made, half + 1)
                    nc.vector.tensor_tensor(state[:], state[:], co["tot"][:, half, j, :].unsqueeze(2).broadcast_to([P, GH, P]),
                                            ALU.mult).then_inc(s_step, 1)
                    dve.wait_ge(kv_made, half + 1)
                    dve.wait_ge(s_step, 2 * half + 1)
                    nc.vector.tensor_tensor(state[:], state[:], ps[:, 4:6, :].rearrange("p b (h d) -> p (b h) d", h=4),
                                            ALU.add).then_inc(s_step, 1)
                mod.store(dve, 2)

            @block.scalar
            def _(act):
                for g in range(2):
                    act.wait_ge(lt, g + 1)
                    nc.scalar.activation(X[g][:], four(2), ACT.Exp).then_inc(exps, 1)
                    nc.scalar.activation(E[g][:], E[g][:], ACT.Exp).then_inc(exps, 1)
                for n in range(NL):
                    if n in (2, 4):
                        mod.copy(act, n // 2 - 1)
                    for g in range(2):
                        act.wait_ge(p_made[g], n + 1)
                        nc.scalar.activation(Pm[g][:], four(P_BANK[g]), ACT.Copy).then_inc(p_copied[g], 1)
                for g in range(2):
                    act.wait_ge(uw_made, g + 1)
                    nc.scalar.activation(wT[:, 4 * g:4 * g + 4, :], four(TT_BANK[g]), ACT.Copy).then_inc(w_copied, 1)
                for half in range(2):
                    r = slice(half * CH, (half + 1) * CH)
                    act.wait_ge(o_made, half + 1)
                    nc.scalar.activation(conv[r, 16:24, tok], ps[r, 2:4, :].rearrange("p b (h d) -> p (b h) d", h=4),
                                         ACT.Copy).then_inc(o_copied, 1)
                mod.copy(act, 2)


def stage_gdn_out(core, t, conv, zs):
    nc, ps = core.nc, core.ps
    with Stage(core, "gdnout") as st:
        gain = st.sb("gain", [P, P])
        sq = st.sb("sq", [P, GH, P])
        ssq, ms, rstd = (st.sb(n, [P, NT * GH]) for n in ("ssq", "ms", "rstd"))
        y = st.sb("y", [P, NT, GH, P])
        loaded, dd, sums, pools, turned, ready = (st.sem(n) for n in ("loaded", "steps", "sums", "pools", "turned", "ready"))
        with st.block() as block:
            @block.sync
            def _(sp):
                sp.dma_start(gain[:], t["gdn_out_norm"].broadcast_to([P, P])).then_inc(loaded, 16)

            @block.vector
            def _(dve):
                steps = 0

                def link(ins):
                    nonlocal steps
                    steps += 1
                    ins.then_inc(dd, 1)
                    dve.wait_ge(dd, steps)

                o = [conv[:, 16:24, j * P:(j + 1) * P] for j in range(NT)]
                for j in range(NT):
                    link(nc.vector.tensor_tensor(sq[:], o[j], o[j], ALU.mult))
                    link(nc.vector.tensor_reduce(ssq[:, j * GH:(j + 1) * GH], sq[:], AX.X, ALU.add))
                nc.vector.memset(ms[:, 0:1], 0.0).then_inc(sums, 1)
                dve.wait_ge(loaded, 16)
                for j in range(NT):
                    z = zs[:, j, :].rearrange("p (h d) -> p h d", h=GH)
                    link(nc.vector.tensor_tensor(z, z, gain[:].unsqueeze(1).broadcast_to([P, GH, P]), ALU.mult))
                dve.wait_ge(pools, 2)
                for j in range(NT):
                    z = zs[:, j, :].rearrange("p (h d) -> p h d", h=GH)
                    link(nc.vector.tensor_tensor(y[:, j, :, :], o[j], rstd[:, j * GH:(j + 1) * GH].unsqueeze(2).broadcast_to([P, GH, P]), ALU.mult))
                    nc.vector.tensor_tensor(y[:, j, :, :], y[:, j, :, :], z, ALU.mult).then_inc(ready, 1)

            @block.gpsimd
            def _(pool):
                pool.wait_ge(sums, 1)
                nc.gpsimd.tensor_scalar(ms[:], ssq[:], 1.0 / P, EPS, ALU.mult, ALU.add).then_inc(pools, 1)
                pool.wait_ge(pools, 1)
                nc.gpsimd.tensor_tensor(rstd[:], ms[:], core.half[:], ALU.pow).then_inc(pools, 1)

            @block.tensor
            def _(pe):
                pe.wait_ge(ready, NT)
                for h in range(GH):
                    for j in range(NT):
                        last = nc.tensor.transpose(ps[:, h, j * P:(j + 1) * P], y[:, j, h, :], core.ident[:])
                    last.then_inc(turned, 1)

            @block.scalar
            def _(act):
                for h in range(GH):
                    act.wait_ge(turned, h + 1)
                    nc.scalar.activation(core.hT[:, h, 0:S], ps[:, h, 0:S], ACT.Copy)


def mixer_gdn(core, t, outer):
    with ExitStack() as stack:
        sb = lambda n, shape: stack.enter_context(core.nc.sbuf_tensor("gdn_" + n, shape, F32))
        zs = core.ctx_x
        conv, ab = sb("conv", [P, 24, S]), sb("ab", [P, NT, 16])
        stage_gdn_project(core, t, conv, zs, ab)
        masks = sb("masks", [P, len(MASKS) * P])
        co = {n: sb(n, [P, NT, GH]) for n in ("beta", "gc", "kbg", "kd")}
        co["eps"], co["tot"] = sb("eps", [P, 1]), sb("tot", [P, 2, NT, GH])
        stage_gdn_gates(core, t, conv, ab, masks, co)
        with ExitStack() as inner:
            wb = lambda n: inner.enter_context(core.nc.sbuf_tensor("gdn_" + n, [P, GH, P], F32))
            work = {n: wb(n) for n in ("aT", "u", "wT", "vnew")}
            state = wb("state")
            free = core.hT[:].rearrange("p c t -> p (c t)")
            for i, n in enumerate(("kbg", "kd", "vb", "qdT")):
                work[n] = free[:, i * GH * P:(i + 1) * GH * P].rearrange("p (h d) -> p h d", h=GH)
            for j in range(NT):
                stage_gdn_tile(core, j, conv, masks, co, work, state)
        stage_gdn_out(core, t, conv, zs)


class Part:

    def __init__(self, c0, heads, step, dim, gain, rope=None):
        self.c0, self.heads, self.step, self.dim, self.gain, self.rope = c0, heads, step, dim, gain, rope

    def of(self, raw, tiles):
        base = self.c0 // self.step * self.step
        v = raw[:, tiles, base:base + self.heads * self.step].rearrange("p t (h d) -> p t h d", h=self.heads)
        return v[:, :, :, self.c0 - base:self.c0 - base + self.dim]


def stage_heads(core, name, lhs, tiles, units, plan, loads=(), before=None):
    nc, ps, ring = core.nc, core.ps, core.ring
    tiles_of = [s.get("tiles", tiles) for s in plan]
    width = max([s["width"] for s in plan if s["parts"]])
    normed = [i for i, s in enumerate(plan) if s["parts"]]
    rank = {s: n for n, s in enumerate(normed)}
    parts = [(s, part) for s in normed for part in plan[s]["parts"]]

    def places(s):
        at, out = 0, []
        for part in plan[s]["parts"]:
            out.append(slice(at, at + tiles_of[s] * part.heads))
            at = out[-1].stop
        return out
    most = max(places(s)[-1].stop for s in normed)
    with Stage(core, name) as st:
        raw = st.sb("raw", [P, 2, tiles, width])
        sq = st.sb("sq", [P, tiles, width])
        ssq, ms, rstd = (st.sb(n, [P, most]) for n in ("ssq", "ms", "rstd"))
        loaded, raw_copied, sums, means, rstds, ready, turned, left, dd = (st.sem(n) for n in (
            "loaded", "raw_copied", "sums", "means", "rstds", "ready", "turned", "left", "steps"))
        half = st.sb("exponent", [P, most])
        filled = st.sem("filled")
        first = ring.take(units)
        assert units == len(plan)
        with st.block() as block:
            @block.sync
            def _(sp):
                for dst, src in loads:
                    sp.dma_start(dst, src).then_inc(loaded, 16)
                ring.load_ahead(sp, ring.taken + SLOTS)

            def bank(s, j):
                return 4 * (s % 2) + j

            @block.tensor
            def _(pe):
                def turn(s):
                    if not plan[s]["parts"]:
                        return
                    n = rank[s]
                    pe.wait_ge(ready, n + 1)
                    for i, (c0, c1, _) in enumerate(plan[s]["turns"]):
                        for j in range(tiles_of[s]):
                            src = (sq if plan[s].get("spread") else raw[:, n % 2])[:, j, c0:c1]
                            last = nc.tensor.transpose(ps[0:c1 - c0, bank(s, j), i * P:(i + 1) * P], src, core.ident[:])
                    last.then_inc(turned, 1)
                for s in range(len(plan)):
                    if s >= 2:
                        pe.wait_ge(left, s - 1)
                    project_strip(core, pe, lhs, tiles_of[s], first + s, 1, [bank(s, j) for j in range(tiles_of[s])])
                    if s >= 1:
                        turn(s - 1)
                turn(len(plan) - 1)

            @block.scalar
            def _(act):
                def finish(s):
                    n = tiles_of[s]
                    banks = ps[:, bank(s, 0):bank(s, 0) + n, :]
                    if plan[s]["parts"]:
                        act.wait_ge(turned, rank[s] + 1)
                        for i, (c0, c1, dest) in enumerate(plan[s]["turns"]):
                            last = nc.scalar.activation(dest.rearrange("p (j t) -> p j t", t=P),
                                                        banks[0:c1 - c0, :, i * P:(i + 1) * P], ACT.Copy)
                    else:
                        ring.wait_read(act, first + s)
                        for c0, c1, dest in plan[s]["values"]:
                            last = nc.scalar.activation(dest, banks[:, :, c0:c1], ACT.Copy)
                    last.then_inc(left, 1)
                for s in range(len(plan)):
                    if plan[s]["parts"]:
                        n, w = rank[s], plan[s]["width"]
                        ring.wait_read(act, first + s)
                        if n >= 2:
                            act.wait_ge(turned, n - 1)
                        for c0, c1, dest in plan[s]["values"]:
                            src = ps[:, bank(s, 0):bank(s, 0) + tiles_of[s], c0:c1]
                            if len(dest.shape) == 4:
                                src = src.rearrange("p j (h d) -> p j h d", h=dest.shape[2] * 2)[:, :, 1::2, :] if plan[s].get("odd") else src
                            nc.scalar.activation(dest, src, ACT.Copy)
                        nc.scalar.activation(raw[:, n % 2, 0:tiles_of[s], 0:w], ps[:, bank(s, 0):bank(s, 0) + tiles_of[s], 0:w],
                                             ACT.Copy).then_inc(raw_copied, 1)
                    if s >= 1:
                        finish(s - 1)
                finish(len(plan) - 1)

            @block.gpsimd
            def _(pool):
                nc.gpsimd.memset(half[:], -0.5).then_inc(filled, 1)
                pool.wait_ge(filled, 1)
                i = 0
                for n, s in enumerate(normed):
                    for part, at in zip(plan[s]["parts"], places(s)):
                        i += 1
                        pool.wait_ge(sums, i)
                        nc.gpsimd.tensor_scalar(ms[:, at], ssq[:, at], 1.0 / part.dim, EPS, ALU.mult, ALU.add).then_inc(means, 1)
                    pool.wait_ge(means, i)
                    m = at.stop
                    nc.gpsimd.tensor_tensor(rstd[:, 0:m], ms[:, 0:m], half[:, 0:m], ALU.pow).then_inc(rstds, 1)

            @block.vector
            def _(dve):
                steps = 0

                def link(ins):
                    nonlocal steps
                    steps += 1
                    ins.then_inc(dd, 1)
                    dve.wait_ge(dd, steps)

                if loads:
                    dve.wait_ge(loaded, 16 * len(loads))
                if before:
                    before(dve, link)
                spread_before = False
                for n, s in enumerate(normed):
                    T = tiles_of[s]
                    dve.wait_ge(raw_copied, n + 1)
                    r = raw[:, n % 2]
                    for i, (part, at) in enumerate(zip(plan[s]["parts"], places(s))):
                        v = part.of(r, slice(0, T))
                        if plan[s].get("odd"):
                            q = r[:, 0:T, :].rearrange("p t (h d) -> p t h d", h=part.heads)[:, :, :, part.dim:]
                        else:
                            assert not spread_before
                            c = part.c0 if part.heads == 1 else sum(p.heads * p.dim for p in plan[s]["parts"][:i])
                            q = sq[:, 0:T, c:c + part.heads * part.dim].rearrange("p t (h d) -> p t h d", h=part.heads)
                        link(nc.vector.tensor_tensor(q, v, v, ALU.mult))
                        nc.vector.tensor_reduce(ssq[:, at].rearrange("p (t h) -> p t h", t=T), q, AX.X, ALU.add).then_inc(sums, 1)
                    dve.wait_ge(rstds, n + 1)
                    for part, at in zip(plan[s]["parts"], places(s)):
                        v = part.of(r, slice(0, T))
                        by_part = rstd[:, at].rearrange("p (t h) -> p t h", t=T)
                        link(nc.vector.tensor_tensor(v, v, by_part.unsqueeze(3).broadcast_to([P, T, part.heads, part.dim]), ALU.mult))
                        link(nc.vector.tensor_tensor(v, v, part.gain.unsqueeze(1).unsqueeze(1).broadcast_to([P, T, part.heads, part.dim]), ALU.mult))
                        if part.rope:
                            for j in range(NT):
                                d4 = part.dim // 4
                                x = part.of(r, slice(j, j + 1))[:, 0].rearrange("p h (b a d) -> p h b a d", b=2, a=2)
                                o = sq[:, j, 0:part.heads * part.dim].rearrange("p (h b a d) -> p h b a d", h=part.heads, b=2, a=2)
                                m = part.heads * part.dim
                                o2 = (sq[:, 2 + j, 0:m] if tiles >= 4 else sq[:, j, m:2 * m]).rearrange(
                                    "p (h b a d) -> p h b a d", h=part.heads, b=2, a=2)
                                cos, sin = (part.rope[k][:, j].unsqueeze(1).broadcast_to([P, part.heads, 2, d4]) for k in range(2))
                                for a in range(2):
                                    nc.vector.tensor_tensor(o[:, :, :, a], x[:, :, :, a], cos, ALU.mult)
                                    link(nc.vector.tensor_tensor(o2[:, :, :, a], x[:, :, :, 1 - a], sin, ALU.mult))
                                nc.vector.tensor_tensor(x[:, :, :, 0], o[:, :, :, 0], o2[:, :, :, 0], ALU.subtract)
                                link(nc.vector.tensor_tensor(x[:, :, :, 1], o[:, :, :, 1], o2[:, :, :, 1], ALU.add))
                    if plan[s].get("spread"):
                        if spread_before:
                            dve.wait_ge(turned, n)
                        spread_before = True
                        plan[s]["spread"](link, r, sq)
                    if plan[s].get("keep"):
                        plan[s]["keep"](link, r)
                    nc.vector.engine_nop().then_inc(ready, 1)


def stage_attend(core, name, items, lam=None, bias_loads=(), flip=None):
    nc, ps = core.nc, core.ps
    N = len(items)
    comps = len(items[0]["comps"])
    width = max(it["keys"] for it in items)
    with Stage(core, name) as st:
        deep = 3 if comps == 1 else 2
        E = st.sb("E", [P, deep, comps, width])
        Wt = st.sb("Wt", [P, 2, width]) if comps == 2 else None
        ET = st.sb("ET", [P, 2, width])
        nm, l, r = (st.sb(n, [P, 4, comps]) for n in ("nm", "l", "r"))
        scored, maxed, exped, weighted, turned, et_copied, summed, out_left, dd = (st.sem(n) for n in (
            "scored", "maxed", "exped", "weighted", "turned", "et_copied", "summed", "out_left", "steps"))
        bias_in = st.sem("bias_in")
        with st.block() as block:
            @block.sync
            def _(sp):
                for dst, src in bias_loads:
                    sp.dma_start(dst, src).then_inc(bias_in, 16)
                core.ring.load_ahead(sp, core.ring.taken + SLOTS)

            def stat(a, i, c):
                return a[:, i % 4, c:c + 1]

            def stats(i, c):
                s = items[i].get("sums")
                return (stat(nm, i, c), stat(l, i, c)) if s is None else s

            @block.tensor
            def _(pe):
                for i in range(N + 3):
                    if i < N:
                        if i >= 2:
                            pe.wait_ge(exped, comps * (i - 1))
                        for c, (q, k) in enumerate(items[i]["comps"]):
                            scores = ps[:, 2 * (i % 2) + c, 0:items[i]["keys"]]
                            if items[i].get("bias") is not None:
                                if i == 0:
                                    pe.wait_ge(bias_in, 16 * len(bias_loads))
                                nc.tensor.matmul(scores, flip, items[i]["bias"], start=True, stop=False)
                            last = nc.tensor.matmul(scores, q, k, start=items[i].get("bias") is None, stop=True)
                        last.then_inc(scored, 1)
                    if 0 <= i - 2 < N:
                        m = i - 2
                        pe.wait_ge(weighted if comps == 2 else exped, m + 1)
                        if m >= 2:
                            pe.wait_ge(et_copied, m - 1)
                        for b in range(items[m]["keys"] // P):
                            src = (Wt[:, m % 2] if comps == 2 else E[:, m % deep, 0])[:, b * P:(b + 1) * P]
                            last = nc.tensor.transpose(ps[:, 4 + m % 2, b * P:(b + 1) * P], src, core.ident[:])
                        last.then_inc(turned, 1)
                    if 0 <= i - 3 < N:
                        m = i - 3
                        pe.wait_ge(et_copied, m + 1)
                        if m >= 2:
                            pe.wait_ge(out_left, m - 1)
                        blocks = items[m]["values"]
                        for b, v in enumerate(blocks):
                            last = nc.tensor.matmul(ps[:, 6 + m % 2, 0:v.shape[1]], ET[:, m % 2, b * P:(b + 1) * P], v,
                                                    start=(b == 0), stop=(b == len(blocks) - 1))
                        last.then_inc(summed, 1)

            @block.scalar
            def _(act):
                for i in range(N + 2):
                    if i < N:
                        w = items[i]["keys"]
                        act.wait_ge(maxed, i + 1)
                        if i >= deep:
                            act.wait_ge(weighted if comps == 2 else turned, i - deep + 1)
                        for c in range(comps):
                            src = ps[:, 2 * (i % 2) + c, 0:w]
                            neg, tot = stats(i, c)
                            nc.scalar.activation(E[:, i % deep, c, 0:w], src, ACT.Exp, bias=neg, accum_out=tot).then_inc(exped, 1)
                    if i >= 2:
                        m = i - 2
                        w = items[m]["keys"]
                        act.wait_ge(turned, m + 1)
                        if m >= 2:
                            act.wait_ge(summed, m - 1)
                        nc.scalar.activation(ET[:, m % 2, 0:w], ps[:, 4 + m % 2, 0:w], ACT.Copy).then_inc(et_copied, 1)

            @block.vector
            def _(dve):
                steps = 0

                def link(ins):
                    nonlocal steps
                    steps += 1
                    ins.then_inc(dd, 1)
                    dve.wait_ge(dd, steps)

                for i in range(N + 3):
                    if i < N:
                        w = items[i]["keys"]
                        dve.wait_ge(scored, i + 1)
                        for c in range(comps):
                            src = ps[:, 2 * (i % 2) + c, 0:w]
                            last = nc.vector.tensor_reduce(stats(i, c)[0], src, AX.X, ALU.max, negate=True)
                        last.then_inc(maxed, 1)
                    if comps == 2 and 0 <= i - 1 < N:
                        m = i - 1
                        w = items[m]["keys"]
                        dve.wait_ge(exped, 2 * (m + 1))
                        link(nc.vector.reciprocal(r[:, m % 4, :], l[:, m % 4, :]))
                        link(nc.vector.tensor_tensor(stat(r, m, 1), stat(r, m, 1), lam, ALU.mult))
                        if m >= 2:
                            dve.wait_ge(turned, m - 1)
                        link(nc.vector.tensor_scalar(Wt[:, m % 2, 0:w], E[:, m % deep, 0, 0:w], stat(r, m, 0), None, ALU.mult))
                        nc.vector.scalar_tensor_tensor(Wt[:, m % 2, 0:w], E[:, m % deep, 1, 0:w], stat(r, m, 1), Wt[:, m % 2, 0:w],
                                                       ALU.mult, ALU.add).then_inc(weighted, 1)
                    if 0 <= i - 3 < N:
                        m = i - 3
                        plain = comps == 2 or items[m].get("sums") is not None
                        if not plain:
                            link(nc.vector.reciprocal(stat(r, m, 0), stat(l, m, 0)))
                        dve.wait_ge(summed, m + 1)
                        src = ps[:, 6 + m % 2, 0:items[m]["out"].shape[1]]
                        if plain:
                            nc.vector.tensor_copy(items[m]["out"], src).then_inc(out_left, 1)
                        else:
                            nc.vector.tensor_scalar(items[m]["out"], src, stat(r, m, 0), None, ALU.mult).then_inc(out_left, 1)


def stage_turn(core, name, o, tiles, chunks):
    nc, ps = core.nc, core.ps
    with Stage(core, name) as st:
        turned = st.sem("turned")
        with st.block() as block:
            @block.tensor
            def _(pe):
                for c in range(chunks):
                    for j in range(tiles):
                        last = nc.tensor.transpose(ps[:, c, j * P:(j + 1) * P], o(j, c), core.ident[:])
                    last.then_inc(turned, 1)

            @block.scalar
            def _(act):
                for c in range(0, chunks, 2):
                    act.wait_ge(turned, c + 1)
                    nc.scalar.activation(core.hT[:, c, 0:tiles * P], ps[:, c, 0:tiles * P], ACT.Copy)

            @block.vector
            def _(dve):
                for c in range(1, chunks, 2):
                    dve.wait_ge(turned, c + 1)
                    nc.vector.tensor_copy(core.hT[:, c, 0:tiles * P], ps[:, c, 0:tiles * P])


GROUPS = ((128, 1), (512, 4), (2048, 16))
DH = 64
NG = len(GROUPS)
REL = 32
MASKED = -1e30


def bucket_of(dist):
    exact = REL // 2
    d = np.float32(max(dist, 1))
    scaled = np.float32(np.log(d / np.float32(exact))) / np.float32(math.log(2048 / exact))
    return dist if dist < exact else min(exact + int(np.float32(scaled) * np.float32(REL - exact)), REL - 1)


def bias_constants():
    out = np.zeros((REL + NG, 2 * S + NG * GH), np.float32)
    for i in range(2 * S):
        d = S - 1 - i
        if d >= 0:
            out[bucket_of(d), i] = 1
        for g, (window, dilation) in enumerate(GROUPS):
            out[REL + g, i] = not (0 <= d <= window and d % dilation == 0)
    for g in range(NG):
        out[REL + g, 2 * S + g * GH:2 * S + (g + 1) * GH] = MASKED
    return out


def stage_bias(core, t):
    nc, ps = core.nc, core.ps
    with Stage(core, "bias") as st:
        marks = st.sb("marks", [REL + NG, 2 * S])
        table = st.sb("table", [REL + NG, NG * GH])
        rows = st.sb("rows", [NG * GH, 2 * S])
        loaded, made, copied, kept = (st.sem(n) for n in ("loaded", "made", "copied", "kept"))
        with st.block() as block:
            @block.sync
            def _(sp):
                sp.dma_start(marks[:], t["marks"][:, 0:2 * S]).then_inc(loaded, 16)
                sp.dma_start(table[0:REL, :], t["rel_bias"]).then_inc(loaded, 16)
                sp.dma_start(table[REL:, :], t["marks"][REL:, 2 * S:]).then_inc(loaded, 16)
                sp.wait_ge(copied, 1)
                sp.dma_start(t["bias_rows"], rows[:]).then_inc(kept, 16)
                sp.wait_ge(kept, 16)

            @block.tensor
            def _(pe):
                pe.wait_ge(loaded, 48)
                nc.tensor.matmul(ps[0:NG * GH, 0, :], table[:], marks[:], start=True, stop=True).then_inc(made, 1)

            @block.scalar
            def _(act):
                act.wait_ge(made, 1)
                nc.scalar.activation(rows[:], ps[0:NG * GH, 0, :], ACT.Copy).then_inc(copied, 1)


def bias_view(t, j):
    rows = t["bias_rows"]
    return bass.AP(tensor=rows.tensor, offset=S - (j + 1) * P, ap=[[1, P], [2 * S, NG * GH], [1, (j + 1) * P]])


def stage_merge(core, j, o, nm, l, out):
    nc = core.nc
    with Stage(core, f"merge{j}") as st:
        lse, w = st.sb("lse", [P, NG, GH]), st.sb("w", [P, NG, GH])
        top, tot = st.sb("top", [P, GH]), st.sb("tot", [P, GH])
        acts, dd = st.sem("acts"), st.sem("steps")
        over_g = lambda a: a[:].unsqueeze(1).broadcast_to([P, NG, GH])
        with st.block() as block:
            @block.scalar
            def _(act):
                nc.scalar.activation(lse[:], l, ACT.Ln).then_inc(acts, 1)
                act.wait_ge(dd, 3)
                nc.scalar.activation(w[:], lse[:], ACT.Exp).then_inc(acts, 1)

            @block.vector
            def _(dve):
                steps = 0

                def link(ins):
                    nonlocal steps
                    steps += 1
                    ins.then_inc(dd, 1)
                    dve.wait_ge(dd, steps)

                dve.wait_ge(acts, 1)
                link(nc.vector.tensor_tensor(lse[:], lse[:], nm, ALU.subtract))
                link(nc.vector.tensor_reduce(top[:], lse[:].rearrange("p g h -> p h g"), AX.X, ALU.max))
                link(nc.vector.tensor_tensor(lse[:], lse[:], over_g(top), ALU.subtract))
                dve.wait_ge(acts, 2)
                link(nc.vector.tensor_reduce(tot[:], w[:].rearrange("p g h -> p h g"), AX.X, ALU.add))
                link(nc.vector.tensor_tensor(lse[:], l, over_g(tot), ALU.mult))
                link(nc.vector.reciprocal(lse[:], lse[:]))
                link(nc.vector.tensor_tensor(w[:], w[:], lse[:], ALU.mult))
                for g in range(NG):
                    link(nc.vector.tensor_tensor(o[:, g], o[:, g], w[:, g, :].unsqueeze(2).broadcast_to([P, GH, DH]), ALU.mult))
                link(nc.vector.tensor_tensor(o[:, 0], o[:, 0], o[:, 1], ALU.add))
                link(nc.vector.tensor_tensor(out, o[:, 0], o[:, 2], ALU.add))


def mixer_dsw(core, t):
    nc = core.nc
    with ExitStack() as stack:
        sb = lambda n, shape: stack.enter_context(nc.sbuf_tensor("dsw_" + n, shape, F32))
        stage_bias(core, t)
        qT, kT = sb("qT", [P, NG * GH // 2, S]), sb("kT", [P, NG * GH // 2, S])
        v = sb("v", [P, NT, NG, GH * DH])
        gains, flip = sb("gains", [P, 2, DH]), sb("flip", [P, P])
        loads = [(flip[:], t["const"][:, (1 + len(MASKS)) * P:(2 + len(MASKS)) * P]), (gains[:, 0, :], t["dsw_q_norm"].broadcast_to([P, DH])), (gains[:, 1, :], t["dsw_k_norm"].broadcast_to([P, DH]))]

        def scale_q(dve, link):
            link(nc.vector.tensor_scalar(gains[:, 0, :], gains[:, 0, :], DH ** -0.5, None, ALU.mult))

        plan = []
        for which in range(2):
            for g in range(NG):
                dest = (qT, kT)[which]
                plan.append(dict(width=STRIP, values=[], parts=[Part(0, GH, DH, DH, gains[:, which, :])],
                                 turns=[(i * P, (i + 1) * P, dest[:, 4 * g + i, :]) for i in range(4)]))
        for g in range(NG):
            plan.append(dict(width=STRIP, parts=[], values=[(0, STRIP, v[:, :, g, :])], turns=[]))
        stage_heads(core, "dswproj", lambda k, j: core.hT[:, k, j * P:(j + 1) * P], NT, 9, plan, loads, scale_q)
        merged = core.ctx_x[:, :, 0:GH * DH]
        nm, l = sb("nm", [P, NG, GH]), sb("l", [P, NG, GH])
        for j in range(NT):
            with nc.sbuf_tensor(f"dsw_bias{j}", [P, NG * GH, (j + 1) * P], F32) as bias, \
                 nc.sbuf_tensor(f"dsw_o{j}", [P, NG, GH, DH], F32) as o:
                items = []
                for n in range(NG * GH):
                    g, h, r = n // GH, n % GH, slice(DH * (n % 2), DH * (n % 2 + 1))
                    items.append(dict(
                        comps=[(qT[r, n // 2, j * P:(j + 1) * P], kT[r, n // 2, 0:(j + 1) * P])], keys=(j + 1) * P,
                        values=[v[:, b, g, h * DH:(h + 1) * DH] for b in range(j + 1)], bias=bias[:, n, :],
                        out=o[:, g, h, :], sums=(nm[:, g, h:h + 1], l[:, g, h:h + 1])))
                stage_attend(core, f"dswatt{j}", items, bias_loads=[(bias[:], bias_view(t, j))], flip=flip[:])
                stage_merge(core, j, o, nm[:], l[:], merged[:, j, :].rearrange("p (h d) -> p h d", h=GH))
        stage_turn(core, "dswturn", lambda j, c: merged[:, j, c * P:(c + 1) * P], NT, GH * DH // P)


def rope_constants(dim):
    token = np.arange(S)
    half = dim // 2
    freqs = (np.float32(10000.0) ** (-np.arange(0, half, 2, dtype=np.float32) / np.float32(half))).astype(np.float32)
    place = np.stack([token // 64, token % 64], axis=1).astype(np.float32)
    ang = (place[:, :, None] * freqs).astype(np.float32)
    both = np.stack([np.cos(ang), np.sin(ang)]).astype(np.float32).reshape(2, NT, P, -1)
    return np.ascontiguousarray(both.transpose(2, 0, 1, 3)).reshape(P, -1)


def rope_view(tile, dim):
    v = tile.rearrange("p (k j b d) -> p k j b d", k=2, j=NT, b=2)
    return [v[:, k] for k in range(2)]


def stage_lambda(core, t, lam, init):
    nc = core.nc
    with Stage(core, "lambda") as st:
        vec, prod, tot = st.sb("vec", [P, 4, DH]), st.sb("prod", [P, 2, DH]), st.sb("tot", [P, 2])
        loaded, dd, acts = st.sem("loaded"), st.sem("steps"), st.sem("acts")
        with st.block() as block:
            @block.sync
            def _(sp):
                sp.dma_start(vec[:].rearrange("p a d -> p (a d)"),
                             t["diff_lambda_2"].rearrange("n a d -> n (a d)").broadcast_to([P, 4 * DH])).then_inc(loaded, 16)

            @block.scalar
            def _(act):
                act.wait_ge(dd, 2)
                nc.scalar.activation(tot[:], tot[:], ACT.Exp).then_inc(acts, 1)

            @block.vector
            def _(dve):
                steps = 0

                def link(ins):
                    nonlocal steps
                    steps += 1
                    ins.then_inc(dd, 1)
                    dve.wait_ge(dd, steps)

                dve.wait_ge(loaded, 16)
                link(nc.vector.tensor_tensor(prod[:], vec[:, 0::2, :], vec[:, 1::2, :], ALU.mult))
                link(nc.vector.tensor_reduce(tot[:], prod[:], AX.X, ALU.add))
                dve.wait_ge(acts, 1)
                link(nc.vector.tensor_tensor(lam[:], tot[:, 1:2], tot[:, 0:1], ALU.subtract))
                link(nc.vector.tensor_scalar(lam[:], lam[:], -init, None, ALU.add))


def stage_subln(core, o, gain_src, factor, tiles):
    nc = core.nc
    heads = 4
    with Stage(core, "subln") as st:
        gain, sq = st.sb("gain", [P, P]), st.sb("sq", [P, tiles, heads, P])
        ssq, ms, rstd = (st.sb(n, [P, tiles * heads]) for n in ("ssq", "ms", "rstd"))
        loaded, dd, sums, pools = (st.sem(n) for n in ("loaded", "steps", "sums", "pools"))
        with st.block() as block:
            @block.sync
            def _(sp):
                sp.dma_start(gain[:], gain_src.broadcast_to([P, P])).then_inc(loaded, 16)

            @block.vector
            def _(dve):
                steps = 0

                def link(ins):
                    nonlocal steps
                    steps += 1
                    ins.then_inc(dd, 1)
                    dve.wait_ge(dd, steps)

                by_head = lambda a: a[:].rearrange("p (t h) -> p t h", t=tiles)
                link(nc.vector.tensor_tensor(sq[:], o, o, ALU.mult))
                nc.vector.tensor_reduce(by_head(ssq), sq[:], AX.X, ALU.add).then_inc(sums, 1)
                dve.wait_ge(loaded, 16)
                link(nc.vector.tensor_scalar(gain[:], gain[:], factor, None, ALU.mult))
                dve.wait_ge(pools, 2)
                link(nc.vector.tensor_tensor(o, o, by_head(rstd).unsqueeze(3).broadcast_to([P, tiles, heads, P]), ALU.mult))
                link(nc.vector.tensor_tensor(o, o, gain[:].unsqueeze(1).unsqueeze(1).broadcast_to([P, tiles, heads, P]), ALU.mult))

            @block.gpsimd
            def _(pool):
                pool.wait_ge(sums, 1)
                nc.gpsimd.tensor_scalar(ms[:], ssq[:], 1.0 / P, EPS, ALU.mult, ALU.add).then_inc(pools, 1)
                pool.wait_ge(pools, 1)
                nc.gpsimd.tensor_tensor(rstd[:], ms[:], core.half[:, 0:tiles * heads], ALU.pow).then_inc(pools, 1)


T2 = 2 * NT
LAM_INIT = 0.8 - 0.6 * math.exp(-0.3 * 0)


def mixer_even(core, t):
    nc = core.nc
    with ExitStack() as stack:
        sb = lambda n, shape: stack.enter_context(nc.sbuf_tensor("even_" + n, shape, F32))
        qa, ka, qb = (sb(n, [P, 4, T2 * P]) for n in ("qaT", "kaT", "qbT"))
        kb = sb("kbT", [P, 2, T2 * P])
        va, vb = sb("va", [P, T2, STRIP]), sb("vb", [P, T2, 2 * DH])
        gains, rope, lam = sb("gains", [P, 4, DH]), sb("rope", [P, 4 * DH // 2]), sb("lam", [P, 1])
        loads = [(gains[:, 0:2, :].rearrange("p a d -> p (a d)"), t["a_qk_norm_2"].rearrange("n a d -> n (a d)").broadcast_to([P, 2 * DH])),
                 (gains[:, 2:4, :].rearrange("p a d -> p (a d)"), t["b_qk_norm_2"].rearrange("n a d -> n (a d)").broadcast_to([P, 2 * DH])),
                 (rope[:], t["rope_even"])]
        turn = rope_view(rope[:], DH)

        def scale_q(dve, link):
            for i in (0, 2):
                link(nc.vector.tensor_scalar(gains[:, i, :], gains[:, i, :], DH ** -0.5, None, ALU.mult))

        def twice(link, r, other):
            for kv in range(2):
                for to in range(2):
                    link(nc.vector.tensor_copy(other[:, 0:T2, (2 * kv + to) * DH:(2 * kv + to + 1) * DH],
                                               r[:, 0:T2, kv * DH:(kv + 1) * DH]))

        def full(gain, dest):
            return dict(width=STRIP, values=[], parts=[Part(0, 8, DH, DH, gains[:, gain, :], turn)],
                        turns=[(i * P, (i + 1) * P, dest[:, i, :]) for i in range(4)])
        plan = [full(0, qa), full(1, ka), dict(width=STRIP, parts=[], values=[(0, STRIP, va[:])], turns=[]), full(2, qb),
                dict(width=2 * P, values=[(P, 2 * P, vb[:])], parts=[Part(0, 2, DH, DH, gains[:, 3, :], turn)], spread=twice,
                     turns=[(0, P, kb[:, 0, :]), (P, 2 * P, kb[:, 1, :])])]
        stage_heads(core, "evenproj", lambda k, j: core.hT[:, k, j * P:(j + 1) * P], T2, 5, plan, loads, scale_q)
        stage_lambda(core, t, lam, LAM_INIT)
        with nc.sbuf_tensor("even_o", [P, T2, D], F32) as o:
            a_items, b_items = [], []
            for j in range(T2):
                blocks = range(0, T2) if j < NT else range(NT, T2)
                keys = slice(blocks[0] * P, T2 * P)
                tok = slice(j * P, (j + 1) * P)
                for h in range(4):
                    a_items.append(dict(comps=[(qa[c * DH:(c + 1) * DH, h, tok], ka[c * DH:(c + 1) * DH, h, keys]) for c in range(2)],
                                        keys=len(blocks) * P, values=[va[:, b, h * P:(h + 1) * P] for b in blocks],
                                        out=o[:, j, h * P:(h + 1) * P]))
                for h in range(8):
                    r = slice(h % 2 * DH, (h % 2 + 1) * DH)
                    b_items.append(dict(comps=[(qb[r, h // 2, tok], kb[r, h // 4, keys])], keys=len(blocks) * P,
                                        values=[vb[:, b, h // 4 * DH:(h // 4 + 1) * DH] for b in blocks],
                                        out=o[:, j, STRIP + h * DH:STRIP + (h + 1) * DH]))
            stage_attend(core, "diffatt", a_items, lam=lam[:])
            stage_attend(core, "gqatt", b_items)
            stage_subln(core, o[:, :, 0:STRIP].rearrange("p t (h d) -> p t h d", h=4), t["a_subln_2"], 1.0 - LAM_INIT, T2)
            stage_turn(core, "eventurn", lambda j, c: o[:, j, c * P:(c + 1) * P], T2, KC)


MLA_HEADS, NOPE, ROPE = 16, 64, 32
QK = NOPE + ROPE


def mixer_odd(core, t):
    nc = core.nc
    with ExitStack() as stack:
        sb = lambda n, shape: stack.enter_context(nc.sbuf_tensor("odd_" + n, shape, F32))
        kr, small, rope = sb("kr", [P, T2, ROPE]), sb("small", [P, 2 * QK]), sb("rope", [P, 4 * ROPE // 2])
        turn = rope_view(rope[:], ROPE)
        qT = core.hT[:].rearrange("p c t -> p (c t)").rearrange("p (h t) -> p h t", h=MLA_HEADS)
        o = core.ctx_x
        cT = core.ctx_x[:].rearrange("p j d -> p (j d)")[:, 0:3 * T2 * P].rearrange("p (c t) -> p c t", c=3)
        with nc.sbuf_tensor("odd_gains", [P, 3 * P], F32) as gains:
            def keep(link, r):
                link(nc.vector.tensor_copy(kr[:], r[:, :, 3 * P:3 * P + ROPE]))
            loads = [(gains[:, 0:2 * P], t["mla_q_norm_2"].broadcast_to([P, 2 * P])),
                     (gains[:, 2 * P:], t["mla_kv_norm_2"].broadcast_to([P, P])),
                     (small[:], t["mla_qk_norm_2"].rearrange("n a d -> n (a d)").broadcast_to([P, 2 * QK])), (rope[:], t["rope_odd"])]
            plan = [dict(width=3 * P + ROPE, values=[], keep=keep,
                         parts=[Part(0, 1, 2 * P, 2 * P, gains[:, 0:2 * P]), Part(2 * P, 1, P, P, gains[:, 2 * P:]),
                                Part(3 * P, 1, ROPE, ROPE, small[:, QK + NOPE:], turn)],
                         turns=[(i * P, (i + 1) * P, cT[:, i, :]) for i in range(3)])]
            stage_heads(core, "oddproj", lambda k, j: core.hT[:, k, j * P:(j + 1) * P], T2, 1, plan, loads)

        def scale_q(dve, link):
            link(nc.vector.tensor_scalar(small[:, 0:QK], small[:, 0:QK], QK ** -0.5, None, ALU.mult))
        plan = [dict(width=4 * QK, values=[], parts=[Part(0, 4, QK, NOPE, small[:, 0:NOPE]), Part(NOPE, 4, QK, ROPE, small[:, NOPE:QK], turn)],
                     turns=[(i * QK, (i + 1) * QK, qT[0:QK, 4 * n + i, :]) for i in range(4)]) for n in range(4)]
        stage_heads(core, "oddq", lambda k, j: cT[:, k, j * P:(j + 1) * P], NT, 4, plan, before=scale_q)

        kT, v = sb("kT", [P, MLA_HEADS, T2 * P]), sb("v", [P, T2, MLA_HEADS, NOPE])

        def join(link, r, other):
            to = other[:, 0:T2, 0:4 * QK].rearrange("p t (h d) -> p t h d", h=4)
            link(nc.vector.tensor_copy(to[:, :, :, 0:NOPE], r[:, 0:T2, :].rearrange("p t (h d) -> p t h d", h=4)[:, :, :, 0:NOPE]))
            link(nc.vector.tensor_copy(to[:, :, :, NOPE:], kr[:].unsqueeze(2).broadcast_to([P, T2, 4, ROPE])))
        plan = [dict(width=STRIP, odd=True, values=[(0, STRIP, v[:, :, 4 * n:4 * n + 4, :])], spread=join,
                     parts=[Part(0, 4, P, NOPE, small[:, QK:QK + NOPE])],
                     turns=[(i * QK, (i + 1) * QK, kT[0:QK, 4 * n + i, :]) for i in range(4)]) for n in range(4)]
        stage_heads(core, "oddkv", lambda k, j: cT[:, 2, j * P:(j + 1) * P], T2, 4, plan)
        items = [dict(comps=[(qT[0:QK, h, j * P:(j + 1) * P], kT[0:QK, h, :])], keys=T2 * P,
                      values=[v[:, b, h, :] for b in range(T2)], out=o[:, j, h * NOPE:(h + 1) * NOPE])
                 for j in range(NT) for h in range(MLA_HEADS)]
        stage_attend(core, "mlatt", items)
        stage_turn(core, "oddturn", lambda j, c: o[:, j, c * P:(c + 1) * P], NT, KC)


def route_constants():
    p, s = np.arange(P)[:, None], np.arange(S)[None, :]
    least = -float(np.finfo(np.float32).tiny)
    bounds = [np.where(s < p + P * j, least, 0.0) for j in range(NT)]
    return np.concatenate(bounds + [np.broadcast_to(np.arange(CAP), (P, CAP))], axis=1).astype(np.float32)


def stage_route(core, t, name, streams, aff, rows, sel, picked):
    nc, ps, ring = core.nc, core.ps, core.ring
    T = NT * streams
    with Stage(core, name) as st:
        consts = st.sb("consts", [P, 2 * S + CAP])
        nm, l = st.sb("nm", [P, T]), st.sb("l", [P, T])
        higher = st.sb("higher", [P, T, EXPERTS])
        affT = st.sb("affT", [EXPERTS, T * P])
        junk = st.sb("junk", [P, 4, S])
        loaded, dd, exps, affs, turned, copied, stored, spread = (st.sem(n) for n in (
            "loaded", "steps", "exps", "affs", "turned", "copied", "stored", "spread"))
        counted = st.sem("counted")
        first = ring.take(1)
        with st.block() as block:
            @block.sync
            def _(sp):
                sp.dma_start(consts[:], t["route"]).then_inc(loaded, 16)
                ring.load_ahead(sp, ring.taken + SLOTS)

            @block.tensor
            def _(pe):
                project_strip(core, pe, lambda k, j: core.hT[:, k, j * P:(j + 1) * P], T, first, 1, list(range(T)))
                pe.wait_ge(affs, T)
                for j in range(T):
                    last = nc.tensor.transpose(ps[0:EXPERTS, 4, j * P:(j + 1) * P], aff[:, j, :], core.ident[:])
                last.then_inc(turned, 1)

            @block.scalar
            def _(act):
                act.wait_ge(dd, T)
                for j in range(T):
                    nc.scalar.activation(aff[:, j, :], ps[:, j, 0:EXPERTS], ACT.Exp, bias=nm[:, j:j + 1],
                                         accum_out=l[:, j:j + 1]).then_inc(exps, 1)
                act.wait_ge(turned, 1)
                nc.scalar.activation(affT[:], ps[0:EXPERTS, 4, 0:T * P], ACT.Copy).then_inc(copied, 1)
                act.wait_ge(copied, 1)
                act.dma_start(t["affinity"][:, 0:T * P], affT[:]).then_inc(stored, 16)
                act.wait_ge(stored, 16)
                act.dma_start(rows, t["affinity"][:, 0:T * P].unsqueeze(0).broadcast_to([P, EXPERTS, T * P])).then_inc(spread, 16)

            @block.vector
            def _(dve):
                steps = 0

                def link(ins):
                    nonlocal steps
                    steps += 1
                    ins.then_inc(dd, 1)
                    dve.wait_ge(dd, steps)

                ring.wait_read(dve, first)
                for j in range(T):
                    link(nc.vector.tensor_reduce(nm[:, j:j + 1], ps[:, j, 0:EXPERTS], AX.X, ALU.max, negate=True))
                dve.wait_ge(exps, T)
                link(nc.vector.reciprocal(l[:], l[:]))
                for j in range(T):
                    nc.vector.tensor_scalar(aff[:, j, :], aff[:, j, :], l[:, j:j + 1], None, ALU.mult).then_inc(affs, 1)
                dve.wait_ge(affs, T)
                dve.wait_ge(loaded, 16)
                dve.wait_ge(spread, 16)
                for j in range(T):
                    for e in range(EXPERTS):
                        row = rows[:, e, j // NT * S:(j // NT + 1) * S]
                        own = aff[:, j, e:e + 1]
                        n = j * EXPERTS + e
                        if n >= 4:
                            dve.wait_ge(counted, n - 3)
                        nc.vector.scalar_tensor_tensor(junk[:, n % 4, :], row, own, consts[:, j % NT * S:(j % NT + 1) * S],
                                                       ALU.subtract, ALU.is_gt, accum_out=higher[:, j, e:e + 1]).then_inc(counted, 1)
                dve.wait_ge(counted, T * EXPERTS)
                for j in range(T):
                    s = sel[:, j, :].rearrange("p (e r) -> p e r", e=EXPERTS)
                    ranks = consts[:, 2 * S:].unsqueeze(1).broadcast_to([P, EXPERTS, CAP])
                    wide = lambda a: a[:, j, :].unsqueeze(2).broadcast_to([P, EXPERTS, CAP])
                    link(nc.vector.tensor_tensor(s, ranks, wide(higher), ALU.is_equal))
                    nc.vector.tensor_tensor(picked[:, j, :].rearrange("p (e r) -> p e r", e=EXPERTS), s, wide(aff), ALU.mult)


def stage_gather(core, name, s, xn, sel, picked, xsT, pickedT, streams):
    nc, ps = core.nc, core.ps
    with Stage(core, name) as st:
        scale = st.sb("scale", [P, 2, KC])
        scales, gathered, act_left, dve_left, turned, turned_left = (st.sem(n) for n in (
            "scales", "gathered", "act_left", "dve_left", "turned", "turned_left"))
        with st.block() as block:
            def dest(c, i):
                return xsT[:, c, :, CAP * i:CAP * (i + 1)]

            def src(c):
                return ps[:, c, :].rearrange("p (e r) -> p e r", e=EXPERTS)

            @block.tensor
            def _(pe):
                for i in range(streams):
                    for c in range(KC):
                        if i:
                            pe.wait_ge((act_left, dve_left)[c % 2], KC // 2 * (i - 1) + c // 2 + 1)
                        for j in range(NT):
                            last = nc.tensor.matmul(ps[:, c, :], xn[:, NT * i + j, c * P:(c + 1) * P], sel[:, NT * i + j, :],
                                                    start=(j == 0), stop=(j == NT - 1))
                        last.then_inc(gathered, 1)
                for q in range(4):
                    pe.wait_ge((act_left, dve_left)[q % 2], KC // 2 * (streams - 1) + q // 2 + 1)
                    for j in range(NT * streams):
                        last = nc.tensor.transpose(ps[:, q, j * P:(j + 1) * P], picked[:, j, q * P:(q + 1) * P], core.ident[:])
                    last.then_inc(turned, 1)

            @block.scalar
            def _(act):
                act.wait_ge(scales, 2 * streams)
                for i in range(streams):
                    for c in range(0, KC, 2):
                        act.wait_ge(gathered, KC * i + c + 1)
                        nc.scalar.activation(dest(c, i), src(c), ACT.Identity, bias=core.mod(s, 3, i)[:, c:c + 1],
                                             scale=scale[:, i, c:c + 1]).then_inc(act_left, 1)
                for q in range(4):
                    act.wait_ge(turned, q + 1)
                    nc.scalar.activation(pickedT[:, q, 0:NT * streams * P], ps[:, q, 0:NT * streams * P], ACT.Copy)

            @block.vector
            def _(dve):
                for i in range(streams):
                    nc.vector.tensor_scalar(scale[:, i, :], core.mod(s, 4, i), 1.0, None, ALU.add).then_inc(scales, 1)
                    dve.wait_ge(scales, 2 * i + 1)
                    nc.vector.tensor_tensor(scale[:, i, :], scale[:, i, :], core.gain(1, s), ALU.mult).then_inc(scales, 1)
                dve.wait_ge(scales, 2 * streams)
                for i in range(streams):
                    for c in range(1, KC, 2):
                        dve.wait_ge(gathered, KC * i + c + 1)
                        nc.vector.tensor_scalar(dest(c, i), src(c), scale[:, i, c:c + 1], core.mod(s, 3, i)[:, c:c + 1],
                                                ALU.mult, ALU.add).then_inc(dve_left, 1)


HALF_K = KC // 2


def expert_unit(t, layer, e, u):
    w = t[("w_exp_gate_2", "w_exp_up_2", "w_exp_down_2")[u // 2]]
    return w[layer, e, u % 2 * HALF_K * P:(u % 2 + 1) * HALF_K * P, :].rearrange("(k p) n -> p k n", p=P)


def expert_units(t, layer):
    return [(expert_unit(t, layer, e, u), HALF_K, D) for e in range(EXPERTS) for u in range(6)]


def stage_experts(core, t, name, layer, streams, xsT, ys):
    nc, ps, ring = core.nc, core.ps, core.ring
    M = CAP * streams
    G = P // M
    W = D // G
    WC = W // P
    spare = core.hT[:].rearrange("p c t -> p (c t)")[:, 4 * STRIP:]
    xs = spare[:, 0:2 * KC * M].rearrange("p (b c m) -> p b c m", b=2, c=KC)
    a = spare[:, 1024:1536]
    actT = spare[:, 1536:1536 + WC * P].rearrange("p (w m) -> p w m", w=WC)
    with Stage(core, name) as st:
        sg = st.sb("sg", [P, W])
        xs_ready, silus, a_ready, turned, act_ready, y_act, y_dve = (st.sem(n) for n in (
            "xs_ready", "silus", "a_ready", "turned", "act_ready", "y_act", "y_dve"))
        first = ring.take(6 * EXPERTS)
        slot = [(first + u) % SLOTS for u in range(6)]
        lap = [(first + u) // SLOTS for u in range(6)]

        with st.block() as block:
            @block.sync
            def _(sp):
                def load(e, u):
                    sp.wait_ge(ring.read[slot[u]], e + lap[u])
                    sp.dma_start(ring.tile[:, slot[u], :].rearrange("p (k n) -> p k n", k=HALF_K),
                                 expert_unit(t, layer, e, u)).then_inc(ring.full[slot[u]], 16)
                ring.load_ahead(sp, first + 6)
                with sp.Fori(0, 3) as i:
                    for v in range(4):
                        for u in range(6):
                            load(i * 4 + (v + 1), u)
                for e in range(13, EXPERTS):
                    for u in range(6):
                        load(e, u)
                ring.loaded = first + 6 * EXPERTS
                ring.load_ahead(sp, ring.taken + SLOTS)

            @block.tensor
            def _(pe):
                def unit(i, v, u):
                    pe.wait_ge(ring.full[slot[u]], i * 64 + 16 * (lap[u] + v + 1))
                    return ring.tile[:, slot[u], :].rearrange("p (k n) -> p k n", k=HALF_K)

                def product(i, v, m, bank, lhs):
                    for u in range(2 * m, 2 * m + 2):
                        w = unit(i, v, u)
                        for k in range(HALF_K):
                            f = u % 2 * HALF_K + k
                            for g in range(G):
                                last = nc.tensor.matmul(ps[g * M:(g + 1) * M, bank, 0:W], lhs(f), w[:, k, g * W:(g + 1) * W],
                                                        start=(f == 0), stop=(f == KC - 1), skip_group_check=True)
                        last.then_inc(ring.read[slot[u]], 1)

                with pe.Fori(0, 4) as i:
                    for v in range(4):
                        pe.wait_ge(xs_ready, i * 4 + (v + 1))
                        x = lambda f: xs[:, v % 2, f, :]
                        product(i, v, 0, v % 2, x)
                        product(i, v, 1, 2 + v % 2, x)
                        pe.wait_ge(a_ready, i * 4 + (v + 1))
                        for w in range(WC):
                            last = nc.tensor.transpose(ps[:, 4 + v % 2, w * P:(w + 1) * P], a[:, w * P:(w + 1) * P], core.ident[:])
                        last.then_inc(turned, 1)
                        pe.wait_ge(act_ready, i * 4 + (v + 1))
                        pe.wait_ge(y_act, i * 4 + (v + 1))
                        pe.wait_ge(y_dve, i * 4 + (v + 1))
                        product(i, v, 2, 6, lambda f: actT[:, f % WC, f // WC * M:(f // WC + 1) * M])

            def y_copies(i, v, engine):
                out = []
                for n in range(4):
                    g, stream = n // streams, n % streams
                    if n % 2 == engine:
                        out.append((ys[CAP * v:CAP * (v + 1), i, stream, g * W:(g + 1) * W],
                                    ps[n * CAP:(n + 1) * CAP, 6, 0:W]))
                return out

            @block.scalar
            def _(act):
                act.nop().then_inc(y_act, 1)
                with act.Fori(0, 4) as i:
                    for v in range(4):
                        act.wait_ge(ring.read[slot[1]], i * 4 + (lap[1] + v + 1))
                        nc.scalar.activation(sg[:], ps[:, v % 2, 0:W], ACT.Silu).then_inc(silus, 1)
                        act.wait_ge(turned, i * 4 + (v + 1))
                        nc.scalar.activation(actT, ps[:, 4 + v % 2, 0:W].rearrange("p (w m) -> p w m", w=WC), ACT.Copy).then_inc(act_ready, 1)
                        act.wait_ge(ring.read[slot[5]], i * 4 + (lap[5] + v + 1))
                        for dst, src in y_copies(i, v, 0):
                            last = nc.scalar.activation(dst, src, ACT.Copy)
                        last.then_inc(y_act, 1)

            @block.vector
            def _(dve):
                dve.nop().then_inc(y_dve, 1)
                with dve.Fori(0, 4) as i:
                    for v in range(4):
                        nc.vector.tensor_copy(xs[:, v % 2, :, :], xsT[:, :, i * 4 + v, :]).then_inc(xs_ready, 1)
                        dve.wait_ge(silus, i * 4 + (v + 1))
                        dve.wait_ge(ring.read[slot[3]], i * 4 + (lap[3] + v + 1))
                        nc.vector.tensor_tensor(a, sg[:], ps[:, 2 + v % 2, 0:W], ALU.mult).then_inc(a_ready, 1) if W == STRIP else \
                            nc.vector.tensor_tensor(a[:, 0:W], sg[:], ps[:, 2 + v % 2, 0:W], ALU.mult).then_inc(a_ready, 1)
                        dve.wait_ge(ring.read[slot[5]], i * 4 + (lap[5] + v + 1))
                        for dst, src in y_copies(i, v, 1):
                            last = nc.vector.tensor_copy(dst, src)
                        last.then_inc(y_dve, 1)


def moe(core, t, layer, lat_and_ctx):
    nc = core.nc
    s, streams = 2 + layer, len(lat_and_ctx)
    T = NT * streams
    M = CAP * streams
    with ExitStack() as stack:
        sb = lambda n, shape: stack.enter_context(nc.sbuf_tensor(f"moe{layer}_" + n, shape, F32))
        ys = sb("ys", [P, 4, streams, D])
        inner = stack.enter_context(ExitStack())
        xsT = inner.enter_context(nc.sbuf_tensor(f"moe{layer}_xsT", [P, KC, EXPERTS, M], F32))
        xn = ys[:].rearrange("p q s d -> p (q s d)")[:, 0:T * D].rearrange("p (t d) -> p t d", t=T)
        sel = ys[:].rearrange("p q s d -> p (q s d)")[:, T * D:T * (D + STRIP)].rearrange("p (t n) -> p t n", t=T)
        rows = xsT[:].rearrange("p c e m -> p (c e m)")[:, 0:EXPERTS * T * P].rearrange("p (e t) -> p e t", e=EXPERTS)
        spare = core.hT[:].rearrange("p c t -> p (c t)")
        pickedT = spare[:, 0:4 * STRIP].rearrange("p (q t) -> p q t", q=4)
        picked = spare[:, 4 * STRIP:4 * STRIP + T * STRIP].rearrange("p (t n) -> p t n", t=T)
        with nc.sbuf_tensor(f"moe{layer}_aff", [P, T, EXPERTS], F32) as aff:
            stage_norm(core, s, 1, lat_and_ctx, f"norm_moe{layer}", xn_keep=xn)
            stage_route(core, t, f"route{layer}", streams, aff[:], rows, sel, picked)
            stage_gather(core, f"gather{layer}", s, xn, sel, picked, xsT[:], pickedT, streams)
        stage_experts(core, t, f"experts{layer}", layer, streams, xsT[:], ys[:])
        inner.close()
        stage_residual(core, f"moe{layer}_res", s, 5, lambda k, j: pickedT[:, k, j * P:(j + 1) * P], 4 * P, lat_and_ctx,
                       rhs=lambda k, i, n: ys[:, k, i, n * STRIP:(n + 1) * STRIP])


def stage_context(core, t):
    with Stage(core, "context") as st:
        loaded = st.sem("loaded")
        with st.block() as block:
            @block.scalar
            def _(act):
                act.dma_start(core.ctx_x[:], t["ctx_2"].rearrange("b (j p) d -> p (b j) d", p=P)).then_inc(loaded, 16)
                act.wait_ge(loaded, 16)
def build(nc, t, out, stop=None):
    with ExitStack() as ctx:
        core = Core(nc, ctx)
        units = core.ring.units
        plan = ["gdn", "ffn0", "dsw", "ffn1", "even", "moe0", "odd", "moe1"]
        upto = plan.index(stop) + 1 if stop else len(plan)
        units += ada_units(t["w_ada"], 0)
        g = t["gdn_w_in"][0]
        units += [u for c in range(0, 4096, STRIP) for u in k_units(g, c, c + STRIP)] + k_units(g, 4096, 4112)
        units += ada_units(t["w_ada"], 1) + ada_units(t["w_ada_2"], 0) + ada_units(t["w_ada_2"], 1)
        units += residual_units(t["gdn_w_out"][0], D)
        if upto > 1:
            units += ffn_units(t["w_ffn_in"], 0) + residual_units(t["w_ffn_out"][0], HIDDEN)
        if upto > 2:
            w = t["dsw_w_in"][0]
            units += [u for c in range(0, 9 * STRIP, STRIP) for u in k_units(w, c, c + STRIP)]
            units += residual_units(t["dsw_w_out"][0], GH * DH)
        if upto > 3:
            units += ffn_units(t["w_ffn_in"], 1) + residual_units(t["w_ffn_out"][1], HIDDEN)
        if upto > 4:
            w = t["w_in_even_2"][0]
            units += [u for c0, c1 in strips(4 * STRIP + 2 * P) for u in k_units(w, c0, c1)]
            units += residual_units(t["w_out_even_2"][0], D)
        if upto > 5:
            units += k_units(t["w_router_2"][0], 0, EXPERTS) + expert_units(t, 0)
        if upto > 6:
            units += k_units(t["w_in_odd_2"][0], 0, 3 * P + ROPE)
            units += [u for c in range(0, 16 * QK, 4 * QK) for u in k_units(t["w_q_up_2"][0], c, c + 4 * QK, 2 * P)]
            units += [u for c in range(0, 4 * STRIP, STRIP) for u in k_units(t["w_kv_up_2"][0], c, c + STRIP, P)]
            units += residual_units(t["w_out_odd_2"][0], D)
        if upto > 7:
            units += k_units(t["w_router_2"][1], 0, EXPERTS) + expert_units(t, 1)
        stage_setup(core, t)
        stage_ada(core, 0)
        lat = [(core.x, 0)]
        hT = lambda k, j: core.hT[:, k, j * P:(j + 1) * P]
        stage_norm(core, 0, 0, lat, "norm_gdn")
        mixer_gdn(core, t, ctx)
        stage_residual(core, "gdn_res", 0, 2, hT, D, lat)
        if upto > 1:
            stage_norm(core, 0, 1, lat, "norm_ffn0")
            with nc.sbuf_tensor("aT0", [P, HC, S], F32) as aT:
                stage_ffn(core, "ffn0", aT)
                stage_residual(core, "ffn0_res", 0, 5, lambda k, j: aT[:, k, j * P:(j + 1) * P], HIDDEN, lat)
        if upto > 2:
            stage_norm(core, 1, 0, lat, "norm_dsw")
            mixer_dsw(core, t)
            stage_residual(core, "dsw_res", 1, 2, hT, GH * DH, lat)
        if upto > 3:
            stage_norm(core, 1, 1, lat, "norm_ffn1")
            with nc.sbuf_tensor("aT1", [P, HC, S], F32) as aT:
                stage_ffn(core, "ffn1", aT)
                stage_residual(core, "ffn1_res", 1, 5, lambda k, j: aT[:, k, j * P:(j + 1) * P], HIDDEN, lat)
        if upto > 4:
            both = lat + [(core.ctx_x, 1)]
            stage_context(core, t)
            stage_norm(core, 2, 0, both, "norm_even")
            mixer_even(core, t)
            stage_residual(core, "even_res", 2, 2, hT, D, both)
        if upto > 5:
            moe(core, t, 0, both)
        if upto > 6:
            stage_norm(core, 3, 0, both, "norm_odd")
            mixer_odd(core, t)
            stage_residual(core, "odd_res", 3, 2, hT, D, lat)
        if upto > 7:
            moe(core, t, 1, lat)
        assert core.ring.taken == len(units) == core.ring.loaded
        with Stage(core, "store") as st:
            with st.block() as block:
                @block.sync
                def _(sp):
                    sp.dma_start(out.rearrange("b (j p) d -> p (b j) d", p=P), core.x[:]).then_inc(core.stored, 16)
                    sp.wait_ge(core.stored, 16)


def kernel(**inputs):
    import concourse.bacc as bacc
    from concourse.bass_utils import run_bass_kernel_spmd

    nc = bacc.Bacc("TRN2", target_bir_lowering=False, num_devices=1)
    arrays, t = {}, {}
    named = {n: np.ascontiguousarray(a) for n, a in inputs.items()}
    named["const"] = shape_constants()
    named["marks"] = bias_constants()
    named["rope_even"], named["rope_odd"] = rope_constants(DH), rope_constants(ROPE)
    named["route"] = route_constants()
    for name, a in named.items():
        arrays[f"in_{name}"] = a
        t[name] = nc.dram_tensor(f"in_{name}", a.shape, mybir.dt.from_np(a.dtype), kind="ExternalInput").ap()
    t["bias_rows"] = nc.dram_tensor("distance_bias", (NG * GH, 2 * S), F32, kind="Internal").ap()
    t["affinity"] = nc.dram_tensor("affinity", (EXPERTS, 2 * S), F32, kind="Internal").ap()
    out = nc.dram_tensor("out", (1, S, D), F32, kind="ExternalOutput").ap()
    build(nc, t, out, STOP)
    r = run_bass_kernel_spmd(nc, [arrays], core_ids=[0])
    return r.results[0]["out"]


STOP = None
```

```python
import math
from contextlib import ExitStack

import numpy as np
import concourse.bass as bass
from concourse import mybir

F32 = mybir.dt.float32
ALU = mybir.AluOpType
ACT = mybir.ActivationFunctionType
AX = mybir.AxisListType

P = 128
D = 1024
KC = D // P
S = 256
NT = S // P
STRIP = 512
SLOTS = 6
SLOT = KC * STRIP
EPS = 1e-6
HIDDEN = 2816
HC = HIDDEN // P
N_MOD = 6
MODC = N_MOD * KC
GH = 8
CH = 64
TAPS = 4
LEVELS = [1, 2, 4, 8, 16, 32]
EXPERTS = 16
CAP = 2 * S // EXPERTS


class Ring:

    def __init__(self, nc, ctx):
        self.tile = ctx.enter_context(nc.sbuf_tensor("weight_ring", [P, SLOTS, SLOT], F32))
        self.full = [ctx.enter_context(nc.semaphore(f"ring_full_{s}")) for s in range(SLOTS)]
        self.read = [ctx.enter_context(nc.semaphore(f"ring_read_{s}")) for s in range(SLOTS)]
        self.units = []
        self.loaded = 0
        self.taken = 0

    def take(self, count):
        first = self.taken
        self.taken += count
        return first

    def view(self, n):
        _, k, w = self.units[n]
        return self.tile[:, n % SLOTS, 0:k * w].rearrange("p (k w) -> p k w", k=k)

    def load(self, sp, n):
        if n >= SLOTS:
            sp.wait_ge(self.read[n % SLOTS], n // SLOTS)
        sp.dma_start(self.view(n), self.units[n][0]).then_inc(self.full[n % SLOTS], 16)

    def load_ahead(self, sp, upto):
        while self.loaded < min(upto, len(self.units)):
            self.load(sp, self.loaded)
            self.loaded += 1

    def wait(self, pe, n):
        pe.wait_ge(self.full[n % SLOTS], 16 * (n // SLOTS + 1))

    def wait_read(self, eng, n):
        eng.wait_ge(self.read[n % SLOTS], n // SLOTS + 1)


class Core:

    def __init__(self, nc, ctx):
        self.nc = nc
        sb = lambda name, shape: ctx.enter_context(nc.sbuf_tensor(name, shape, F32))
        self.ring = Ring(nc, ctx)
        self.x = sb("x", [P, NT, D])
        self.ctx_x = sb("ctx_x", [P, NT, D])
        self.hT = sb("hT", [P, KC, 2 * S])
        self.ident = sb("ident", [P, P])
        self.ones = sb("ones", [P, P])
        self.mods = sb("mods", [P, 4, MODC, 2])
        self.cond = sb("cond", [P, 2, KC, 32])
        self.norms = sb("norms", [P, 88])
        self.bias = sb("bias", [P, 4, MODC])
        self.convw = sb("convw", [P, TAPS, 24])
        self.half = sb("half", [P, 16])
        self.stored = ctx.enter_context(nc.semaphore("result_stored"))
        self.ps = ctx.enter_context(nc.psum_tensor("ps", [P, 8, STRIP], F32))

    def gain(self, kind, s):
        v = (s // 2) * 4 + kind * 2 + s % 2
        return self.norms[:, v * KC:(v + 1) * KC]

    def mod(self, s, which, m=0):
        return self.mods[:, s, which * KC:(which + 1) * KC, m]


class Stage:

    def __init__(self, core, name):
        self.core, self.nc, self.name = core, core.nc, name
        self.sems = []
        self.stack = ExitStack()

    def sb(self, name, shape):
        return self.stack.enter_context(self.nc.sbuf_tensor(f"{self.name}_{name}", shape, F32))

    def sem(self, name):
        s = self.nc.alloc_semaphore(f"{self.name}_{name}")
        self.sems.append(s)
        return s

    def __enter__(self):
        return self

    def block(self):
        return self.nc.Block(no_gpsimd_drain=True)

    def __exit__(self, *error):
        self.stack.__exit__(*error)
        if error[0] is None and self.sems:
            for s in self.sems:
                self.nc.gpsimd.sem_clear(s)
                self.nc.release_semaphore(s)
        return False


def ring_in_stage(core, block, count):
    ring = core.ring

    @block.sync
    def _(sp):
        ring.load_ahead(sp, ring.taken + SLOTS)


def stage_setup(core, t):
    nc, ps = core.nc, core.ps
    with Stage(core, "setup") as st:
        rows = st.sb("rows", [96, 4, P])
        filled = st.sem("filled")
        loaded_const, loaded_x, loaded_rows = st.sem("loaded_const"), st.sem("loaded_x"), st.sem("loaded_rows")
        transposed, cols_ready, zeroed, conds = (st.sem(n) for n in ("transposed", "cols_ready", "zeroed", "conds"))
        row_loads = [(0, rows[0:16, 0, :], t["norm_mix"].rearrange("l (c p) -> (l c) p", p=P)),
                     (0, rows[16:32, 0, :], t["norm_ffn"].rearrange("l (c p) -> (l c) p", p=P)),
                     (0, rows[32:48, 0, :], t["norm_mix_2"].rearrange("l (c p) -> (l c) p", p=P)),
                     (0, rows[48:64, 0, :], t["norm_ffn_2"].rearrange("l (c p) -> (l c) p", p=P)),
                     (0, rows[64:72, 0, :], t["c"].rearrange("l (c p) -> (l c) p", p=P)),
                     (0, rows[72:80, 0, :], t["c_2"].rearrange("l (c p) -> (l c) p", p=P)),
                     (0, rows[80:88, 0, :], t["c_ctx_2"].rearrange("(c p) -> c p", p=P)),
                     (0, rows[:, 1, :], t["b_ada"].rearrange("l (c p) -> (l c) p", p=P)),
                     (0, rows[:, 2, :], t["b_ada_2"].rearrange("l (c p) -> (l c) p", p=P)),
                     (0, rows[:, 3, :], t["gdn_conv"].rearrange("l k (c p) -> (l k c) p", p=P))]
        with st.block() as block:
            @block.sync
            def _(sp):
                sp.wait_ge(loaded_rows, 16 * len(row_loads))
                core.ring.load_ahead(sp, SLOTS)

            @block.scalar
            def _(act):
                act.dma_start(core.ident[:], t["const"][:, 0:P]).then_inc(loaded_const, 16)
                for _, dst, src in row_loads:
                    act.dma_start(dst, src).then_inc(loaded_rows, 16)
                act.dma_start(core.x[:], t["x"].rearrange("b (j p) d -> p (b j) d", p=P)).then_inc(loaded_x, 16)
                act.wait_ge(transposed, 1)
                act.wait_ge(zeroed, 1)
                pairs = ((64, 64), (72, 80))
                for b in range(2):
                    for m in range(2):
                        v = pairs[b][m]
                        nc.scalar.activation(core.cond[:, b, :, m], ps[:, 0, v:v + KC], ACT.Silu).then_inc(conds, 1)
                act.wait_ge(conds, 4)
                act.wait_ge(loaded_x, 16)
                act.wait_ge(filled, 2)

            @block.gpsimd
            def _(pool):
                nc.gpsimd.memset(core.half[:], -0.5).then_inc(filled, 1)
                nc.gpsimd.memset(core.ones[:], 1.0).then_inc(filled, 1)

            @block.tensor
            def _(pe):
                pe.wait_ge(loaded_const, 16)
                pe.wait_ge(loaded_rows, 16 * len(row_loads))
                for i in range(4):
                    n = 88 if i == 0 else 96
                    nc.tensor.transpose(ps[:, i, 0:n], rows[0:n, i, :], core.ident[0:n, 0:n]).then_inc(transposed, 1)

            @block.vector
            def _(dve):
                nc.vector.memset(core.cond[:], 0.0).then_inc(zeroed, 1)
                dve.wait_ge(transposed, 4)
                dve.wait_ge(conds, 4)
                nc.vector.tensor_copy(core.norms[:], ps[:, 0, 0:88])
                nc.vector.tensor_copy(core.bias[:, 0:2, :], ps[:, 1, 0:96].rearrange("p (l c) -> p l c", l=2))
                nc.vector.tensor_copy(core.bias[:, 2:4, :], ps[:, 2, 0:96].rearrange("p (l c) -> p l c", l=2))
                nc.vector.tensor_copy(core.convw[:], ps[:, 3, 0:96].rearrange("p (k c) -> p k c", k=TAPS))


ADA_COLS = 2048


def ada_units(w, layer):
    return [(w[layer, 2 * P * i:2 * P * (i + 1), g * ADA_COLS:(g + 1) * ADA_COLS].rearrange("(k p) n -> p k n", p=P), 2, ADA_COLS)
            for g in range(3) for i in range(4)]


class Modulation:

    def __init__(self, core, st, groups, units=None):
        self.core, self.groups = core, groups
        if units is None:
            first = core.ring.take(4 * len(groups))
            units = range(first, first + 4 * len(groups))
        self.units = units
        self.rows = st.sb("mod_rows", [P, STRIP])
        self.rows_copied, self.turned, self.stored = (st.sem("mod_" + n) for n in ("rows_copied", "turned", "stored"))

    def multiply(self, pe, u):
        nc, ps, ring = self.core.nc, self.core.ps, self.core.ring
        q, i = u // 4, u % 4
        s, _, bank, _ = self.groups[q]
        if q and i == 0:
            pe.wait_ge(self.rows_copied, q)
        ring.wait(pe, self.units[u])
        for k in range(2):
            for f in range(4):
                last = nc.tensor.matmul(ps[32 * f:32 * f + 32, bank, :], self.core.cond[:, s // 2, 2 * i + k, :],
                                        ring.view(self.units[u])[:, k, f * STRIP:(f + 1) * STRIP],
                                        start=(i + k == 0), stop=(i + k == 4), skip_group_check=True)
        last.then_inc(ring.read[self.units[u] % SLOTS], 1)

    def copy(self, act, q):
        self.core.ring.wait_read(act, self.units[4 * q + 3])
        if q:
            act.wait_ge(self.turned, q)
        self.core.nc.scalar.activation(self.rows[:], self.core.ps[:, self.groups[q][2], :], ACT.Copy).then_inc(self.rows_copied, 1)

    def turn(self, pe, q):
        nc, ps = self.core.nc, self.core.ps
        pe.wait_ge(self.rows_copied, q + 1)
        if q:
            pe.wait_ge(self.stored, q)
        for n in range(4):
            last = nc.tensor.transpose(ps[:, self.groups[q][3], n * P:(n + 1) * P], self.rows[:, n * P:(n + 1) * P], self.core.ident[:])
        last.then_inc(self.turned, 1)

    def store(self, dve, q):
        core, nc = self.core, self.core.nc
        s, g, _, bank = self.groups[q]
        dve.wait_ge(self.turned, q + 1)
        src = core.ps[:, bank, :].rearrange("p (n f r) -> p f n r", n=4, f=4)
        for m in range(2):
            out = core.mods[:, s, 16 * g:16 * (g + 1), m].rearrange("p (f n) -> p f n", f=4)
            b = core.bias[:, s, 16 * g:16 * (g + 1)].rearrange("p (f n) -> p f n", f=4)
            last = nc.vector.tensor_tensor(out, src[:, :, :, m], b, ALU.add)
        last.then_inc(self.stored, 1)


def stage_ada(core, s, groups):
    with Stage(core, f"ada{s}") as st:
        mod = Modulation(core, st, [(s, g, g % 2, 2 + g % 2) for g in range(groups)])
        with st.block() as block:
            ring_in_stage(core, block, 4 * groups)

            @block.tensor
            def _(pe):
                for g in range(groups):
                    for i in range(4):
                        mod.multiply(pe, 4 * g + i)
                    mod.turn(pe, g)

            @block.scalar
            def _(act):
                for g in range(groups):
                    mod.copy(act, g)

            @block.vector
            def _(dve):
                for g in range(groups):
                    mod.store(dve, g)


def stage_norm(core, s, kind, streams, name, xn_keep=None):
    nc, ps = core.nc, core.ps
    T = NT * len(streams)
    with Stage(core, name) as st:
        junk = st.sb("junk", [P, 2, D])
        xn = xn_keep if xn_keep is not None else st.sb("xn", [P, T, D])
        ssq, rstd, ms = st.sb("ssq", [P, T]), st.sb("rstd", [P, T]), st.sb("ms", [P, T])
        scale = st.sb("scale", [P, 2, KC])
        squared, normed = ([st.sem(f"{n}_{e}") for e in ("act", "dve")] for n in ("squared", "normed"))
        mean, rstds, turned, scales = (st.sem(n) for n in ("mean", "rstds", "turned", "scales"))
        tile = lambda j: streams[j // NT][0][:, j % NT, :]
        with st.block() as block:
            @block.scalar
            def _(act):
                for j in range(0, T, 2):
                    if j:
                        act.wait_ge(squared[0], j // 2)
                    nc.scalar.activation(junk[:, 0, :], tile(j), ACT.Square, accum_out=ssq[:, j:j + 1]).then_inc(squared[0], 1)
                act.wait_ge(rstds, 1)
                for j in range(0, T, 2):
                    nc.scalar.activation(xn[:, j, :], tile(j), ACT.Copy, scale=rstd[:, j:j + 1]).then_inc(normed[0], 1)
                act.wait_ge(scales, 2 * len(streams))
                for c in range(0, KC, 2):
                    act.wait_ge(turned, c + 1)
                    for i, (_, m) in enumerate(streams):
                        nc.scalar.activation(core.hT[:, c, i * S:(i + 1) * S], ps[:, c, i * S:(i + 1) * S], ACT.Identity,
                                             bias=core.mod(s, 3 * kind, m)[:, c:c + 1], scale=scale[:, m, c:c + 1])

            @block.gpsimd
            def _(pool):
                pool.wait_ge(mean, 1)
                nc.gpsimd.tensor_tensor(rstd[:], ms[:], core.half[:, 0:T], ALU.pow).then_inc(rstds, 1)

            @block.vector
            def _(dve):
                for j in range(1, T, 2):
                    if j > 1:
                        dve.wait_ge(squared[1], j // 2)
                    nc.vector.scalar_tensor_tensor(junk[:, 1, :], tile(j), 1.0, tile(j), ALU.mult, ALU.mult,
                                                   accum_out=ssq[:, j:j + 1]).then_inc(squared[1], 1)
                for i, (_, m) in enumerate(streams):
                    nc.vector.tensor_scalar(scale[:, m, :], core.mod(s, 3 * kind + 1, m), 1.0, None, ALU.add).then_inc(scales, 1)
                    dve.wait_ge(scales, 2 * i + 1)
                    nc.vector.tensor_tensor(scale[:, m, :], scale[:, m, :], core.gain(kind, s), ALU.mult).then_inc(scales, 1)
                for by in squared:
                    dve.wait_ge(by, T // 2)
                nc.vector.tensor_scalar(ms[:], ssq[:], 1.0 / D, EPS, ALU.mult, ALU.add).then_inc(mean, 1)
                dve.wait_ge(rstds, 1)
                for j in range(1, T, 2):
                    nc.vector.tensor_scalar(xn[:, j, :], tile(j), rstd[:, j:j + 1], None, ALU.mult).then_inc(normed[1], 1)
                dve.wait_ge(scales, 2 * len(streams))
                for c in range(1, KC, 2):
                    dve.wait_ge(turned, c + 1)
                    for i, (_, m) in enumerate(streams):
                        nc.vector.tensor_scalar(core.hT[:, c, i * S:(i + 1) * S], ps[:, c, i * S:(i + 1) * S],
                                                scale[:, m, c:c + 1], core.mod(s, 3 * kind, m)[:, c:c + 1], ALU.mult, ALU.add)

            @block.tensor
            def _(pe):
                for j in range(T):
                    pe.wait_ge(normed[j % 2], j // 2 + 1)
                    for c in range(KC):
                        done = nc.tensor.transpose(ps[:, c, j * P:(j + 1) * P], xn[:, j, c * P:(c + 1) * P], core.ident[:])
                        if j == T - 1:
                            done.then_inc(turned, 1)


def k_units(w, c0, c1, rows=D):
    out = []
    for k0 in range(0, rows // P, KC):
        k1 = min(k0 + KC, rows // P)
        out.append((w[k0 * P:k1 * P, c0:c1].rearrange("(k p) n -> p k n", p=P), k1 - k0, c1 - c0))
    return out


def strips(cols):
    return [(c, min(c + STRIP, cols)) for c in range(0, cols, STRIP)]


def residual_units(w, rows):
    return [u for c0, c1 in strips(D) for u in k_units(w, c0, c1, rows)]


def project_strip(core, pe, lhs, tiles, first, count, banks):
    nc, ring = core.nc, core.ring
    total = sum(ring.units[i][1] for i in range(first, first + count))
    k0 = 0
    for n in range(first, first + count):
        ring.wait(pe, n)
        kc, w = ring.units[n][1:]
        for j in range(tiles):
            for k in range(kc):
                last = nc.tensor.matmul(core.ps[:, banks[j], 0:w], lhs(k0 + k, j), ring.view(n)[:, k, :],
                                        start=(k0 + k == 0), stop=(k0 + k == total - 1))
        last.then_inc(ring.read[n % SLOTS], 1)
        k0 += kc


def stage_residual(core, name, s, which, lhs, rows, streams, rhs=None, out=None):
    nc, ps, ring = core.nc, core.ps, core.ring
    T = NT * len(streams)
    per = (rows // P + KC - 1) // KC
    with Stage(core, name) as st:
        diag = st.sb("diag", [P, len(streams), D])
        gate = st.sb("gate", [P, len(streams), D])
        part = st.sb("part", [P, 2, STRIP])
        diags, spread, gates, gated, added = (st.sem(n) for n in ("diags", "spread", "gates", "gated", "added"))
        first = ring.take(0 if rhs else 2 * per)
        multiplied = st.sem("multiplied")

        def product(pe, n, banks):
            if not rhs:
                return project_strip(core, pe, lhs, T, first + n * per, per, banks)
            for j in range(T):
                for k in range(rows // P):
                    last = nc.tensor.matmul(ps[:, banks[j], :], lhs(k, j), rhs(k, j // NT, n), start=(k == 0), stop=(k == rows // P - 1))
            last.then_inc(multiplied, 1)

        with st.block() as block:
            @block.sync
            def _(sp):
                ring.load_ahead(sp, ring.taken + SLOTS)
                if out is not None:
                    for n in range(2):
                        cols = slice(n * STRIP, (n + 1) * STRIP)
                        sp.wait_ge(added, T * (n + 1))
                        sp.dma_start(out.rearrange("b (j p) d -> p (b j) d", p=P)[:, :, cols],
                                     streams[0][0][:, :, cols]).then_inc(core.stored, 16)
                    sp.wait_ge(core.stored, 32)

            @block.tensor
            def _(pe):
                pe.wait_ge(diags, len(streams))
                for i in range(len(streams)):
                    for half in range(2):
                        last = nc.tensor.matmul(ps[:, 2 * i + half, :], core.ones[:], diag[:, i, half * STRIP:(half + 1) * STRIP],
                                                start=True, stop=True)
                last.then_inc(spread, 1)
                product(pe, 0, [4 + j for j in range(T)])
                pe.wait_ge(gates, 1)
                product(pe, 1, list(range(T)))

            @block.scalar
            def _(act):
                act.wait_ge(spread, 1)
                nc.scalar.activation(gate[:].rearrange("p i n -> p (i n)"),
                                     ps[:, 0:2 * len(streams), :].rearrange("p b n -> p (b n)"), ACT.Copy).then_inc(gates, 1)

            @block.vector
            def _(dve):
                for i, (_, m) in enumerate(streams):
                    nc.vector.tensor_tensor(diag[:, i, :].rearrange("p (c q) -> p c q", c=KC),
                                            core.ident[:].unsqueeze(1).broadcast_to([P, KC, P]),
                                            core.mod(s, which, m).unsqueeze(2).broadcast_to([P, KC, P]), ALU.mult).then_inc(diags, 1)
                dve.wait_ge(gates, 1)
                i = 0
                for n in range(2):
                    if rhs:
                        dve.wait_ge(multiplied, n + 1)
                    else:
                        ring.wait_read(dve, first + (n + 1) * per - 1)
                    for j in range(T):
                        if i >= 2:
                            dve.wait_ge(added, i - 1)
                        nc.vector.tensor_tensor(part[:, i % 2, :], ps[:, (4 if n == 0 else 0) + j, :],
                                                gate[:, j // NT, n * STRIP:(n + 1) * STRIP], ALU.mult).then_inc(gated, 1)
                        i += 1
                dve.wait_ge(added, 2 * T)

            @block.gpsimd
            def _(pool):
                i = 0
                for n in range(2):
                    for j in range(T):
                        pool.wait_ge(gated, i + 1)
                        x = streams[j // NT][0][:, j % NT, n * STRIP:(n + 1) * STRIP]
                        nc.gpsimd.tensor_tensor(x, x, part[:, i % 2, :], ALU.add).then_inc(added, 1)
                        i += 1


def ffn_units(w, layer):
    out = []
    for c0, c1 in strips(HIDDEN):
        out += k_units(w[layer], c0, c1) + k_units(w[layer], HIDDEN + c0, HIDDEN + c1)
    return out


def stage_ffn(core, name, aT, loads=()):
    nc, ps, ring = core.nc, core.ps, core.ring
    pairs = strips(HIDDEN)
    with Stage(core, name) as st:
        sg = st.sb("sg", [P, 2, NT, STRIP])
        a = st.sb("a", [P, 2, NT, STRIP])
        silus, products, turned, copied = (st.sem(n) for n in ("silus", "products", "turned", "copied"))
        first = ring.take(2 * len(pairs))
        loaded = st.sem("loaded")
        with st.block() as block:
            ring_in_stage(core, block, 2 * len(pairs))

            @block.tensor
            def _(pe):
                def turn(i):
                    pe.wait_ge(products, i + 1)
                    for j in range(NT):
                        for q in range((pairs[i][1] - pairs[i][0]) // P):
                            last = nc.tensor.transpose(ps[:, 4 * (i % 2) + j, q * P:(q + 1) * P],
                                                       a[:, i % 2, j, q * P:(q + 1) * P], core.ident[:])
                    last.then_inc(turned, 1)
                for i in range(len(pairs)):
                    if i >= 2:
                        pe.wait_ge(copied, i - 1)
                    for up in range(2):
                        project_strip(core, pe, lambda k, j: core.hT[:, k, j * P:(j + 1) * P], NT, first + 2 * i + up, 1,
                                      [4 * (i % 2) + 2 * up + j for j in range(NT)])
                    if i >= 1:
                        turn(i - 1)
                turn(len(pairs) - 1)

            @block.scalar
            def _(act):
                def copy(i):
                    w = pairs[i][1] - pairs[i][0]
                    act.wait_ge(turned, i + 1)
                    for j in range(NT):
                        last = nc.scalar.activation(aT[:, pairs[i][0] // P:pairs[i][1] // P, j * P:(j + 1) * P],
                                                    ps[:, 4 * (i % 2) + j, 0:w].rearrange("p (q t) -> p q t", t=P), ACT.Copy)
                    last.then_inc(copied, 1)
                for dst, src in loads:
                    act.dma_start(dst, src).then_inc(loaded, 16)
                for i, (c0, c1) in enumerate(pairs):
                    ring.wait_read(act, first + 2 * i)
                    if i >= 2:
                        act.wait_ge(products, i - 1)
                    for j in range(NT):
                        last = nc.scalar.activation(sg[:, i % 2, j, 0:c1 - c0], ps[:, 4 * (i % 2) + j, 0:c1 - c0], ACT.Silu)
                    last.then_inc(silus, 1)
                    if i >= 1:
                        copy(i - 1)
                copy(len(pairs) - 1)
                if loads:
                    act.wait_ge(loaded, 16 * len(loads))

            @block.vector
            def _(dve):
                for i, (c0, c1) in enumerate(pairs):
                    dve.wait_ge(silus, i + 1)
                    ring.wait_read(dve, first + 2 * i + 1)
                    if i >= 2:
                        dve.wait_ge(turned, i - 1)
                    for j in range(NT):
                        last = nc.vector.tensor_tensor(a[:, i % 2, j, 0:c1 - c0], sg[:, i % 2, j, 0:c1 - c0],
                                                       ps[:, 4 * (i % 2) + 2 + j, 0:c1 - c0], ALU.mult)
                    last.then_inc(products, 1)


def stage_gdn_project(core, t, conv, zs, ab):
    nc, ps, ring = core.nc, core.ps, core.ring
    with Stage(core, "gdnproj") as st:
        pre = st.sb("pre", [P, 2, 4, TAPS - 1 + S])
        acc = st.sb("acc", [P, 2, 4, S])
        padded, pre_copied, convolved, tap, silus = (st.sem(n) for n in ("padded", "pre_copied", "convolved", "tap", "silus"))
        first = ring.take(17)
        units = [first + 2 * u for u in range(9)]
        mod = Modulation(core, st, [(0, 1, 6, 7), (0, 2, 6, 7)], [first + 2 * u + 1 for u in range(8)])
        with st.block() as block:
            ring_in_stage(core, block, 17)

            @block.tensor
            def _(pe):
                for u in range(6):
                    ring.wait(pe, units[u])
                    if u >= 2:
                        pe.wait_ge(pre_copied, u - 1)
                    w = ring.view(units[u])
                    for q in range(4):
                        for k in range(KC):
                            last = nc.tensor.matmul(ps[:, 2 * (u % 2) + q // 2, (q % 2) * S:(q % 2 + 1) * S],
                                                    w[:, k, q * P:(q + 1) * P], core.hT[:, k, 0:S],
                                                    start=(k == 0), stop=(k == KC - 1))
                    last.then_inc(ring.read[units[u] % SLOTS], 1)
                    if u == 4:
                        mod.turn(pe, 0)
                    mod.multiply(pe, u)
                lhs = lambda k, j: core.hT[:, k, j * P:(j + 1) * P]
                project_strip(core, pe, lhs, NT, units[6], 1, [4, 5])
                mod.multiply(pe, 6)
                pe.wait_ge(pre_copied, 6)
                project_strip(core, pe, lhs, NT, units[7], 1, [2, 3])
                mod.multiply(pe, 7)
                project_strip(core, pe, lhs, NT, units[8], 1, [0, 1])
                mod.turn(pe, 1)

            @block.scalar
            def _(act):
                act.wait_ge(padded, 1)
                for u in range(6):
                    if u == 4:
                        mod.copy(act, 0)
                    if u >= 2:
                        act.wait_ge(convolved, 4 * (u - 1))
                    ring.wait_read(act, units[u])
                    nc.scalar.activation(pre[:, u % 2, :, TAPS - 1:], ps[:, 2 * (u % 2):2 * (u % 2) + 2, :].rearrange(
                        "p b (q t) -> p (b q) t", t=S), ACT.Copy).then_inc(pre_copied, 1)
                    if u >= 1:
                        act.wait_ge(convolved, 4 * u)
                        nc.scalar.activation(conv[:, 4 * (u - 1):4 * u, :], acc[:, (u - 1) % 2, :, :], ACT.Silu).then_inc(silus, 1)
                act.wait_ge(convolved, 24)
                nc.scalar.activation(conv[:, 20:24, :], acc[:, 1, :, :], ACT.Silu).then_inc(silus, 1)
                for i in range(2):
                    ring.wait_read(act, units[6 + i])
                    nc.scalar.activation(zs[:, :, i * STRIP:(i + 1) * STRIP], ps[:, 4 - 2 * i:6 - 2 * i, :], ACT.Silu)
                mod.copy(act, 1)
                ring.wait_read(act, units[8])
                nc.scalar.activation(ab[:], ps[:, 0:2, 0:16], ACT.Copy)

            @block.vector
            def _(dve):
                nc.vector.memset(pre[:, :, :, 0:TAPS - 1], 0.0).then_inc(padded, 1)
                taps = 0
                for u in range(6):
                    if u == 5:
                        mod.store(dve, 0)
                    dve.wait_ge(pre_copied, u + 1)
                    if u >= 2:
                        dve.wait_ge(silus, u - 1)
                    for q in range(4):
                        c, b = 4 * u + q, u % 2
                        w = core.convw
                        nc.vector.tensor_scalar(acc[:, b, q, :], pre[:, b, q, 0:S], w[:, 0, c:c + 1], None, ALU.mult).then_inc(tap, 1)
                        for k in range(1, TAPS):
                            taps += 1
                            dve.wait_ge(tap, taps)
                            nc.vector.scalar_tensor_tensor(acc[:, b, q, :], pre[:, b, q, k:k + S], w[:, k, c:c + 1], acc[:, b, q, :],
                                                           ALU.mult, ALU.add).then_inc(tap if k < TAPS - 1 else convolved, 1)
                mod.store(dve, 1)


def stage_gdn_gates(core, t, conv, zs, ab, masks, co):
    nc, ps = core.nc, core.ps
    with Stage(core, "gdngate") as st:
        sq, lnr = st.sb("sq", [P, 2, 2 * S]), st.sb("lnr", [P, GH, 2 * S])
        alog, dtb = st.sb("alog", [P, GH]), st.sb("dtb", [P, GH])
        y, e, l, nb, ea, g = (st.sb(n, [P, NT, GH]) for n in ("y", "e", "l", "nb", "ea", "g"))
        gain, gain_in, gained = st.sb("gain", [P, P]), st.sem("gain_in"), st.sem("gained")
        loaded, masks_in = st.sem("loaded"), st.sem("masks_in")
        squares, sums, logs, rsqrts = (st.sem(n) for n in ("squares", "sums", "logs", "rsqrts"))
        acts, dves, gsums = st.sem("gate_acts"), st.sem("gate_dves"), st.sem("gsums")
        mod = Modulation(core, st, [(1, g, 4, 5) for g in range(3)])
        with st.block() as block:
            @block.sync
            def _(sp):
                sp.dma_start(alog[:], t["gdn_a_log"].broadcast_to([P, GH])).then_inc(loaded, 16)
                sp.dma_start(dtb[:], t["gdn_dt_bias"].broadcast_to([P, GH])).then_inc(loaded, 16)
                sp.dma_start(masks[:], t["const"][:, P:P + masks.shape[1]]).then_inc(masks_in, 16)
                sp.dma_start(gain[:], t["gdn_out_norm"].broadcast_to([P, P])).then_inc(gain_in, 16)
                core.ring.load_ahead(sp, core.ring.taken + SLOTS)

            @block.gpsimd
            def _(pool):
                pool.wait_ge(gain_in, 16)
                z = zs[:].rearrange("p j (h d) -> p (j h) d", d=P)
                nc.gpsimd.tensor_tensor(z, z, gain[:].unsqueeze(1).broadcast_to([P, NT * GH, P]), ALU.mult).then_inc(gained, 1)

            @block.scalar
            def _(act):
                def link(i, ins):
                    ins.then_inc(acts, 1)
                act.wait_ge(loaded, 32)
                act.wait_ge(dves, 2)
                nc.scalar.activation(e[:], l[:], ACT.Exp, scale=-1.0).then_inc(acts, 1)
                nc.scalar.activation(nb[:], ab[:, :, GH:], ACT.Exp, scale=-1.0).then_inc(acts, 1)
                nc.scalar.activation(ea[:, 0, :], alog[:], ACT.Exp).then_inc(acts, 1)
                act.wait_ge(dves, 3)
                nc.scalar.activation(l[:], e[:], ACT.Ln).then_inc(acts, 1)
                for i in range(8):
                    if i in (3, 6):
                        mod.copy(act, i // 3 - 1)
                    act.wait_ge(sums, i + 1)
                    nc.scalar.activation(lnr[:, i, :], ps[:, i % 2, :], ACT.Ln, bias=co["eps"][:, 0:1]).then_inc(logs, 1)
                act.wait_ge(logs, 8)
                for i in range(8):
                    nc.scalar.activation(lnr[:, i, :], lnr[:, i, :], ACT.Exp, scale=-0.5).then_inc(rsqrts, 1)
                act.wait_ge(gsums, 1)
                act.wait_ge(dves, 9)
                nc.scalar.activation(co["kbg"][:], co["gc"][:], ACT.Exp).then_inc(acts, 1)
                nc.scalar.activation(co["kd"][:], y[:], ACT.Exp)
                nc.scalar.activation(co["tot"][:], ps[:, 3, 64:96].rearrange("p (f j h) -> p f j h", f=2, j=NT), ACT.Exp)
                mod.copy(act, 2)
                act.wait_ge(gained, 1)

            @block.vector
            def _(dve):
                def square(i):
                    pair = conv[:, 2 * i:2 * i + 2, :].rearrange("p c t -> p (c t)")
                    if i >= 2:
                        dve.wait_ge(sums, i - 1)
                    nc.vector.tensor_tensor(sq[:, i % 2, :], pair, pair, ALU.mult).then_inc(squares, 1)
                nc.vector.memset(co["eps"][:], EPS)
                square(0)
                square(1)
                dve.wait_ge(loaded, 32)
                nc.vector.tensor_tensor(y[:], ab[:, :, 0:GH], dtb[:].unsqueeze(1).broadcast_to([P, NT, GH]), ALU.add).then_inc(dves, 1)
                dve.wait_ge(dves, 1)
                nc.vector.scalar_tensor_tensor(l[:], y[:], -1.0, y[:], ALU.mult, ALU.max).then_inc(dves, 1)
                dve.wait_ge(acts, 3)
                nc.vector.tensor_scalar(e[:], e[:], 1.0, None, ALU.add).then_inc(dves, 1)
                nc.vector.tensor_scalar(nb[:], nb[:], 1.0, None, ALU.add).then_inc(dves, 1)
                dve.wait_ge(dves, 4)
                nc.vector.reciprocal(co["beta"][:], nb[:]).then_inc(dves, 1)
                dve.wait_ge(acts, 4)
                nc.vector.scalar_tensor_tensor(g[:], y[:], 0.0, l[:], ALU.max, ALU.add).then_inc(dves, 1)
                dve.wait_ge(dves, 6)
                nc.vector.scalar_tensor_tensor(g[:], g[:], -1.0, ea[:, 0, :].unsqueeze(1).broadcast_to([P, NT, GH]),
                                               ALU.mult, ALU.mult).then_inc(dves, 1)
                dve.wait_ge(gsums, 1)
                nc.vector.tensor_copy(co["gc"][:], ps[:, 3, 0:16].rearrange("p (j h) -> p j h", j=NT)).then_inc(dves, 1)
                dve.wait_ge(dves, 8)
                nc.vector.scalar_tensor_tensor(y[:], co["gc"][:], -1.0, ps[:, 3, 32:48].rearrange("p (j h) -> p j h", j=NT),
                                               ALU.mult, ALU.add).then_inc(dves, 1)
                for i in range(2, 8):
                    square(i)
                    if i == 5:
                        mod.store(dve, 0)
                mod.store(dve, 1)
                for i in range(8):
                    pair = conv[:, 2 * i:2 * i + 2, :].rearrange("p c t -> p (c t)")
                    dve.wait_ge(rsqrts, i + 1)
                    nc.vector.scalar_tensor_tensor(pair, pair, P ** -0.5 if i < 4 else 1.0, lnr[:, i, :],
                                                   ALU.mult, ALU.mult)
                dve.wait_ge(acts, 5)
                nc.vector.tensor_tensor(co["kbg"][:], co["kbg"][:], co["beta"][:], ALU.mult)
                mod.store(dve, 2)

            @block.tensor
            def _(pe):
                for i in range(8):
                    if i == 2:
                        pe.wait_ge(masks_in, 16)
                        pe.wait_ge(dves, 7)
                        gg = g[:].rearrange("p j h -> p (j h)")
                        for n, mask in enumerate(("upto", "chunk", "first_half", "second_half")):
                            at = (0, 32, 64, 80)[n]
                            last = nc.tensor.matmul(ps[:, 3, at:at + 16], mask_of(masks, mask), gg, start=True, stop=True)
                        last.then_inc(gsums, 1)
                    pe.wait_ge(squares, i + 1)
                    if i >= 2:
                        pe.wait_ge(logs, i - 1)
                    nc.tensor.matmul(ps[:, i % 2, :], core.ones[:], sq[:, i % 2, :], start=True, stop=True).then_inc(sums, 1)
                    for u in ((0, 1), (2,), (3,), (4, 5), (6,), (7,), (8, 9), (10, 11))[i]:
                        mod.multiply(pe, u)
                    if i in (3, 6):
                        mod.turn(pe, i // 3 - 1)
                mod.turn(pe, 2)


MASKS = ["upto", "chunk", "first_half", "second_half"] + [f"level{s}" for s in LEVELS]


def mask_of(masks, name):
    i = MASKS.index(name)
    return masks[:, i * P:(i + 1) * P]


def shape_constants():
    m, t = np.meshgrid(np.arange(P), np.arange(P), indexing="ij")
    same = m // CH == t // CH
    out = [m == t, same & (m <= t), same, m < CH, m >= CH]
    for s in LEVELS:
        out.append((m // (2 * s) == t // (2 * s)) & (t % (2 * s) >= s) & (m % (2 * s) < s))
    out.append(m + t == P - 1)
    return np.concatenate(out, axis=1).astype(np.float32)


def stage_gdn_tile(core, j, conv, masks, co, work, state):
    nc, ps = core.nc, core.ps
    kbg, kd, vb, qdT = work["kbg"], work["kd"], work["vb"], work["qdT"]
    aT, u, wT, vnew = work["aT"], work["u"], work["wT"], work["vnew"]
    tok = slice(j * P, (j + 1) * P)
    NL = len(LEVELS) - 1
    with Stage(core, f"gdntile{j}") as st:
        mod = Modulation(core, st, [(2 + j, 0, 4, 5), (2 + j, 1, 4, 5), (2 + j, 2, 6, 7)])
        both = lambda n: [st.sb(f"{n}{g}", [P, 4, P]) for g in range(2)]
        L, X, Pm, T, TT = both("L"), both("X"), both("Pm"), both("T"), both("TT")
        dg, db, E = Pm, T, TT
        pair = lambda n: [st.sem(f"{n}{g}") for g in range(2)]
        turned, tok_scaled, diags, spread, raws, raws_read = (st.sem(n) for n in ("turned", "tok_scaled", "diags", "spread", "raws", "raws_read"))
        exps, dd, lt, solved = st.sem("exps"), st.sem("decay_steps"), st.sem("lead"), st.sem("solved")
        x_ready, p_made, p_copied, tp_made, t_ready = (pair(n) for n in ("x_ready", "p_made", "p_copied", "tp_made", "t_ready"))
        uw_made, w_copied = st.sem("uw_made"), st.sem("w_copied")
        ws_made, v_ready, o_made, kv_made, o_copied, s_step = (st.sem(n) for n in ("ws_made", "v_ready", "o_made", "kv_made", "o_copied", "s_step"))
        flat = lambda a: a[:].rearrange("p h t -> p (h t)")
        four = lambda b: ps[:, b, :].rearrange("p (h t) -> p h t", h=4)
        over_t = lambda a: a.unsqueeze(2).broadcast_to([P, 4, P])
        over_h = lambda a: a.unsqueeze(1).broadcast_to([P, 4, P])
        K_BANK, V_BANK = (0, 6), (1, 7)
        P_BANK, TT_BANK, T_BANK = (7, 1), (6, 2), (0, 3)
        with st.block() as block:
            ring_in_stage(core, block, 12)

            @block.tensor
            def _(pe):
                for g in range(2):
                    for i in range(4):
                        h = 4 * g + i
                        nc.tensor.transpose(ps[:, K_BANK[g], i * P:(i + 1) * P], conv[:, 8 + h, tok], core.ident[:])
                        last = nc.tensor.transpose(ps[:, V_BANK[g], i * P:(i + 1) * P], conv[:, 16 + h, tok], core.ident[:])
                    last.then_inc(turned, 1)
                    if g:
                        pe.wait_ge(raws_read, 1)
                    for i in range(4):
                        h = 4 * g + i
                        nc.tensor.matmul(ps[:, 4, i * P:(i + 1) * P], conv[:, 8 + h, tok], conv[:, 8 + h, tok], start=True, stop=True)
                        last = nc.tensor.matmul(ps[:, 5, i * P:(i + 1) * P], conv[:, 8 + h, tok], conv[:, h, tok], start=True, stop=True)
                    last.then_inc(raws, 1)
                    pe.wait_ge(diags, 2 * (g + 1))
                    nc.tensor.matmul(ps[:, 2, :], core.ones[:], flat(dg[g]), start=True, stop=True)
                    nc.tensor.matmul(ps[:, 3, :], core.ones[:], flat(db[g]), start=True, stop=True).then_inc(spread, 1)
                pe.wait_ge(raws_read, 2)
                for g in range(2):
                    pe.wait_ge(t_ready[g], 1)
                    for i in range(4):
                        last = nc.tensor.transpose(ps[:, TT_BANK[g], i * P:(i + 1) * P], TT[g][:, i, :], core.ident[:])
                    last.then_inc(tp_made[g], 1)
                for n in range(NL):
                    for g in range(2):
                        pe.wait_ge(x_ready[g], n + 1)
                        pe.wait_ge(t_ready[g], 2 * (n + 1))
                        for i in range(4):
                            last = nc.tensor.matmul(ps[:, P_BANK[g], i * P:(i + 1) * P], X[g][:, i, :], T[g][:, i, :], start=True, stop=True)
                        last.then_inc(p_made[g], 1)
                    if n < 4:
                        mod.multiply(pe, 2 * n)
                    for g in range(2):
                        pe.wait_ge(p_copied[g], n + 1)
                        for i in range(4):
                            last = nc.tensor.matmul(ps[:, TT_BANK[g], i * P:(i + 1) * P], Pm[g][:, i, :], TT[g][:, i, :], start=True, stop=True)
                            if n < NL - 1:
                                last = nc.tensor.matmul(ps[:, T_BANK[g], i * P:(i + 1) * P], TT[g][:, i, :], Pm[g][:, i, :], start=True, stop=True)
                        last.then_inc(tp_made[g], 1)
                    if n < 4:
                        mod.multiply(pe, 2 * n + 1)
                    if n in (2, 4):
                        mod.turn(pe, n // 2 - 1)
                for g in range(2):
                    pe.wait_ge(t_ready[g], 2 * NL + 1)
                    for i in range(4):
                        h = 4 * g + i
                        nc.tensor.matmul(ps[:, P_BANK[g], i * P:(i + 1) * P], TT[g][:, i, :], vb[:, h, :], start=True, stop=True)
                        last = nc.tensor.matmul(ps[:, TT_BANK[g], i * P:(i + 1) * P], kbg[:, h, :], TT[g][:, i, :], start=True, stop=True)
                    last.then_inc(uw_made, 1)
                pe.wait_ge(w_copied, 2)
                pe.wait_ge(solved, 2)
                for half in range(2):
                    r = slice(half * CH, (half + 1) * CH)
                    if half:
                        pe.wait_ge(s_step, 2)
                    for h in range(GH):
                        last = nc.tensor.matmul(ps[r, h // 4, (h % 4) * P:(h % 4 + 1) * P], wT[:, h, r], state[:, h, :],
                                                start=True, stop=True)
                    last.then_inc(ws_made, 1)
                    mod.multiply(pe, 8 + 2 * half)
                    pe.wait_ge(v_ready, half + 1)
                    if half:
                        pe.wait_ge(o_copied, 1)
                    else:
                        pe.wait_ge(mod.stored, 2)
                    for h in range(GH):
                        o = ps[r, 2 + h // 4, (h % 4) * P:(h % 4 + 1) * P]
                        nc.tensor.matmul(o, qdT[:, h, r], state[:, h, :], start=True, stop=False)
                        last = nc.tensor.matmul(o, aT[:, h, r], vnew[:, h, :], start=False, stop=True)
                    last.then_inc(o_made, 1)
                    for h in range(GH):
                        last = nc.tensor.matmul(ps[:, 4 + h // 4, (h % 4) * P:(h % 4 + 1) * P], kd[r, h, :], vnew[r, h, :],
                                                start=True, stop=True)
                    last.then_inc(kv_made, 1)
                    mod.multiply(pe, 9 + 2 * half)
                mod.turn(pe, 2)

            @block.vector
            def _(dve):
                steps = 0

                def link(ins):
                    nonlocal steps
                    steps += 1
                    ins.then_inc(dd, 1)
                    dve.wait_ge(dd, steps)

                if j == 0:
                    nc.vector.memset(state[:], 0.0)
                    nc.vector.memset(vnew[:], 0.0)
                for g in range(2):
                    h4 = slice(4 * g, 4 * g + 4)
                    gc, beta = co["gc"][:, j, h4], co["beta"][:, j, h4]
                    nc.vector.tensor_tensor(dg[g][:], over_h(core.ident[:]), over_t(gc), ALU.mult).then_inc(diags, 1)
                    nc.vector.tensor_tensor(db[g][:], over_h(core.ident[:]), over_t(beta), ALU.mult).then_inc(diags, 1)
                for g in range(2):
                    h4 = slice(4 * g, 4 * g + 4)
                    gc, beta = co["gc"][:, j, h4], co["beta"][:, j, h4]
                    dve.wait_ge(turned, g + 1)
                    nc.vector.tensor_tensor(kbg[:, h4, :], four(K_BANK[g]), over_t(co["kbg"][:, j, h4]), ALU.mult)
                    nc.vector.tensor_tensor(kd[:, h4, :], four(K_BANK[g]), over_t(co["kd"][:, j, h4]), ALU.mult)
                    dve.wait_ge(spread, g + 1)
                    link(nc.vector.tensor_tensor(E[g][:], four(2), over_t(gc), ALU.subtract))
                    nc.vector.tensor_scalar(E[g][:], E[g][:], 0.0, None, ALU.min).then_inc(lt, 1)
                    nc.vector.tensor_tensor(vb[:, h4, :], four(V_BANK[g]), over_t(beta), ALU.mult).then_inc(tok_scaled, 1)
                    dve.wait_ge(exps, 2 * g + 1)
                    nc.vector.tensor_tensor(qdT[:, h4, :], conv[:, h4, tok], X[g][:], ALU.mult)
                    dve.wait_ge(exps, 2 * g + 2)
                    link(nc.vector.tensor_tensor(E[g][:], E[g][:], over_h(mask_of(masks, "upto")), ALU.mult))
                    dve.wait_ge(raws, g + 1)
                    nc.vector.tensor_tensor(aT[:, h4, :], four(5), E[g][:], ALU.mult)
                    link(nc.vector.tensor_tensor(L[g][:], E[g][:], four(3), ALU.mult))
                    nc.vector.tensor_tensor(L[g][:], four(4), L[g][:], ALU.mult).then_inc(raws_read, 1)
                    dve.wait_ge(raws_read, g + 1)
                    link(nc.vector.tensor_tensor(X[g][:], L[g][:], over_h(mask_of(masks, "level1")), ALU.mult))
                    nc.vector.tensor_tensor(TT[g][:], over_h(core.ident[:]), X[g][:], ALU.subtract).then_inc(t_ready[g], 1)
                for n in range(NL + 1):
                    for g in range(2):
                        dve.wait_ge(tp_made[g], n + 1)
                        if n == 0:
                            nc.vector.tensor_copy(T[g][:], four(TT_BANK[g])).then_inc(t_ready[g], 1)
                        else:
                            nc.vector.tensor_tensor(TT[g][:], TT[g][:], four(TT_BANK[g]), ALU.subtract).then_inc(t_ready[g], 1)
                            if n < NL:
                                nc.vector.tensor_tensor(T[g][:], T[g][:], four(T_BANK[g]), ALU.subtract).then_inc(t_ready[g], 1)
                        if n < NL:
                            nc.vector.tensor_tensor(X[g][:], L[g][:], over_h(mask_of(masks, f"level{LEVELS[n + 1]}")),
                                                    ALU.mult).then_inc(x_ready[g], 1)
                    if n == 3:
                        mod.store(dve, 0)
                mod.store(dve, 1)
                for g in range(2):
                    dve.wait_ge(uw_made, g + 1)
                    nc.vector.tensor_copy(u[:, 4 * g:4 * g + 4, :], four(P_BANK[g])).then_inc(solved, 1)
                dve.wait_ge(solved, 2)
                for half in range(2):
                    r = slice(half * CH, (half + 1) * CH)
                    dve.wait_ge(ws_made, half + 1)
                    nc.vector.tensor_tensor(vnew[r, :, :], u[r, :, :], ps[r, 0:2, :].rearrange("p b (h d) -> p (b h) d", h=4),
                                            ALU.subtract).then_inc(v_ready, 1)
                    dve.wait_ge(o_made, half + 1)
                    nc.vector.tensor_tensor(state[:], state[:], co["tot"][:, half, j, :].unsqueeze(2).broadcast_to([P, GH, P]),
                                            ALU.mult).then_inc(s_step, 1)
                    dve.wait_ge(kv_made, half + 1)
                    dve.wait_ge(s_step, 2 * half + 1)
                    nc.vector.tensor_tensor(state[:], state[:], ps[:, 4:6, :].rearrange("p b (h d) -> p (b h) d", h=4),
                                            ALU.add).then_inc(s_step, 1)
                mod.store(dve, 2)

            @block.scalar
            def _(act):
                for g in range(2):
                    act.wait_ge(lt, g + 1)
                    nc.scalar.activation(X[g][:], four(2), ACT.Exp).then_inc(exps, 1)
                    nc.scalar.activation(E[g][:], E[g][:], ACT.Exp).then_inc(exps, 1)
                for n in range(NL):
                    if n in (2, 4):
                        mod.copy(act, n // 2 - 1)
                    for g in range(2):
                        act.wait_ge(p_made[g], n + 1)
                        nc.scalar.activation(Pm[g][:], four(P_BANK[g]), ACT.Copy).then_inc(p_copied[g], 1)
                for g in range(2):
                    act.wait_ge(uw_made, g + 1)
                    nc.scalar.activation(wT[:, 4 * g:4 * g + 4, :], four(TT_BANK[g]), ACT.Copy).then_inc(w_copied, 1)
                for half in range(2):
                    r = slice(half * CH, (half + 1) * CH)
                    act.wait_ge(o_made, half + 1)
                    nc.scalar.activation(conv[r, 16:24, tok], ps[r, 2:4, :].rearrange("p b (h d) -> p (b h) d", h=4),
                                         ACT.Copy).then_inc(o_copied, 1)
                mod.copy(act, 2)


def stage_gdn_out(core, t, conv, zs):
    nc, ps = core.nc, core.ps
    with Stage(core, "gdnout") as st:
        sq, ssq, ms, rstd = st.sb("sq", [P, NT, GH, P]), *(st.sb(n, [P, NT * GH]) for n in ("ssq", "ms", "rstd"))
        y = st.sb("y", [P, NT, GH, P])
        dd, sums, act_sums, pools, act_scaled, turned, ready = (st.sem(n) for n in (
            "steps", "sums", "act_sums", "pools", "act_scaled", "turned", "ready"))
        o = [conv[:, 16:24, j * P:(j + 1) * P] for j in range(NT)]
        z = [zs[:, j, :].rearrange("p (h d) -> p h d", h=GH) for j in range(NT)]
        with st.block() as block:
            @block.vector
            def _(dve):
                nc.vector.tensor_tensor(sq[:, 0], o[0], o[0], ALU.mult).then_inc(dd, 1)
                dve.wait_ge(dd, 1)
                nc.vector.tensor_reduce(ssq[:, 0:GH], sq[:, 0], AX.X, ALU.add).then_inc(sums, 1)
                dve.wait_ge(pools, 2)
                nc.vector.tensor_tensor(y[:, 0], o[0], rstd[:, 0:GH].unsqueeze(2).broadcast_to([P, GH, P]), ALU.mult).then_inc(dd, 1)
                dve.wait_ge(dd, 2)
                nc.vector.tensor_tensor(y[:, 0], y[:, 0], z[0], ALU.mult).then_inc(ready, 1)
                dve.wait_ge(act_scaled, 1)
                nc.vector.tensor_tensor(y[:, 1], y[:, 1], z[1], ALU.mult).then_inc(ready, 1)
                for h in range(1, GH, 2):
                    dve.wait_ge(turned, h + 1)
                    nc.vector.tensor_copy(core.hT[:, h, 0:S], ps[:, h, 0:S])

            @block.gpsimd
            def _(pool):
                pool.wait_ge(sums, 1)
                pool.wait_ge(act_sums, 1)
                nc.gpsimd.tensor_scalar(ms[:], ssq[:], 1.0 / P, EPS, ALU.mult, ALU.add).then_inc(pools, 1)
                pool.wait_ge(pools, 1)
                nc.gpsimd.tensor_tensor(rstd[:], ms[:], core.half[:], ALU.pow).then_inc(pools, 1)

            @block.tensor
            def _(pe):
                for j in range(NT):
                    pe.wait_ge(ready, j + 1)
                    for h in range(GH):
                        done = nc.tensor.transpose(ps[:, h, j * P:(j + 1) * P], y[:, j, h, :], core.ident[:])
                        if j == NT - 1:
                            done.then_inc(turned, 1)

            @block.scalar
            def _(act):
                for h in range(GH):
                    last = nc.scalar.activation(sq[:, 1, h], o[1][:, h], ACT.Square, accum_out=ssq[:, GH + h:GH + h + 1])
                last.then_inc(act_sums, 1)
                act.wait_ge(pools, 2)
                for h in range(GH):
                    last = nc.scalar.activation(y[:, 1, h], o[1][:, h], ACT.Copy, scale=rstd[:, GH + h:GH + h + 1])
                last.then_inc(act_scaled, 1)
                for h in range(0, GH, 2):
                    act.wait_ge(turned, h + 1)
                    nc.scalar.activation(core.hT[:, h, 0:S], ps[:, h, 0:S], ACT.Copy)


def mixer_gdn(core, t, outer):
    with ExitStack() as stack:
        sb = lambda n, shape: stack.enter_context(core.nc.sbuf_tensor("gdn_" + n, shape, F32))
        zs = core.ctx_x
        conv, ab = sb("conv", [P, 24, S]), sb("ab", [P, NT, 16])
        stage_gdn_project(core, t, conv, zs, ab)
        masks = sb("masks", [P, len(MASKS) * P])
        co = {n: sb(n, [P, NT, GH]) for n in ("beta", "gc", "kbg", "kd")}
        co["eps"], co["tot"] = sb("eps", [P, 1]), sb("tot", [P, 2, NT, GH])
        stage_gdn_gates(core, t, conv, zs, ab, masks, co)
        with ExitStack() as inner:
            wb = lambda n: inner.enter_context(core.nc.sbuf_tensor("gdn_" + n, [P, GH, P], F32))
            work = {n: wb(n) for n in ("aT", "u", "wT", "vnew")}
            state = wb("state")
            free = core.hT[:].rearrange("p c t -> p (c t)")
            for i, n in enumerate(("kbg", "kd", "vb", "qdT")):
                work[n] = free[:, i * GH * P:(i + 1) * GH * P].rearrange("p (h d) -> p h d", h=GH)
            for j in range(NT):
                stage_gdn_tile(core, j, conv, masks, co, work, state)
        stage_gdn_out(core, t, conv, zs)


class Part:

    def __init__(self, c0, heads, step, dim, gain, rope=None):
        self.c0, self.heads, self.step, self.dim, self.gain, self.rope = c0, heads, step, dim, gain, rope

    def of(self, raw, tiles):
        base = self.c0 // self.step * self.step
        v = raw[:, tiles, base:base + self.heads * self.step].rearrange("p t (h d) -> p t h d", h=self.heads)
        return v[:, :, :, self.c0 - base:self.c0 - base + self.dim]


def stage_heads(core, name, lhs, tiles, units, plan, loads=(), before=None, late=()):
    nc, ps, ring = core.nc, core.ps, core.ring
    tiles_of = [s.get("tiles", tiles) for s in plan]
    width = max([s["width"] for s in plan if s["parts"]])
    normed = [i for i, s in enumerate(plan) if s["parts"]]
    rank = {s: n for n, s in enumerate(normed)}
    parts = [(s, part) for s in normed for part in plan[s]["parts"]]

    def places(s):
        at, out = 0, []
        for part in plan[s]["parts"]:
            out.append(slice(at, at + tiles_of[s] * part.heads))
            at = out[-1].stop
        return out
    most = max(places(s)[-1].stop for s in normed)
    with Stage(core, name) as st:
        raw = st.sb("raw", [P, 2, tiles, width])
        sq = st.sb("sq", [P, tiles, width])
        ssq, ms, rstd = (st.sb(n, [P, most]) for n in ("ssq", "ms", "rstd"))
        loaded, raw_copied, means, rstds, ready, turned, left, dd = (st.sem(n) for n in (
            "loaded", "raw_copied", "means", "rstds", "ready", "turned", "left", "steps"))
        half = st.sb("exponent", [P, most])
        filled, late_loaded = st.sem("filled"), st.sem("late_loaded")
        first = ring.take(units)
        assert units == len(plan)
        with st.block() as block:
            @block.sync
            def _(sp):
                for dst, src in loads:
                    sp.dma_start(dst, src).then_inc(loaded, 16)
                for dst, src in late:
                    sp.dma_start(dst, src).then_inc(late_loaded, 16)
                ring.load_ahead(sp, ring.taken + SLOTS)

            def bank(s, j):
                return 4 * (s % 2) + j

            @block.tensor
            def _(pe):
                def turn(s):
                    if not plan[s]["parts"]:
                        return
                    n = rank[s]
                    pe.wait_ge(ready, n + 1)
                    for i, (c0, c1, _) in enumerate(plan[s]["turns"]):
                        for j in range(tiles_of[s]):
                            src = (sq if plan[s].get("spread") else raw[:, n % 2])[:, j, c0:c1]
                            last = nc.tensor.transpose(ps[0:c1 - c0, bank(s, j), i * P:(i + 1) * P], src, core.ident[:])
                    last.then_inc(turned, 1)
                for s in range(len(plan)):
                    if s >= 2:
                        pe.wait_ge(left, s - 1)
                    project_strip(core, pe, lhs, tiles_of[s], first + s, 1, [bank(s, j) for j in range(tiles_of[s])])
                    if s >= 1:
                        turn(s - 1)
                turn(len(plan) - 1)

            @block.scalar
            def _(act):
                def finish(s):
                    n = tiles_of[s]
                    banks = ps[:, bank(s, 0):bank(s, 0) + n, :]
                    if plan[s]["parts"]:
                        act.wait_ge(turned, rank[s] + 1)
                        for i, (c0, c1, dest) in enumerate(plan[s]["turns"]):
                            last = nc.scalar.activation(dest.rearrange("p (j t) -> p j t", t=P),
                                                        banks[0:c1 - c0, :, i * P:(i + 1) * P], ACT.Copy)
                    else:
                        ring.wait_read(act, first + s)
                        for c0, c1, dest in plan[s]["values"]:
                            last = nc.scalar.activation(dest, banks[:, :, c0:c1], ACT.Copy)
                    last.then_inc(left, 1)
                for s in range(len(plan)):
                    if plan[s]["parts"]:
                        n, w = rank[s], plan[s]["width"]
                        ring.wait_read(act, first + s)
                        if n >= 2:
                            act.wait_ge(turned, n - 1)
                        for c0, c1, dest in plan[s]["values"]:
                            src = ps[:, bank(s, 0):bank(s, 0) + tiles_of[s], c0:c1]
                            if len(dest.shape) == 4:
                                src = src.rearrange("p j (h d) -> p j h d", h=dest.shape[2] * 2)[:, :, 1::2, :] if plan[s].get("odd") else src
                            nc.scalar.activation(dest, src, ACT.Copy)
                        nc.scalar.activation(raw[:, n % 2, 0:tiles_of[s], 0:w], ps[:, bank(s, 0):bank(s, 0) + tiles_of[s], 0:w],
                                             ACT.Copy).then_inc(raw_copied, 1)
                    if s >= 1:
                        finish(s - 1)
                finish(len(plan) - 1)
                if late:
                    act.wait_ge(late_loaded, 16 * len(late))

            @block.gpsimd
            def _(pool):
                nc.gpsimd.memset(half[:], -0.5).then_inc(filled, 1)
                pool.wait_ge(filled, 1)
                for n, s in enumerate(normed):
                    pool.wait_ge(means, n + 1)
                    m = places(s)[-1].stop
                    nc.gpsimd.tensor_tensor(rstd[:, 0:m], ms[:, 0:m], half[:, 0:m], ALU.pow).then_inc(rstds, 1)

            @block.vector
            def _(dve):
                steps = 0

                def link(ins):
                    nonlocal steps
                    steps += 1
                    ins.then_inc(dd, 1)
                    dve.wait_ge(dd, steps)

                if loads:
                    dve.wait_ge(loaded, 16 * len(loads))
                if before:
                    before(dve, link)
                spread_before = False
                for n, s in enumerate(normed):
                    T = tiles_of[s]
                    dve.wait_ge(raw_copied, n + 1)
                    r = raw[:, n % 2]
                    for i, (part, at) in enumerate(zip(plan[s]["parts"], places(s))):
                        v = part.of(r, slice(0, T))
                        if plan[s].get("odd"):
                            q = r[:, 0:T, :].rearrange("p t (h d) -> p t h d", h=part.heads)[:, :, :, part.dim:]
                        else:
                            assert not spread_before
                            c = part.c0 if part.heads == 1 else sum(p.heads * p.dim for p in plan[s]["parts"][:i])
                            q = sq[:, 0:T, c:c + part.heads * part.dim].rearrange("p t (h d) -> p t h d", h=part.heads)
                        link(nc.vector.tensor_tensor(q, v, v, ALU.mult))
                        link(nc.vector.tensor_reduce(ssq[:, at].rearrange("p (t h) -> p t h", t=T), q, AX.X, ALU.add))
                        mean = nc.vector.tensor_scalar(ms[:, at], ssq[:, at], 1.0 / part.dim, EPS, ALU.mult, ALU.add)
                    mean.then_inc(means, 1)
                    dve.wait_ge(rstds, n + 1)
                    for part, at in zip(plan[s]["parts"], places(s)):
                        v = part.of(r, slice(0, T))
                        by_part = rstd[:, at].rearrange("p (t h) -> p t h", t=T)
                        link(nc.vector.tensor_tensor(v, v, by_part.unsqueeze(3).broadcast_to([P, T, part.heads, part.dim]), ALU.mult))
                        link(nc.vector.tensor_tensor(v, v, part.gain.unsqueeze(1).unsqueeze(1).broadcast_to([P, T, part.heads, part.dim]), ALU.mult))
                        if part.rope:
                            for j in range(NT):
                                d4 = part.dim // 4
                                x = part.of(r, slice(j, j + 1))[:, 0].rearrange("p h (b a d) -> p h b a d", b=2, a=2)
                                o = sq[:, j, 0:part.heads * part.dim].rearrange("p (h b a d) -> p h b a d", h=part.heads, b=2, a=2)
                                m = part.heads * part.dim
                                o2 = (sq[:, 2 + j, 0:m] if tiles >= 4 else sq[:, j, m:2 * m]).rearrange(
                                    "p (h b a d) -> p h b a d", h=part.heads, b=2, a=2)
                                cos, sin = (part.rope[k][:, j].unsqueeze(1).broadcast_to([P, part.heads, 2, d4]) for k in range(2))
                                for a in range(2):
                                    nc.vector.tensor_tensor(o[:, :, :, a], x[:, :, :, a], cos, ALU.mult)
                                    link(nc.vector.tensor_tensor(o2[:, :, :, a], x[:, :, :, 1 - a], sin, ALU.mult))
                                nc.vector.tensor_tensor(x[:, :, :, 0], o[:, :, :, 0], o2[:, :, :, 0], ALU.subtract)
                                link(nc.vector.tensor_tensor(x[:, :, :, 1], o[:, :, :, 1], o2[:, :, :, 1], ALU.add))
                    if plan[s].get("spread"):
                        if spread_before:
                            dve.wait_ge(turned, n)
                        spread_before = True
                        plan[s]["spread"](link, r, sq)
                    if plan[s].get("keep"):
                        plan[s]["keep"](link, r)
                    nc.vector.engine_nop().then_inc(ready, 1)


def stage_attend(core, name, items, lam=None, loads=(), flip=None):
    nc, ps = core.nc, core.ps
    N = len(items)
    comps = len(items[0]["comps"])
    width = max(it["keys"] for it in items)
    with Stage(core, name) as st:
        deep = 3 if comps == 1 else 2
        E = st.sb("E", [P, deep, comps, width])
        Wt = st.sb("Wt", [P, 2, width]) if comps == 2 else None
        ET = st.sb("ET", [P, 2, width])
        nm, l, r = (st.sb(n, [P, 4, comps]) for n in ("nm", "l", "r"))
        scored, maxed, exped, weighted, turned, et_copied, summed, out_left, dd = (st.sem(n) for n in (
            "scored", "maxed", "exped", "weighted", "turned", "et_copied", "summed", "out_left", "steps"))
        loaded = st.sem("loaded")
        with st.block() as block:
            @block.sync
            def _(sp):
                for dst, src in loads:
                    sp.dma_start(dst, src).then_inc(loaded, 16)
                core.ring.load_ahead(sp, core.ring.taken + SLOTS)

            def stat(a, i, c):
                return a[:, i % 4, c:c + 1]

            def stats(i, c):
                s = items[i].get("sums")
                return (stat(nm, i, c), stat(l, i, c)) if s is None else s

            @block.tensor
            def _(pe):
                for i in range(N + 3):
                    if i < N:
                        if i >= 2:
                            pe.wait_ge(exped, comps * (i - 1))
                        for c, (q, k) in enumerate(items[i]["comps"]):
                            scores = ps[:, 2 * (i % 2) + c, 0:items[i]["keys"]]
                            if items[i].get("bias") is not None:
                                nc.tensor.matmul(scores, flip, items[i]["bias"], start=True, stop=False)
                            last = nc.tensor.matmul(scores, q, k, start=items[i].get("bias") is None, stop=True)
                        last.then_inc(scored, 1)
                    if 0 <= i - 2 < N:
                        m = i - 2
                        pe.wait_ge(weighted if comps == 2 else exped, m + 1)
                        if m >= 2:
                            pe.wait_ge(et_copied, m - 1)
                        for b in range(items[m]["keys"] // P):
                            src = (Wt[:, m % 2] if comps == 2 else E[:, m % deep, 0])[:, b * P:(b + 1) * P]
                            last = nc.tensor.transpose(ps[:, 4 + m % 2, b * P:(b + 1) * P], src, core.ident[:])
                        last.then_inc(turned, 1)
                    if 0 <= i - 3 < N:
                        m = i - 3
                        pe.wait_ge(et_copied, m + 1)
                        if m >= 2:
                            pe.wait_ge(out_left, m - 1)
                        blocks = items[m]["values"]
                        for b, v in enumerate(blocks):
                            last = nc.tensor.matmul(ps[:, 6 + m % 2, 0:v.shape[1]], ET[:, m % 2, b * P:(b + 1) * P], v,
                                                    start=(b == 0), stop=(b == len(blocks) - 1))
                        last.then_inc(summed, 1)

            @block.scalar
            def _(act):
                for i in range(N + 2):
                    if i < N:
                        w = items[i]["keys"]
                        act.wait_ge(maxed, i + 1)
                        if i >= deep:
                            act.wait_ge(weighted if comps == 2 else turned, i - deep + 1)
                        for c in range(comps):
                            src = ps[:, 2 * (i % 2) + c, 0:w]
                            neg, tot = stats(i, c)
                            nc.scalar.activation(E[:, i % deep, c, 0:w], src, ACT.Exp, bias=neg, accum_out=tot).then_inc(exped, 1)
                    if i >= 2:
                        m = i - 2
                        w = items[m]["keys"]
                        act.wait_ge(turned, m + 1)
                        if m >= 2:
                            act.wait_ge(summed, m - 1)
                        nc.scalar.activation(ET[:, m % 2, 0:w], ps[:, 4 + m % 2, 0:w], ACT.Copy).then_inc(et_copied, 1)
                if loads:
                    act.wait_ge(loaded, 16 * len(loads))

            @block.vector
            def _(dve):
                steps = 0

                def link(ins):
                    nonlocal steps
                    steps += 1
                    ins.then_inc(dd, 1)
                    dve.wait_ge(dd, steps)

                for i in range(N + 3):
                    if i < N:
                        w = items[i]["keys"]
                        dve.wait_ge(scored, i + 1)
                        for c in range(comps):
                            src = ps[:, 2 * (i % 2) + c, 0:w]
                            last = nc.vector.tensor_reduce(stats(i, c)[0], src, AX.X, ALU.max, negate=True)
                        last.then_inc(maxed, 1)
                    if comps == 2 and 0 <= i - 1 < N:
                        m = i - 1
                        w = items[m]["keys"]
                        dve.wait_ge(exped, 2 * (m + 1))
                        link(nc.vector.reciprocal(r[:, m % 4, :], l[:, m % 4, :]))
                        link(nc.vector.tensor_tensor(stat(r, m, 1), stat(r, m, 1), lam, ALU.mult))
                        if m >= 2:
                            dve.wait_ge(turned, m - 1)
                        link(nc.vector.tensor_scalar(Wt[:, m % 2, 0:w], E[:, m % deep, 0, 0:w], stat(r, m, 0), None, ALU.mult))
                        nc.vector.scalar_tensor_tensor(Wt[:, m % 2, 0:w], E[:, m % deep, 1, 0:w], stat(r, m, 1), Wt[:, m % 2, 0:w],
                                                       ALU.mult, ALU.add).then_inc(weighted, 1)
                    if 0 <= i - 3 < N:
                        m = i - 3
                        plain = comps == 2 or items[m].get("sums") is not None
                        if not plain:
                            link(nc.vector.reciprocal(stat(r, m, 0), stat(l, m, 0)))
                        dve.wait_ge(summed, m + 1)
                        src = ps[:, 6 + m % 2, 0:items[m]["out"].shape[1]]
                        if plain:
                            nc.vector.tensor_copy(items[m]["out"], src).then_inc(out_left, 1)
                        else:
                            nc.vector.tensor_scalar(items[m]["out"], src, stat(r, m, 0), None, ALU.mult).then_inc(out_left, 1)


def stage_turn(core, name, o, tiles, chunks):
    nc, ps = core.nc, core.ps
    with Stage(core, name) as st:
        turned = st.sem("turned")
        with st.block() as block:
            @block.tensor
            def _(pe):
                for c in range(chunks):
                    for j in range(tiles):
                        last = nc.tensor.transpose(ps[:, c, j * P:(j + 1) * P], o(j, c), core.ident[:])
                    last.then_inc(turned, 1)

            @block.scalar
            def _(act):
                for c in range(0, chunks, 2):
                    act.wait_ge(turned, c + 1)
                    nc.scalar.activation(core.hT[:, c, 0:tiles * P], ps[:, c, 0:tiles * P], ACT.Copy)

            @block.vector
            def _(dve):
                for c in range(1, chunks, 2):
                    dve.wait_ge(turned, c + 1)
                    nc.vector.tensor_copy(core.hT[:, c, 0:tiles * P], ps[:, c, 0:tiles * P])


GROUPS = ((128, 1), (512, 4), (2048, 16))
DH = 64
NG = len(GROUPS)
REL = 32
MASKED = -1e30


def bucket_of(dist):
    exact = REL // 2
    d = np.float32(max(dist, 1))
    scaled = np.float32(np.log(d / np.float32(exact))) / np.float32(math.log(2048 / exact))
    return dist if dist < exact else min(exact + int(np.float32(scaled) * np.float32(REL - exact)), REL - 1)


def bias_constants():
    out = np.zeros((REL + NG, 2 * S + NG * GH), np.float32)
    for i in range(2 * S):
        d = S - 1 - i
        if d >= 0:
            out[bucket_of(d), i] = 1
        for g, (window, dilation) in enumerate(GROUPS):
            out[REL + g, i] = not (0 <= d <= window and d % dilation == 0)
    for g in range(NG):
        out[REL + g, 2 * S + g * GH:2 * S + (g + 1) * GH] = MASKED
    return out


def stage_bias(core, t):
    nc, ps = core.nc, core.ps
    with Stage(core, "bias") as st:
        marks = st.sb("marks", [REL + NG, 2 * S])
        table = st.sb("table", [REL + NG, NG * GH])
        rows = st.sb("rows", [NG * GH, 2 * S])
        loaded, made, copied, kept = (st.sem(n) for n in ("loaded", "made", "copied", "kept"))
        with st.block() as block:
            @block.sync
            def _(sp):
                sp.dma_start(marks[:], t["marks"][:, 0:2 * S]).then_inc(loaded, 16)
                sp.dma_start(table[0:REL, :], t["rel_bias"]).then_inc(loaded, 16)
                sp.dma_start(table[REL:, :], t["marks"][REL:, 2 * S:]).then_inc(loaded, 16)
                sp.wait_ge(copied, 1)
                sp.dma_start(t["bias_rows"], rows[:]).then_inc(kept, 16)
                sp.wait_ge(kept, 16)

            @block.tensor
            def _(pe):
                pe.wait_ge(loaded, 48)
                nc.tensor.matmul(ps[0:NG * GH, 0, :], table[:], marks[:], start=True, stop=True).then_inc(made, 1)

            @block.scalar
            def _(act):
                act.wait_ge(made, 1)
                nc.scalar.activation(rows[:], ps[0:NG * GH, 0, :], ACT.Copy).then_inc(copied, 1)


def bias_view(t, j, n0, n1):
    rows = t["bias_rows"]
    return bass.AP(tensor=rows.tensor, offset=n0 * 2 * S + S - (j + 1) * P, ap=[[1, P], [2 * S, n1 - n0], [1, (j + 1) * P]])


def stage_merge_turn(core, o, nm, l):
    nc, ps = core.nc, core.ps
    chunks = GH * DH // P
    with Stage(core, "dswturn") as st:
        lse, w = st.sb("lse", [P, NT, NG, GH]), st.sb("w", [P, NT, NG, GH])
        top, tot = st.sb("top", [P, NT, GH]), st.sb("tot", [P, NT, GH])
        acts, dd, merged, turned = st.sem("acts"), st.sem("steps"), st.sem("merged"), st.sem("turned")
        over_g = lambda a: a[:].unsqueeze(2).broadcast_to([P, NT, NG, GH])
        by_head = lambda a: a[:].rearrange("p t g h -> p t h g")
        with st.block() as block:
            @block.scalar
            def _(act):
                nc.scalar.activation(lse[:], l, ACT.Ln).then_inc(acts, 1)
                act.wait_ge(dd, 3)
                nc.scalar.activation(w[:], lse[:], ACT.Exp).then_inc(acts, 1)
                for c in range(0, chunks, 2):
                    act.wait_ge(turned, c + 1)
                    nc.scalar.activation(core.hT[:, c, 0:S], ps[:, c, 0:S], ACT.Copy)

            @block.tensor
            def _(pe):
                for j in range(NT):
                    pe.wait_ge(merged, j + 1)
                    rows = o[:, j, 0].rearrange("p h d -> p (h d)")
                    for c in range(chunks):
                        done = nc.tensor.transpose(ps[:, c, j * P:(j + 1) * P], rows[:, c * P:(c + 1) * P], core.ident[:])
                        if j == NT - 1:
                            done.then_inc(turned, 1)

            @block.vector
            def _(dve):
                steps = 0

                def link(ins):
                    nonlocal steps
                    steps += 1
                    ins.then_inc(dd, 1)
                    dve.wait_ge(dd, steps)

                dve.wait_ge(acts, 1)
                link(nc.vector.tensor_tensor(lse[:], lse[:], nm, ALU.subtract))
                link(nc.vector.tensor_reduce(top[:], by_head(lse), AX.X, ALU.max))
                link(nc.vector.tensor_tensor(lse[:], lse[:], over_g(top), ALU.subtract))
                dve.wait_ge(acts, 2)
                link(nc.vector.tensor_reduce(tot[:], by_head(w), AX.X, ALU.add))
                link(nc.vector.tensor_tensor(lse[:], l, over_g(tot), ALU.mult))
                link(nc.vector.reciprocal(lse[:], lse[:]))
                link(nc.vector.tensor_tensor(w[:], w[:], lse[:], ALU.mult))
                for j in range(NT):
                    all_heads = o[:, j].rearrange("p g h d -> p (g h) d")
                    weights = w[:, j].rearrange("p g h -> p (g h)").unsqueeze(2).broadcast_to([P, NG * GH, DH])
                    link(nc.vector.tensor_tensor(all_heads, all_heads, weights, ALU.mult))
                    link(nc.vector.tensor_tensor(o[:, j, 0], o[:, j, 0], o[:, j, 1], ALU.add))
                    nc.vector.tensor_tensor(o[:, j, 0], o[:, j, 0], o[:, j, 2], ALU.add).then_inc(merged, 1)
                for c in range(1, chunks, 2):
                    dve.wait_ge(turned, c + 1)
                    nc.vector.tensor_copy(core.hT[:, c, 0:S], ps[:, c, 0:S])


def mixer_dsw(core, t):
    nc = core.nc
    with ExitStack() as stack:
        sb = lambda n, shape: stack.enter_context(nc.sbuf_tensor("dsw_" + n, shape, F32))
        stage_bias(core, t)
        qT, kT = sb("qT", [P, NG * GH // 2, S]), sb("kT", [P, NG * GH // 2, S])
        v = sb("v", [P, NT, NG, GH * DH])
        gains, flip = sb("gains", [P, 2, DH]), sb("flip", [P, P])
        loads = [(flip[:], t["const"][:, (1 + len(MASKS)) * P:(2 + len(MASKS)) * P]), (gains[:, 0, :], t["dsw_q_norm"].broadcast_to([P, DH])), (gains[:, 1, :], t["dsw_k_norm"].broadcast_to([P, DH]))]

        def scale_q(dve, link):
            link(nc.vector.tensor_scalar(gains[:, 0, :], gains[:, 0, :], DH ** -0.5, None, ALU.mult))

        plan = []
        for which in range(2):
            for g in range(NG):
                dest = (qT, kT)[which]
                plan.append(dict(width=STRIP, values=[], parts=[Part(0, GH, DH, DH, gains[:, which, :])],
                                 turns=[(i * P, (i + 1) * P, dest[:, 4 * g + i, :]) for i in range(4)]))
        for g in range(NG):
            plan.append(dict(width=STRIP, parts=[], values=[(0, STRIP, v[:, :, g, :])], turns=[]))
        heads = NG * GH
        bias0 = sb("bias0", [P, heads, P])
        bias1 = core.ctx_x[:].rearrange("p j d -> p (j d)").rearrange("p (n t) -> p n t", n=heads - 16)
        bias1_first = core.hT[:].rearrange("p c t -> p (c t)").rearrange("p (n t) -> p n t", n=16)
        bias = ([bias0[:, n, :] for n in range(heads)],
                [bias1_first[:, n, :] if n < 16 else bias1[:, n - 16, :] for n in range(heads)])
        stage_heads(core, "dswproj", lambda k, j: core.hT[:, k, j * P:(j + 1) * P], NT, 9, plan, loads, scale_q,
                    late=[(bias0[:], bias_view(t, 0, 0, heads)), (bias1, bias_view(t, 1, 16, heads))])
        nm, l = sb("nm", [P, NT, NG, GH]), sb("l", [P, NT, NG, GH])
        o = sb("o", [P, NT, NG, GH, DH])
        for j in range(NT):
            items = []
            for n in range(heads):
                g, h, r = n // GH, n % GH, slice(DH * (n % 2), DH * (n % 2 + 1))
                items.append(dict(
                    comps=[(qT[r, n // 2, j * P:(j + 1) * P], kT[r, n // 2, 0:(j + 1) * P])], keys=(j + 1) * P,
                    values=[v[:, b, g, h * DH:(h + 1) * DH] for b in range(j + 1)], bias=bias[j][n],
                    out=o[:, j, g, h, :], sums=(nm[:, j, g, h:h + 1], l[:, j, g, h:h + 1])))
            stage_attend(core, f"dswatt{j}", items, flip=flip[:],
                         loads=[(bias1_first, bias_view(t, 1, 0, 16))] if j == 0 else ())
        stage_merge_turn(core, o, nm[:], l[:])


def rope_constants(dim):
    token = np.arange(S)
    half = dim // 2
    freqs = (np.float32(10000.0) ** (-np.arange(0, half, 2, dtype=np.float32) / np.float32(half))).astype(np.float32)
    place = np.stack([token // 64, token % 64], axis=1).astype(np.float32)
    ang = (place[:, :, None] * freqs).astype(np.float32)
    both = np.stack([np.cos(ang), np.sin(ang)]).astype(np.float32).reshape(2, NT, P, -1)
    return np.ascontiguousarray(both.transpose(2, 0, 1, 3)).reshape(P, -1)


def rope_view(tile, dim):
    v = tile.rearrange("p (k j b d) -> p k j b d", k=2, j=NT, b=2)
    return [v[:, k] for k in range(2)]


def stage_lambda(core, t, lam, init):
    nc = core.nc
    with Stage(core, "lambda") as st:
        vec, prod, tot = st.sb("vec", [P, 4, DH]), st.sb("prod", [P, 2, DH]), st.sb("tot", [P, 2])
        loaded, dd, acts = st.sem("loaded"), st.sem("steps"), st.sem("acts")
        with st.block() as block:
            @block.sync
            def _(sp):
                sp.dma_start(vec[:].rearrange("p a d -> p (a d)"),
                             t["diff_lambda_2"].rearrange("n a d -> n (a d)").broadcast_to([P, 4 * DH])).then_inc(loaded, 16)

            @block.scalar
            def _(act):
                act.wait_ge(dd, 2)
                nc.scalar.activation(tot[:], tot[:], ACT.Exp).then_inc(acts, 1)

            @block.vector
            def _(dve):
                steps = 0

                def link(ins):
                    nonlocal steps
                    steps += 1
                    ins.then_inc(dd, 1)
                    dve.wait_ge(dd, steps)

                dve.wait_ge(loaded, 16)
                link(nc.vector.tensor_tensor(prod[:], vec[:, 0::2, :], vec[:, 1::2, :], ALU.mult))
                link(nc.vector.tensor_reduce(tot[:], prod[:], AX.X, ALU.add))
                dve.wait_ge(acts, 1)
                link(nc.vector.tensor_tensor(lam[:], tot[:, 1:2], tot[:, 0:1], ALU.subtract))
                link(nc.vector.tensor_scalar(lam[:], lam[:], -init, None, ALU.add))


def stage_even_turn(core, o, gain_src, factor):
    nc, ps = core.nc, core.ps
    heads = 4
    n = NT * heads
    with Stage(core, "eventurn") as st:
        gain, sq = st.sb("gain", [P, 1]), st.sb("sq", [P, T2, heads, P])
        ssq, ms, rstd = (st.sb(name, [P, 2 * n]) for name in ("ssq", "ms", "rstd"))
        loaded, dd, sums, act_sums, pools, gains, scaled, act_scaled, plain, turned = (st.sem(name) for name in (
            "loaded", "steps", "sums", "act_sums", "pools", "gains", "scaled", "act_scaled", "plain", "turned"))
        a = o[:, :, 0:STRIP].rearrange("p t (h d) -> p t h d", h=heads)
        with st.block() as block:
            @block.sync
            def _(sp):
                sp.dma_start(gain[:], gain_src.rearrange("n d -> d n")).then_inc(loaded, 16)

            @block.tensor
            def _(pe):
                for c in range(heads, KC):
                    for j in range(T2):
                        last = nc.tensor.transpose(ps[:, c, j * P:(j + 1) * P], o[:, j, c * P:(c + 1) * P], core.ident[:])
                    last.then_inc(plain, 1)
                for j in range(T2):
                    if j in (0, NT):
                        pe.wait_ge(scaled if j == 0 else act_scaled, 1)
                    for c in range(heads):
                        done = nc.tensor.transpose(ps[:, c, j * P:(j + 1) * P], a[:, j, c], core.ident[:])
                        if j == T2 - 1:
                            done.then_inc(turned, 1)

            @block.vector
            def _(dve):
                v = a[:, 0:NT]
                by_head = lambda s: s[:, 0:n].rearrange("p (t h) -> p t h", t=NT)
                nc.vector.tensor_tensor(sq[:, 0:NT], v, v, ALU.mult).then_inc(dd, 1)
                dve.wait_ge(dd, 1)
                nc.vector.tensor_reduce(by_head(ssq), sq[:, 0:NT], AX.X, ALU.add).then_inc(sums, 1)
                dve.wait_ge(loaded, 16)
                nc.vector.tensor_scalar(gain[:], gain[:], factor, None, ALU.mult).then_inc(gains, 1)
                dve.wait_ge(pools, 2)
                nc.vector.tensor_tensor(v, v, by_head(rstd).unsqueeze(3).broadcast_to([P, NT, heads, P]), ALU.mult).then_inc(scaled, 1)
                for c in range(heads, KC):
                    dve.wait_ge(plain, c - heads + 1)
                    nc.vector.tensor_copy(core.hT[:, c, :], ps[:, c, :])
                dve.wait_ge(gains, 1)
                for c in range(1, heads, 2):
                    dve.wait_ge(turned, c + 1)
                    nc.vector.tensor_scalar(core.hT[:, c, :], ps[:, c, :], gain[:], None, ALU.mult)

            @block.scalar
            def _(act):
                for i in range(n):
                    last = nc.scalar.activation(sq[:, NT + i // heads, i % heads], a[:, NT + i // heads, i % heads], ACT.Square,
                                                accum_out=ssq[:, n + i:n + i + 1])
                last.then_inc(act_sums, 1)
                act.wait_ge(pools, 2)
                for i in range(n):
                    v = a[:, NT + i // heads, i % heads]
                    last = nc.scalar.activation(v, v, ACT.Copy, scale=rstd[:, n + i:n + i + 1])
                last.then_inc(act_scaled, 1)
                act.wait_ge(gains, 1)
                for c in range(0, heads, 2):
                    act.wait_ge(turned, c + 1)
                    nc.scalar.activation(core.hT[:, c, :], ps[:, c, :], ACT.Copy, scale=gain[:, 0:1])

            @block.gpsimd
            def _(pool):
                pool.wait_ge(sums, 1)
                pool.wait_ge(act_sums, 1)
                nc.gpsimd.tensor_scalar(ms[:], ssq[:], 1.0 / P, EPS, ALU.mult, ALU.add).then_inc(pools, 1)
                pool.wait_ge(pools, 1)
                nc.gpsimd.tensor_tensor(rstd[:], ms[:], core.half[:, 0:2 * n], ALU.pow).then_inc(pools, 1)


T2 = 2 * NT
LAM_INIT = 0.8 - 0.6 * math.exp(-0.3 * 0)


def mixer_even(core, t):
    nc = core.nc
    with ExitStack() as stack:
        sb = lambda n, shape: stack.enter_context(nc.sbuf_tensor("even_" + n, shape, F32))
        qa, ka, qb = (sb(n, [P, 4, T2 * P]) for n in ("qaT", "kaT", "qbT"))
        kb = sb("kbT", [P, 2, T2 * P])
        va, vb = sb("va", [P, T2, STRIP]), sb("vb", [P, T2, 2 * DH])
        gains, rope, lam = sb("gains", [P, 4, DH]), sb("rope", [P, 4 * DH // 2]), sb("lam", [P, 1])
        loads = [(gains[:, 0:2, :].rearrange("p a d -> p (a d)"), t["a_qk_norm_2"].rearrange("n a d -> n (a d)").broadcast_to([P, 2 * DH])),
                 (gains[:, 2:4, :].rearrange("p a d -> p (a d)"), t["b_qk_norm_2"].rearrange("n a d -> n (a d)").broadcast_to([P, 2 * DH])),
                 (rope[:], t["rope_even"])]
        turn = rope_view(rope[:], DH)

        def scale_q(dve, link):
            for i in (0, 2):
                link(nc.vector.tensor_scalar(gains[:, i, :], gains[:, i, :], DH ** -0.5, None, ALU.mult))

        def twice(link, r, other):
            for kv in range(2):
                for to in range(2):
                    link(nc.vector.tensor_copy(other[:, 0:T2, (2 * kv + to) * DH:(2 * kv + to + 1) * DH],
                                               r[:, 0:T2, kv * DH:(kv + 1) * DH]))

        def full(gain, dest):
            return dict(width=STRIP, values=[], parts=[Part(0, 8, DH, DH, gains[:, gain, :], turn)],
                        turns=[(i * P, (i + 1) * P, dest[:, i, :]) for i in range(4)])
        plan = [full(0, qa), full(1, ka), dict(width=STRIP, parts=[], values=[(0, STRIP, va[:])], turns=[]), full(2, qb),
                dict(width=2 * P, values=[(P, 2 * P, vb[:])], parts=[Part(0, 2, DH, DH, gains[:, 3, :], turn)], spread=twice,
                     turns=[(0, P, kb[:, 0, :]), (P, 2 * P, kb[:, 1, :])])]
        stage_heads(core, "evenproj", lambda k, j: core.hT[:, k, j * P:(j + 1) * P], T2, 5, plan, loads, scale_q)
        stage_lambda(core, t, lam, LAM_INIT)
        with nc.sbuf_tensor("even_o", [P, T2, D], F32) as o:
            a_items, b_items = [], []
            for j in range(T2):
                blocks = range(0, T2) if j < NT else range(NT, T2)
                keys = slice(blocks[0] * P, T2 * P)
                tok = slice(j * P, (j + 1) * P)
                for h in range(4):
                    a_items.append(dict(comps=[(qa[c * DH:(c + 1) * DH, h, tok], ka[c * DH:(c + 1) * DH, h, keys]) for c in range(2)],
                                        keys=len(blocks) * P, values=[va[:, b, h * P:(h + 1) * P] for b in blocks],
                                        out=o[:, j, h * P:(h + 1) * P]))
                for h in range(8):
                    r = slice(h % 2 * DH, (h % 2 + 1) * DH)
                    b_items.append(dict(comps=[(qb[r, h // 2, tok], kb[r, h // 4, keys])], keys=len(blocks) * P,
                                        values=[vb[:, b, h // 4 * DH:(h // 4 + 1) * DH] for b in blocks],
                                        out=o[:, j, STRIP + h * DH:STRIP + (h + 1) * DH]))
            stage_attend(core, "diffatt", a_items, lam=lam[:])
            stage_attend(core, "gqatt", b_items)
            stage_even_turn(core, o, t["a_subln_2"], 1.0 - LAM_INIT)


MLA_HEADS, NOPE, ROPE = 16, 64, 32
QK = NOPE + ROPE


def mixer_odd(core, t):
    nc = core.nc
    with ExitStack() as stack:
        sb = lambda n, shape: stack.enter_context(nc.sbuf_tensor("odd_" + n, shape, F32))
        kr, small, rope = sb("kr", [P, T2, ROPE]), sb("small", [P, 2 * QK]), sb("rope", [P, 4 * ROPE // 2])
        turn = rope_view(rope[:], ROPE)
        qT = core.hT[:].rearrange("p c t -> p (c t)").rearrange("p (h t) -> p h t", h=MLA_HEADS)
        o = core.ctx_x
        cT = core.ctx_x[:].rearrange("p j d -> p (j d)")[:, 0:3 * T2 * P].rearrange("p (c t) -> p c t", c=3)
        with nc.sbuf_tensor("odd_gains", [P, 3 * P], F32) as gains:
            def keep(link, r):
                link(nc.vector.tensor_copy(kr[:], r[:, :, 3 * P:3 * P + ROPE]))
            loads = [(gains[:, 0:2 * P], t["mla_q_norm_2"].broadcast_to([P, 2 * P])),
                     (gains[:, 2 * P:], t["mla_kv_norm_2"].broadcast_to([P, P])),
                     (small[:], t["mla_qk_norm_2"].rearrange("n a d -> n (a d)").broadcast_to([P, 2 * QK])), (rope[:], t["rope_odd"])]
            plan = [dict(width=3 * P + ROPE, values=[], keep=keep,
                         parts=[Part(0, 1, 2 * P, 2 * P, gains[:, 0:2 * P]), Part(2 * P, 1, P, P, gains[:, 2 * P:]),
                                Part(3 * P, 1, ROPE, ROPE, small[:, QK + NOPE:], turn)],
                         turns=[(i * P, (i + 1) * P, cT[:, i, :]) for i in range(3)])]
            stage_heads(core, "oddproj", lambda k, j: core.hT[:, k, j * P:(j + 1) * P], T2, 1, plan, loads)

        def scale_q(dve, link):
            link(nc.vector.tensor_scalar(small[:, 0:QK], small[:, 0:QK], QK ** -0.5, None, ALU.mult))
        plan = [dict(width=4 * QK, values=[], parts=[Part(0, 4, QK, NOPE, small[:, 0:NOPE]), Part(NOPE, 4, QK, ROPE, small[:, NOPE:QK], turn)],
                     turns=[(i * QK, (i + 1) * QK, qT[0:QK, 4 * n + i, :]) for i in range(4)]) for n in range(4)]
        stage_heads(core, "oddq", lambda k, j: cT[:, k, j * P:(j + 1) * P], NT, 4, plan, before=scale_q)

        kT, v = sb("kT", [P, MLA_HEADS, T2 * P]), sb("v", [P, T2, MLA_HEADS, NOPE])

        def join(link, r, other):
            to = other[:, 0:T2, 0:4 * QK].rearrange("p t (h d) -> p t h d", h=4)
            link(nc.vector.tensor_copy(to[:, :, :, 0:NOPE], r[:, 0:T2, :].rearrange("p t (h d) -> p t h d", h=4)[:, :, :, 0:NOPE]))
            link(nc.vector.tensor_copy(to[:, :, :, NOPE:], kr[:].unsqueeze(2).broadcast_to([P, T2, 4, ROPE])))
        plan = [dict(width=STRIP, odd=True, values=[(0, STRIP, v[:, :, 4 * n:4 * n + 4, :])], spread=join,
                     parts=[Part(0, 4, P, NOPE, small[:, QK:QK + NOPE])],
                     turns=[(i * QK, (i + 1) * QK, kT[0:QK, 4 * n + i, :]) for i in range(4)]) for n in range(4)]
        stage_heads(core, "oddkv", lambda k, j: cT[:, 2, j * P:(j + 1) * P], T2, 4, plan)
        items = [dict(comps=[(qT[0:QK, h, j * P:(j + 1) * P], kT[0:QK, h, :])], keys=T2 * P,
                      values=[v[:, b, h, :] for b in range(T2)], out=o[:, j, h * NOPE:(h + 1) * NOPE])
                 for j in range(NT) for h in range(MLA_HEADS)]
        stage_attend(core, "mlatt", items)
        stage_turn(core, "oddturn", lambda j, c: o[:, j, c * P:(c + 1) * P], NT, KC)


def route_constants():
    p, s = np.arange(P)[:, None], np.arange(S)[None, :]
    least = -float(np.finfo(np.float32).tiny)
    bounds = [np.where(s < p + P * j, least, 0.0) for j in range(NT)]
    return np.concatenate(bounds + [np.broadcast_to(np.arange(CAP), (P, CAP))], axis=1).astype(np.float32)


def stage_route(core, t, name, streams, aff, rows, sel, picked):
    nc, ps, ring = core.nc, core.ps, core.ring
    T = NT * streams
    with Stage(core, name) as st:
        consts = st.sb("consts", [P, 2 * S + CAP])
        nm, l = st.sb("nm", [P, T]), st.sb("l", [P, T])
        higher = st.sb("higher", [P, T, EXPERTS])
        affT = st.sb("affT", [EXPERTS, T * P])
        junk = st.sb("junk", [P, 4, S])
        loaded, dd, exps, affs, turned, copied, stored, spread = (st.sem(n) for n in (
            "loaded", "steps", "exps", "affs", "turned", "copied", "stored", "spread"))
        counted = st.sem("counted")
        first = ring.take(1)
        with st.block() as block:
            @block.sync
            def _(sp):
                sp.dma_start(consts[:], t["route"]).then_inc(loaded, 16)
                ring.load_ahead(sp, ring.taken + SLOTS)

            @block.tensor
            def _(pe):
                project_strip(core, pe, lambda k, j: core.hT[:, k, j * P:(j + 1) * P], T, first, 1, list(range(T)))
                pe.wait_ge(affs, T)
                for j in range(T):
                    last = nc.tensor.transpose(ps[0:EXPERTS, 4, j * P:(j + 1) * P], aff[:, j, :], core.ident[:])
                last.then_inc(turned, 1)

            @block.scalar
            def _(act):
                act.wait_ge(dd, T)
                for j in range(T):
                    nc.scalar.activation(aff[:, j, :], ps[:, j, 0:EXPERTS], ACT.Exp, bias=nm[:, j:j + 1],
                                         accum_out=l[:, j:j + 1]).then_inc(exps, 1)
                act.wait_ge(turned, 1)
                nc.scalar.activation(affT[:], ps[0:EXPERTS, 4, 0:T * P], ACT.Copy).then_inc(copied, 1)
                act.wait_ge(copied, 1)
                act.dma_start(t["affinity"][:, 0:T * P], affT[:]).then_inc(stored, 16)
                act.wait_ge(stored, 16)
                for i in range(streams):
                    act.dma_start(rows[:, :, i * S:(i + 1) * S],
                                  t["affinity"][:, i * S:(i + 1) * S].unsqueeze(0).broadcast_to([P, EXPERTS, S])).then_inc(spread, 16)
                    act.wait_ge(spread, 16 * (i + 1))

            @block.vector
            def _(dve):
                steps = 0

                def link(ins):
                    nonlocal steps
                    steps += 1
                    ins.then_inc(dd, 1)
                    dve.wait_ge(dd, steps)

                ring.wait_read(dve, first)
                for j in range(T):
                    link(nc.vector.tensor_reduce(nm[:, j:j + 1], ps[:, j, 0:EXPERTS], AX.X, ALU.max, negate=True))
                dve.wait_ge(exps, T)
                link(nc.vector.reciprocal(l[:], l[:]))
                for j in range(T):
                    nc.vector.tensor_scalar(aff[:, j, :], aff[:, j, :], l[:, j:j + 1], None, ALU.mult).then_inc(affs, 1)
                dve.wait_ge(affs, T)
                dve.wait_ge(loaded, 16)
                for j in range(T):
                    if j % NT == 0:
                        dve.wait_ge(spread, 16 * (j // NT + 1))
                    for e in range(EXPERTS):
                        n = j * EXPERTS + e
                        if n >= 4:
                            dve.wait_ge(counted, n - 3)
                        nc.vector.scalar_tensor_tensor(junk[:, n % 4, :], rows[:, e, j // NT * S:(j // NT + 1) * S],
                                                       aff[:, j, e:e + 1], consts[:, j % NT * S:(j % NT + 1) * S],
                                                       ALU.subtract, ALU.is_gt, accum_out=higher[:, j, e:e + 1]).then_inc(counted, 1)
                dve.wait_ge(counted, T * EXPERTS)
                for j in range(T):
                    s = sel[:, j, :].rearrange("p (e r) -> p e r", e=EXPERTS)
                    ranks = consts[:, 2 * S:].unsqueeze(1).broadcast_to([P, EXPERTS, CAP])
                    wide = lambda a: a[:, j, :].unsqueeze(2).broadcast_to([P, EXPERTS, CAP])
                    link(nc.vector.tensor_tensor(s, ranks, wide(higher), ALU.is_equal))
                    nc.vector.tensor_tensor(picked[:, j, :].rearrange("p (e r) -> p e r", e=EXPERTS), s, wide(aff), ALU.mult)


def stage_gather(core, name, s, xn, sel, picked, xsT, pickedT, streams):
    nc, ps = core.nc, core.ps
    with Stage(core, name) as st:
        scale = st.sb("scale", [P, 2, KC])
        scales, gathered, act_left, dve_left, turned, turned_left = (st.sem(n) for n in (
            "scales", "gathered", "act_left", "dve_left", "turned", "turned_left"))
        with st.block() as block:
            def dest(c, i):
                return xsT[:, c, :, CAP * i:CAP * (i + 1)]

            def src(c):
                return ps[:, c, :].rearrange("p (e r) -> p e r", e=EXPERTS)

            @block.tensor
            def _(pe):
                for i in range(streams):
                    for c in range(KC):
                        if i:
                            pe.wait_ge((act_left, dve_left)[c % 2], KC // 2 * (i - 1) + c // 2 + 1)
                        for j in range(NT):
                            last = nc.tensor.matmul(ps[:, c, :], xn[:, NT * i + j, c * P:(c + 1) * P], sel[:, NT * i + j, :],
                                                    start=(j == 0), stop=(j == NT - 1))
                        last.then_inc(gathered, 1)
                for q in range(4):
                    pe.wait_ge((act_left, dve_left)[q % 2], KC // 2 * (streams - 1) + q // 2 + 1)
                    for j in range(NT * streams):
                        last = nc.tensor.transpose(ps[:, q, j * P:(j + 1) * P], picked[:, j, q * P:(q + 1) * P], core.ident[:])
                    last.then_inc(turned, 1)

            @block.scalar
            def _(act):
                act.wait_ge(scales, 2 * streams)
                for i in range(streams):
                    for c in range(0, KC, 2):
                        act.wait_ge(gathered, KC * i + c + 1)
                        nc.scalar.activation(dest(c, i), src(c), ACT.Identity, bias=core.mod(s, 3, i)[:, c:c + 1],
                                             scale=scale[:, i, c:c + 1]).then_inc(act_left, 1)
                for q in range(4):
                    act.wait_ge(turned, q + 1)
                    nc.scalar.activation(pickedT[:, q, 0:NT * streams * P], ps[:, q, 0:NT * streams * P], ACT.Copy)

            @block.vector
            def _(dve):
                for i in range(streams):
                    nc.vector.tensor_scalar(scale[:, i, :], core.mod(s, 4, i), 1.0, None, ALU.add).then_inc(scales, 1)
                    dve.wait_ge(scales, 2 * i + 1)
                    nc.vector.tensor_tensor(scale[:, i, :], scale[:, i, :], core.gain(1, s), ALU.mult).then_inc(scales, 1)
                dve.wait_ge(scales, 2 * streams)
                for i in range(streams):
                    for c in range(1, KC, 2):
                        dve.wait_ge(gathered, KC * i + c + 1)
                        nc.vector.tensor_scalar(dest(c, i), src(c), scale[:, i, c:c + 1], core.mod(s, 3, i)[:, c:c + 1],
                                                ALU.mult, ALU.add).then_inc(dve_left, 1)


HALF_K = KC // 2


def expert_unit(t, layer, e, u):
    w = t[("w_exp_gate_2", "w_exp_up_2", "w_exp_down_2")[u // 2]]
    return w[layer, e, u % 2 * HALF_K * P:(u % 2 + 1) * HALF_K * P, :].rearrange("(k p) n -> p k n", p=P)


def expert_units(t, layer):
    return [(expert_unit(t, layer, e, u), HALF_K, D) for e in range(EXPERTS) for u in range(6)]


def stage_experts(core, t, name, layer, streams, xsT, ys):
    nc, ps, ring = core.nc, core.ps, core.ring
    M = CAP * streams
    G = P // M
    W = D // G
    WC = W // P
    spare = core.hT[:].rearrange("p c t -> p (c t)")[:, 4 * STRIP:]
    xs = spare[:, 0:2 * KC * M].rearrange("p (b c m) -> p b c m", b=2, c=KC)
    a = spare[:, 1024:1536]
    actT = spare[:, 1536:1536 + WC * P].rearrange("p (w m) -> p w m", w=WC)
    with Stage(core, name) as st:
        sg = st.sb("sg", [P, W])
        xs_ready, silus, a_ready, turned, act_ready, y_act, y_dve = (st.sem(n) for n in (
            "xs_ready", "silus", "a_ready", "turned", "act_ready", "y_act", "y_dve"))
        first = ring.take(6 * EXPERTS)
        slot = [(first + u) % SLOTS for u in range(6)]
        lap = [(first + u) // SLOTS for u in range(6)]

        with st.block() as block:
            @block.sync
            def _(sp):
                def load(e, u):
                    sp.wait_ge(ring.read[slot[u]], e + lap[u])
                    sp.dma_start(ring.tile[:, slot[u], :].rearrange("p (k n) -> p k n", k=HALF_K),
                                 expert_unit(t, layer, e, u)).then_inc(ring.full[slot[u]], 16)
                ring.load_ahead(sp, first + 6)
                with sp.Fori(0, 3) as i:
                    for v in range(4):
                        for u in range(6):
                            load(i * 4 + (v + 1), u)
                for e in range(13, EXPERTS):
                    for u in range(6):
                        load(e, u)
                ring.loaded = first + 6 * EXPERTS
                ring.load_ahead(sp, ring.taken + SLOTS)

            @block.tensor
            def _(pe):
                def unit(i, v, u):
                    pe.wait_ge(ring.full[slot[u]], i * 64 + 16 * (lap[u] + v + 1))
                    return ring.tile[:, slot[u], :].rearrange("p (k n) -> p k n", k=HALF_K)

                def product(i, v, m, bank, lhs):
                    for u in range(2 * m, 2 * m + 2):
                        w = unit(i, v, u)
                        for k in range(HALF_K):
                            f = u % 2 * HALF_K + k
                            for g in range(G):
                                last = nc.tensor.matmul(ps[g * M:(g + 1) * M, bank, 0:W], lhs(f), w[:, k, g * W:(g + 1) * W],
                                                        start=(f == 0), stop=(f == KC - 1), skip_group_check=True)
                        last.then_inc(ring.read[slot[u]], 1)

                with pe.Fori(0, 4) as i:
                    for v in range(4):
                        pe.wait_ge(xs_ready, i * 4 + (v + 1))
                        x = lambda f: xs[:, v % 2, f, :]
                        product(i, v, 0, v % 2, x)
                        product(i, v, 1, 2 + v % 2, x)
                        pe.wait_ge(a_ready, i * 4 + (v + 1))
                        for w in range(WC):
                            last = nc.tensor.transpose(ps[:, 4 + v % 2, w * P:(w + 1) * P], a[:, w * P:(w + 1) * P], core.ident[:])
                        last.then_inc(turned, 1)
                        pe.wait_ge(act_ready, i * 4 + (v + 1))
                        pe.wait_ge(y_act, i * 4 + (v + 1))
                        pe.wait_ge(y_dve, i * 4 + (v + 1))
                        product(i, v, 2, 6, lambda f: actT[:, f % WC, f // WC * M:(f // WC + 1) * M])

            def y_copies(i, v, engine):
                out = []
                for n in range(4):
                    g, stream = n // streams, n % streams
                    if n % 2 == engine:
                        out.append((ys[CAP * v:CAP * (v + 1), i, stream, g * W:(g + 1) * W],
                                    ps[n * CAP:(n + 1) * CAP, 6, 0:W]))
                return out

            @block.scalar
            def _(act):
                act.nop().then_inc(y_act, 1)
                with act.Fori(0, 4) as i:
                    for v in range(4):
                        act.wait_ge(ring.read[slot[1]], i * 4 + (lap[1] + v + 1))
                        nc.scalar.activation(sg[:], ps[:, v % 2, 0:W], ACT.Silu).then_inc(silus, 1)
                        act.wait_ge(turned, i * 4 + (v + 1))
                        nc.scalar.activation(actT, ps[:, 4 + v % 2, 0:W].rearrange("p (w m) -> p w m", w=WC), ACT.Copy).then_inc(act_ready, 1)
                        act.wait_ge(ring.read[slot[5]], i * 4 + (lap[5] + v + 1))
                        for dst, src in y_copies(i, v, 0):
                            last = nc.scalar.activation(dst, src, ACT.Copy)
                        last.then_inc(y_act, 1)

            @block.vector
            def _(dve):
                dve.nop().then_inc(y_dve, 1)
                with dve.Fori(0, 4) as i:
                    for v in range(4):
                        nc.vector.tensor_copy(xs[:, v % 2, :, :], xsT[:, :, i * 4 + v, :]).then_inc(xs_ready, 1)
                        dve.wait_ge(silus, i * 4 + (v + 1))
                        dve.wait_ge(ring.read[slot[3]], i * 4 + (lap[3] + v + 1))
                        nc.vector.tensor_tensor(a, sg[:], ps[:, 2 + v % 2, 0:W], ALU.mult).then_inc(a_ready, 1) if W == STRIP else \
                            nc.vector.tensor_tensor(a[:, 0:W], sg[:], ps[:, 2 + v % 2, 0:W], ALU.mult).then_inc(a_ready, 1)
                        dve.wait_ge(ring.read[slot[5]], i * 4 + (lap[5] + v + 1))
                        for dst, src in y_copies(i, v, 1):
                            last = nc.vector.tensor_copy(dst, src)
                        last.then_inc(y_dve, 1)


def moe(core, t, layer, lat_and_ctx, out=None):
    nc = core.nc
    s, streams = 2 + layer, len(lat_and_ctx)
    T = NT * streams
    M = CAP * streams
    with ExitStack() as stack:
        sb = lambda n, shape: stack.enter_context(nc.sbuf_tensor(f"moe{layer}_" + n, shape, F32))
        ys = sb("ys", [P, 4, streams, D])
        inner = stack.enter_context(ExitStack())
        xsT = inner.enter_context(nc.sbuf_tensor(f"moe{layer}_xsT", [P, KC, EXPERTS, M], F32))
        xn = ys[:].rearrange("p q s d -> p (q s d)")[:, 0:T * D].rearrange("p (t d) -> p t d", t=T)
        sel = ys[:].rearrange("p q s d -> p (q s d)")[:, T * D:T * (D + STRIP)].rearrange("p (t n) -> p t n", t=T)
        rows = xsT[:].rearrange("p c e m -> p (c e m)")[:, 0:EXPERTS * T * P].rearrange("p (e t) -> p e t", e=EXPERTS)
        spare = core.hT[:].rearrange("p c t -> p (c t)")
        pickedT = spare[:, 0:4 * STRIP].rearrange("p (q t) -> p q t", q=4)
        picked = spare[:, 4 * STRIP:4 * STRIP + T * STRIP].rearrange("p (t n) -> p t n", t=T)
        with nc.sbuf_tensor(f"moe{layer}_aff", [P, T, EXPERTS], F32) as aff:
            stage_norm(core, s, 1, lat_and_ctx, f"norm_moe{layer}", xn_keep=xn)
            stage_route(core, t, f"route{layer}", streams, aff[:], rows, sel, picked)
            stage_gather(core, f"gather{layer}", s, xn, sel, picked, xsT[:], pickedT, streams)
        stage_experts(core, t, f"experts{layer}", layer, streams, xsT[:], ys[:])
        inner.close()
        stage_residual(core, f"moe{layer}_res", s, 5, lambda k, j: pickedT[:, k, j * P:(j + 1) * P], 4 * P, lat_and_ctx,
                       rhs=lambda k, i, n: ys[:, k, i, n * STRIP:(n + 1) * STRIP], out=out)
def build(nc, t, out, stop=None):
    with ExitStack() as ctx:
        core = Core(nc, ctx)
        units = core.ring.units
        plan = ["gdn", "ffn0", "dsw", "ffn1", "even", "moe0", "odd", "moe1"]
        upto = plan.index(stop) + 1 if stop else len(plan)
        ada, g = ada_units(t["w_ada"], 0), t["gdn_w_in"][0]
        units += ada[0:4]
        gdn = [u for c in range(0, 4096, STRIP) for u in k_units(g, c, c + STRIP)] + k_units(g, 4096, 4112)
        units += [u for pair in zip(gdn, ada[4:]) for u in pair] + gdn[8:]
        units += ada_units(t["w_ada"], 1) + ada_units(t["w_ada_2"], 0) + ada_units(t["w_ada_2"], 1)
        units += residual_units(t["gdn_w_out"][0], D)
        if upto > 1:
            units += ffn_units(t["w_ffn_in"], 0) + residual_units(t["w_ffn_out"][0], HIDDEN)
        if upto > 2:
            w = t["dsw_w_in"][0]
            units += [u for c in range(0, 9 * STRIP, STRIP) for u in k_units(w, c, c + STRIP)]
            units += residual_units(t["dsw_w_out"][0], GH * DH)
        if upto > 3:
            units += ffn_units(t["w_ffn_in"], 1) + residual_units(t["w_ffn_out"][1], HIDDEN)
        if upto > 4:
            w = t["w_in_even_2"][0]
            units += [u for c0, c1 in strips(4 * STRIP + 2 * P) for u in k_units(w, c0, c1)]
            units += residual_units(t["w_out_even_2"][0], D)
        if upto > 5:
            units += k_units(t["w_router_2"][0], 0, EXPERTS) + expert_units(t, 0)
        if upto > 6:
            units += k_units(t["w_in_odd_2"][0], 0, 3 * P + ROPE)
            units += [u for c in range(0, 16 * QK, 4 * QK) for u in k_units(t["w_q_up_2"][0], c, c + 4 * QK, 2 * P)]
            units += [u for c in range(0, 4 * STRIP, STRIP) for u in k_units(t["w_kv_up_2"][0], c, c + STRIP, P)]
            units += residual_units(t["w_out_odd_2"][0], D)
        if upto > 7:
            units += k_units(t["w_router_2"][1], 0, EXPERTS) + expert_units(t, 1)
        stage_setup(core, t)
        stage_ada(core, 0, 1)
        lat = [(core.x, 0)]
        hT = lambda k, j: core.hT[:, k, j * P:(j + 1) * P]
        stage_norm(core, 0, 0, lat, "norm_gdn")
        mixer_gdn(core, t, ctx)
        stage_residual(core, "gdn_res", 0, 2, hT, D, lat)
        if upto > 1:
            stage_norm(core, 0, 1, lat, "norm_ffn0")
            with nc.sbuf_tensor("aT0", [P, HC, S], F32) as aT:
                stage_ffn(core, "ffn0", aT)
                stage_residual(core, "ffn0_res", 0, 5, lambda k, j: aT[:, k, j * P:(j + 1) * P], HIDDEN, lat)
        if upto > 2:
            stage_norm(core, 1, 0, lat, "norm_dsw")
            mixer_dsw(core, t)
            stage_residual(core, "dsw_res", 1, 2, hT, GH * DH, lat)
        if upto > 3:
            stage_norm(core, 1, 1, lat, "norm_ffn1")
            with nc.sbuf_tensor("aT1", [P, HC, S], F32) as aT:
                stage_ffn(core, "ffn1", aT, [(core.ctx_x[:], t["ctx_2"].rearrange("b (j p) d -> p (b j) d", p=P))])
                stage_residual(core, "ffn1_res", 1, 5, lambda k, j: aT[:, k, j * P:(j + 1) * P], HIDDEN, lat)
        if upto > 4:
            both = lat + [(core.ctx_x, 1)]
            stage_norm(core, 2, 0, both, "norm_even")
            mixer_even(core, t)
            stage_residual(core, "even_res", 2, 2, hT, D, both)
        if upto > 5:
            moe(core, t, 0, both)
        if upto > 6:
            stage_norm(core, 3, 0, both, "norm_odd")
            mixer_odd(core, t)
            stage_residual(core, "odd_res", 3, 2, hT, D, lat)
        if upto > 7:
            moe(core, t, 1, lat, out)
        assert core.ring.taken == len(units) == core.ring.loaded


def kernel(**inputs):
    import concourse.bacc as bacc
    from concourse.bass_utils import run_bass_kernel_spmd

    nc = bacc.Bacc("TRN2", target_bir_lowering=False, num_devices=1)
    arrays, t = {}, {}
    named = {n: np.ascontiguousarray(a) for n, a in inputs.items()}
    named["const"] = shape_constants()
    named["marks"] = bias_constants()
    named["rope_even"], named["rope_odd"] = rope_constants(DH), rope_constants(ROPE)
    named["route"] = route_constants()
    for name, a in named.items():
        arrays[f"in_{name}"] = a
        t[name] = nc.dram_tensor(f"in_{name}", a.shape, mybir.dt.from_np(a.dtype), kind="ExternalInput").ap()
    t["bias_rows"] = nc.dram_tensor("distance_bias", (NG * GH, 2 * S), F32, kind="Internal").ap()
    t["affinity"] = nc.dram_tensor("affinity", (EXPERTS, 2 * S), F32, kind="Internal").ap()
    out = nc.dram_tensor("out", (1, S, D), F32, kind="ExternalOutput").ap()
    build(nc, t, out, STOP)
    r = run_bass_kernel_spmd(nc, [arrays], core_ids=[0])
    return r.results[0]["out"]


STOP = None
```
